# Optimizing a Trainium2 kernel written in Bass

```python
import math
import jax, jax.numpy as jnp
from jax import lax
import numpy as np

D_MODEL = 1024
BATCH = 1
SEQ = 256
DEPTH = 2

CTX_LEN = 256
GRID_W = 64
N_EVEN = (DEPTH + 1) // 2
N_ODD = DEPTH // 2

DEEPNORM_ALPHA = (2.0 * DEPTH) ** 0.25
DEEPNORM_BETA = (8.0 * DEPTH) ** -0.25
LN_EPS = 1e-5
RMS_EPS = 1e-6
N_MOD = 9

D_FF = 2816
MACARON_WEIGHT = 0.5

GDN_HEADS = 4
GDN_HEAD_DIM = 128
GDN_WIDTH = GDN_HEADS * GDN_HEAD_DIM
GDN_CONV = 5
GDN_CHUNK = 64
CONV_CH = D_MODEL // 2
CONV_WIDTH = 31
EVEN_SPLITS = (3 * GDN_WIDTH, 4 * GDN_WIDTH, 4 * GDN_WIDTH + 4 * GDN_HEADS)
EVEN_IN = 4 * GDN_WIDTH + 4 * GDN_HEADS + 2 * CONV_CH
EVEN_OUT = GDN_WIDTH + CONV_CH

ATT_HEADS = 8
ATT_KV_HEADS = 2
ATT_GROUP = ATT_HEADS // ATT_KV_HEADS
ATT_HEAD_DIM = 128
ATT_BLOCK = 128
ROPE_THETA = 10000.0
ODD_IN = (ATT_HEADS + 2 * ATT_KV_HEADS) * ATT_HEAD_DIM
ODD_OUT = ATT_HEADS * ATT_HEAD_DIM


def layer_norm(x, g, b):
    xf = x.astype(jnp.float32)
    mu = xf.mean(-1, keepdims=True)
    var = jnp.square(xf - mu).mean(-1, keepdims=True)
    return ((xf - mu) * lax.rsqrt(var + LN_EPS) * g + b).astype(x.dtype)

def rms_norm(x, g):
    xf = x.astype(jnp.float32)
    return (xf * lax.rsqrt(jnp.square(xf).mean(-1, keepdims=True) + RMS_EPS) * g).astype(x.dtype)

def l2_normalize(x):
    xf = x.astype(jnp.float32)
    return xf * lax.rsqrt(jnp.square(xf).sum(-1, keepdims=True) + RMS_EPS)

def modulate(x, shift, scale):
    return x * (1 + scale) + shift

def deepnorm_residual(x, y, g, b):
    return layer_norm(DEEPNORM_ALPHA * x + y, g, b)

def adaln_modulation(cond, w_ada, b_ada):
    return jnp.split(jax.nn.silu(cond) @ w_ada + b_ada, N_MOD, axis=-1)

def swiglu(x, w_gu, w_down):
    gate, up = jnp.split(x @ w_gu, 2, axis=-1)
    return (jax.nn.silu(gate) * up) @ w_down

def ffn_sublayer(x, shift, scale, gate, w_gu, w_down, g, b):
    y = swiglu(modulate(x, shift, scale), w_gu, w_down)
    return deepnorm_residual(x, MACARON_WEIGHT * gate * y, g, b)

def depthwise_conv(x, w):
    k = w.shape[0]
    return lax.conv_general_dilated(
        x, w[:, None, :], window_strides=(1,), padding=[(k // 2, k // 2)],
        dimension_numbers=('NWC', 'WIO', 'NWC'), feature_group_count=x.shape[-1])

def axial_rope_tables(rows, head_dim, dtype):
    row = jnp.repeat(jnp.arange(rows, dtype=jnp.float32), GRID_W)
    col = jnp.tile(jnp.arange(GRID_W, dtype=jnp.float32), rows)
    n_freq = head_dim // 4
    inv_freq = jnp.float32(ROPE_THETA) ** (-jnp.arange(n_freq, dtype=jnp.float32) / n_freq)
    ang = jnp.concatenate([row[:, None] * inv_freq, col[:, None] * inv_freq], axis=-1)
    return jnp.cos(ang).astype(dtype), jnp.sin(ang).astype(dtype)

def apply_rope(x, cos, sin):
    x1, x2 = x[..., 0::2], x[..., 1::2]
    c, s = cos[:, None, :], sin[:, None, :]
    return jnp.stack([x1 * c - x2 * s, x1 * s + x2 * c], axis=-1).reshape(x.shape)

def gated_delta_chunked(q, k, v, g, beta, state0):
    B, L, H, dk = q.shape
    dv = v.shape[-1]
    C = GDN_CHUNK
    n = L // C
    f32 = jnp.float32

    def to_chunks(t):
        t = t.astype(f32).reshape((B, n, C, H) + t.shape[3:])
        return jnp.moveaxis(t, (1, 3), (0, 2))

    qc = to_chunks(q) * (dk ** -0.5)
    kc, vc = to_chunks(k), to_chunks(v)
    gcum = jnp.cumsum(to_chunks(g), axis=-1)
    bc = to_chunks(beta)
    tril = jnp.tril(jnp.ones((C, C), dtype=bool))
    strict = jnp.tril(jnp.ones((C, C), dtype=bool), -1)
    diff = gcum[..., :, None] - gcum[..., None, :]
    decay = jnp.where(tril, jnp.exp(jnp.where(tril, diff, 0.0)), 0.0)
    k_beta = kc * bc[..., None]
    v_beta = vc * bc[..., None]
    m = jnp.where(strict, jnp.einsum('nbhik,nbhjk->nbhij', k_beta, kc) * decay, 0.0)
    a = jnp.eye(C, dtype=f32) + m
    u = lax.linalg.triangular_solve(a, v_beta, left_side=True, lower=True, unit_diagonal=True)
    w = lax.linalg.triangular_solve(a, k_beta * jnp.exp(gcum)[..., None],
                                    left_side=True, lower=True, unit_diagonal=True)
    attn_intra = jnp.where(tril, jnp.einsum('nbhik,nbhjk->nbhij', qc, kc) * decay, 0.0)
    g_last = gcum[..., -1]
    k_tail = kc * jnp.exp(g_last[..., None] - gcum)[..., None]

    def step(S, inp):
        q_i, u_i, w_i, at_i, gc_i, gl_i, kt_i = inp
        v_new = u_i - w_i @ S
        o = (q_i * jnp.exp(gc_i)[..., None]) @ S + at_i @ v_new
        S = S * jnp.exp(gl_i)[..., None, None] + jnp.swapaxes(kt_i, -1, -2) @ v_new
        return S, o

    S, o = lax.scan(step, state0.astype(f32), (qc, u, w, attn_intra, gcum, g_last, k_tail))
    o = jnp.moveaxis(o, (0, 2), (1, 3)).reshape(B, L, H, dv)
    return o, S

def gdn_bidirectional(q, k, v, g_f, g_b, b_f, b_b, s_f0, s_b0):
    flip = lambda t: jnp.flip(t, axis=1)
    o_f, s_f = gated_delta_chunked(q, k, v, g_f, b_f, s_f0)
    o_b, s_b = gated_delta_chunked(flip(q), flip(k), flip(v), flip(g_b), flip(b_b), s_b0)
    return o_f + flip(o_b), s_f, s_b

def gdn_gates(ab, a_log, dt_bias):
    B, L, _ = ab.shape
    af = ab.astype(jnp.float32)
    a = af[..., :2 * GDN_HEADS].reshape(B, L, 2, GDN_HEADS)
    b = af[..., 2 * GDN_HEADS:].reshape(B, L, 2, GDN_HEADS)
    g = -jnp.exp(a_log.astype(jnp.float32)) * jax.nn.softplus(a + dt_bias.astype(jnp.float32))
    beta = jax.nn.sigmoid(b)
    return g[:, :, 0], g[:, :, 1], beta[:, :, 0], beta[:, :, 1]

def even_mixer(h_lat, h_ctx, w_in, qkv_conv, a_log, dt_bias, out_norm,
               dw_conv, dw_bias, cln_g, cln_b, w_out, need_ctx):
    def project(h):
        B, L, _ = h.shape
        qkv, z, ab, glu = jnp.split(h @ w_in, EVEN_SPLITS, axis=-1)
        qkv = jax.nn.silu(depthwise_conv(qkv, qkv_conv))
        q, k, v = [t.reshape(B, L, GDN_HEADS, GDN_HEAD_DIM) for t in jnp.split(qkv, 3, axis=-1)]
        scan_in = (l2_normalize(q), l2_normalize(k), v) + gdn_gates(ab, a_log, dt_bias)
        return scan_in, z, glu

    def conformer(glu):
        val, gate = jnp.split(glu, 2, axis=-1)
        y = depthwise_conv(val * jax.nn.sigmoid(gate), dw_conv) + dw_bias
        return jax.nn.silu(layer_norm(y, cln_g, cln_b))

    def merge(o, z, glu):
        B, L, _ = z.shape
        o = rms_norm(o, out_norm).astype(z.dtype) * jax.nn.silu(z.reshape(B, L, GDN_HEADS, GDN_HEAD_DIM))
        return jnp.concatenate([o.reshape(B, L, GDN_WIDTH), conformer(glu)], axis=-1) @ w_out

    ctx_in, z_c, glu_c = project(h_ctx)
    lat_in, z_l, glu_l = project(h_lat)
    zeros = jnp.zeros((h_ctx.shape[0], GDN_HEADS, GDN_HEAD_DIM, GDN_HEAD_DIM), jnp.float32)
    o_c, s_f, s_b = gdn_bidirectional(*ctx_in, zeros, zeros)
    o_l, _, _ = gdn_bidirectional(*lat_in, s_f, s_b)
    lat_out = merge(o_l, z_l, glu_l)
    ctx_out = merge(o_c, z_c, glu_c) if need_ctx else None
    return lat_out, ctx_out

def gqa_attend(q, k, v):
    s = jnp.einsum('bqhgd,blhd->bhgql', q, k).astype(jnp.float32) * (ATT_HEAD_DIM ** -0.5)
    p = jax.nn.softmax(s, axis=-1).astype(v.dtype)
    return jnp.einsum('bhgql,blhd->bqhgd', p, v)

def odd_mixer(h_lat, h_ctx, w_in, q_norm, k_norm, w_out, rope_cos, rope_sin, need_ctx):
    hd = ATT_HEAD_DIM

    def project(h):
        B, L, _ = h.shape
        q, k, v = jnp.split(h @ w_in, [ATT_HEADS * hd, (ATT_HEADS + ATT_KV_HEADS) * hd], axis=-1)
        q = rms_norm(q.reshape(B, L, ATT_HEADS, hd), q_norm)
        k = rms_norm(k.reshape(B, L, ATT_KV_HEADS, hd), k_norm)
        return q, k, v.reshape(B, L, ATT_KV_HEADS, hd)

    q_c, k_c, v_c = project(h_ctx)
    q_l, k_l, v_l = project(h_lat)
    q_l = apply_rope(q_l, rope_cos, rope_sin)
    k_l = apply_rope(k_l, rope_cos, rope_sin)
    B, L = h_lat.shape[:2]
    k_all = jnp.concatenate([k_l, k_c], axis=1)
    v_all = jnp.concatenate([v_l, v_c], axis=1)
    n_blk = L // ATT_BLOCK
    q_blocks = q_l.reshape(B, n_blk, ATT_BLOCK, ATT_KV_HEADS, ATT_GROUP, hd).swapaxes(0, 1)
    o = lax.map(lambda qb: gqa_attend(qb, k_all, v_all), q_blocks)
    lat_out = o.swapaxes(0, 1).reshape(B, L, ODD_OUT) @ w_out
    ctx_out = None
    if need_ctx:
        Bc, Lc = h_ctx.shape[:2]
        o_c = gqa_attend(q_c.reshape(Bc, Lc, ATT_KV_HEADS, ATT_GROUP, hd), k_c, v_c)
        ctx_out = o_c.reshape(Bc, Lc, ODD_OUT) @ w_out
    return lat_out, ctx_out

def first_inputs(seed: int = 0) -> dict:
    key = jax.random.key(seed)
    ks = jax.random.split(key, 32)
    f32 = jnp.float32
    nrm = lambda k, shape, s: jax.random.normal(k, shape, f32) * s
    dt = jnp.exp(jax.random.uniform(ks[13], (N_EVEN, 2, GDN_HEADS), f32, math.log(1e-3), math.log(1e-1)))
    return {
        "x": nrm(ks[0], (BATCH, SEQ, D_MODEL), 1.0),
        "c": nrm(ks[1], (BATCH, D_MODEL), 1.0),
        "ctx": nrm(ks[2], (BATCH, CTX_LEN, D_MODEL), 1.0),
        "c_ctx": nrm(ks[3], (D_MODEL,), 1.0),
        "ada_w": nrm(ks[4], (DEPTH, D_MODEL, N_MOD * D_MODEL), 0.5 * D_MODEL ** -0.5),
        "ada_b": nrm(ks[5], (DEPTH, N_MOD * D_MODEL), 0.02),
        "ln_g": 1.0 + nrm(ks[6], (DEPTH, 3, D_MODEL), 0.02),
        "ln_b": nrm(ks[7], (DEPTH, 3, D_MODEL), 0.02),
        "ffn_w_gu": nrm(ks[8], (DEPTH, 2, D_MODEL, 2 * D_FF), D_MODEL ** -0.5),
        "ffn_w_down": nrm(ks[9], (DEPTH, 2, D_FF, D_MODEL), DEEPNORM_BETA * D_FF ** -0.5),
        "even_w_in": nrm(ks[10], (N_EVEN, D_MODEL, EVEN_IN), D_MODEL ** -0.5),
        "even_qkv_conv": nrm(ks[11], (N_EVEN, GDN_CONV, 3 * GDN_WIDTH), GDN_CONV ** -0.5),
        "gdn_a_log": jnp.log(jax.random.uniform(ks[12], (N_EVEN, 2, GDN_HEADS), f32, 1.0, 16.0)),
        "gdn_dt_bias": dt + jnp.log(-jnp.expm1(-dt)),
        "gdn_out_norm": 1.0 + nrm(ks[14], (N_EVEN, GDN_HEAD_DIM), 0.02),
        "cf_dw_conv": nrm(ks[15], (N_EVEN, CONV_WIDTH, CONV_CH), CONV_WIDTH ** -0.5),
        "cf_dw_bias": nrm(ks[16], (N_EVEN, CONV_CH), 0.02),
        "cf_ln_g": 1.0 + nrm(ks[17], (N_EVEN, CONV_CH), 0.02),
        "cf_ln_b": nrm(ks[18], (N_EVEN, CONV_CH), 0.02),
        "even_w_out": nrm(ks[19], (N_EVEN, EVEN_OUT, D_MODEL), DEEPNORM_BETA * EVEN_OUT ** -0.5),
        "attn_w_in": nrm(ks[20], (N_ODD, D_MODEL, ODD_IN), D_MODEL ** -0.5),
        "attn_q_norm": 1.0 + nrm(ks[21], (N_ODD, ATT_HEAD_DIM), 0.02),
        "attn_k_norm": 1.0 + nrm(ks[22], (N_ODD, ATT_HEAD_DIM), 0.02),
        "attn_w_out": nrm(ks[23], (N_ODD, ODD_OUT, D_MODEL), DEEPNORM_BETA * ODD_OUT ** -0.5),
    }

def first_block(x, c, ctx, c_ctx, ada_w, ada_b, ln_g, ln_b, ffn_w_gu, ffn_w_down,
              even_w_in, even_qkv_conv, gdn_a_log, gdn_dt_bias, gdn_out_norm,
              cf_dw_conv, cf_dw_bias, cf_ln_g, cf_ln_b, even_w_out,
              attn_w_in, attn_q_norm, attn_k_norm, attn_w_out):
    rows = x.shape[1] // GRID_W
    rope_cos, rope_sin = axial_rope_tables(rows, ATT_HEAD_DIM, x.dtype)
    for layer in range(DEPTH):
        last = layer == DEPTH - 1
        i = layer // 2
        mods_lat = [m[:, None, :] for m in adaln_modulation(c, ada_w[layer], ada_b[layer])]
        mods_ctx = adaln_modulation(c_ctx, ada_w[layer], ada_b[layer])
        x = ffn_sublayer(x, *mods_lat[0:3], ffn_w_gu[layer, 0], ffn_w_down[layer, 0], ln_g[layer, 0], ln_b[layer, 0])
        ctx = ffn_sublayer(ctx, *mods_ctx[0:3], ffn_w_gu[layer, 0], ffn_w_down[layer, 0], ln_g[layer, 0], ln_b[layer, 0])
        h_lat = modulate(x, *mods_lat[3:5])
        h_ctx = modulate(ctx, *mods_ctx[3:5])
        if layer % 2 == 0:
            o_lat, o_ctx = even_mixer(h_lat, h_ctx, even_w_in[i], even_qkv_conv[i], gdn_a_log[i], gdn_dt_bias[i],
                                      gdn_out_norm[i], cf_dw_conv[i], cf_dw_bias[i], cf_ln_g[i], cf_ln_b[i],
                                      even_w_out[i], not last)
        else:
            o_lat, o_ctx = odd_mixer(h_lat, h_ctx, attn_w_in[i], attn_q_norm[i], attn_k_norm[i], attn_w_out[i],
                                     rope_cos, rope_sin, not last)
        x = deepnorm_residual(x, mods_lat[5] * o_lat, ln_g[layer, 1], ln_b[layer, 1])
        x = ffn_sublayer(x, *mods_lat[6:9], ffn_w_gu[layer, 1], ffn_w_down[layer, 1], ln_g[layer, 2], ln_b[layer, 2])
        if not last:
            ctx = deepnorm_residual(ctx, mods_ctx[5] * o_ctx, ln_g[layer, 1], ln_b[layer, 1])
            ctx = ffn_sublayer(ctx, *mods_ctx[6:9], ffn_w_gu[layer, 1], ffn_w_down[layer, 1], ln_g[layer, 2], ln_b[layer, 2])
    return x


HEAD_DIM = 64
A_HEADS = 8
B_HEADS = 8
M_HEADS = 4
M_HEAD_DIM = 128
BRANCH_WIDTH = 512
N_BRANCH = 3
MOBA_BLOCK = 256
MOBA_TOPK = 3
IDX_HEADS = 8
IDX_DIM = 64
IDX_TOPK_MAX = 256
N_MEM = 256
ROPE_THETA_2 = 500000.0
ROT_FRACTION = 4
Q_BLOCK = 128
IN_WIDTHS = (
    BRANCH_WIDTH, BRANCH_WIDTH, BRANCH_WIDTH, BRANCH_WIDTH,
    BRANCH_WIDTH, BRANCH_WIDTH, BRANCH_WIDTH, BRANCH_WIDTH,
    IDX_HEADS * IDX_DIM, IDX_DIM, IDX_HEADS,
    BRANCH_WIDTH, BRANCH_WIDTH,
    N_BRANCH * D_MODEL,
)
IN_COLS = sum(IN_WIDTHS)


def rmsnorm(x, g):
    xf = x.astype(jnp.float32)
    y = xf * lax.rsqrt(jnp.mean(xf * xf, axis=-1, keepdims=True) + RMS_EPS)
    return (y * g.astype(jnp.float32)).astype(x.dtype)

def partial_rope(x, pos):
    d = x.shape[-1]
    rot = d // ROT_FRACTION
    half = rot // 2
    inv_freq = ROPE_THETA_2 ** (-jnp.arange(half, dtype=jnp.float32) / half)
    ang = pos.astype(jnp.float32)[:, None] * inv_freq[None, :]
    cos = jnp.cos(ang)[:, None, :].astype(x.dtype)
    sin = jnp.sin(ang)[:, None, :].astype(x.dtype)
    x1 = x[..., :half]
    x2 = x[..., half:rot]
    return jnp.concatenate([x1 * cos - x2 * sin, x2 * cos + x1 * sin, x[..., rot:]], axis=-1)

def masked_softmax(s, mask):
    s = jnp.where(mask, s.astype(jnp.float32), -jnp.inf)
    return jax.nn.softmax(s, axis=-1)

def moba_attention(q, k, v):
    b, s, h, d = q.shape
    nb = -(-s // MOBA_BLOCK)
    pad = nb * MOBA_BLOCK - s
    padw = ((0, 0), (0, pad), (0, 0), (0, 0))
    kb = jnp.pad(k, padw).reshape(b, nb, MOBA_BLOCK, h, d).transpose(0, 3, 1, 2, 4)
    vb = jnp.pad(v, padw).reshape(b, nb, MOBA_BLOCK, h, d).transpose(0, 3, 1, 2, 4)
    kmean = jnp.mean(kb.astype(jnp.float32), axis=3).astype(q.dtype)
    kk = min(MOBA_TOPK, nb - 1)
    scale = d ** -0.5
    b_idx = jnp.arange(b)[:, None, None, None]
    h_idx = jnp.arange(h)[None, :, None, None]
    blk_ids = jnp.arange(nb)

    def one_block(qi):
        start = qi * Q_BLOCK
        own = start // MOBA_BLOCK
        qpos = start + jnp.arange(Q_BLOCK)
        qb = lax.dynamic_slice_in_dim(q, start, Q_BLOCK, axis=1).transpose(0, 2, 1, 3)
        k_own = lax.dynamic_index_in_dim(kb, own, axis=2, keepdims=False)
        v_own = lax.dynamic_index_in_dim(vb, own, axis=2, keepdims=False)
        kpos_own = own * MOBA_BLOCK + jnp.arange(MOBA_BLOCK)
        s_own = jnp.einsum('bhqd,bhkd->bhqk', qb, k_own) * scale
        m_own = jnp.broadcast_to(kpos_own[None, :] <= qpos[:, None], s_own.shape)
        if kk == 0:
            p = masked_softmax(s_own, m_own).astype(v.dtype)
            o = jnp.einsum('bhqk,bhkd->bhqd', p, v_own)
        else:
            gate = jnp.einsum('bhqd,bhnd->bhqn', qb, kmean).astype(jnp.float32)
            gate = jnp.where(blk_ids < own, gate, -jnp.inf)
            _, sel = lax.top_k(gate, kk)
            valid = sel < own
            kg = kb[b_idx, h_idx, sel]
            vg = vb[b_idx, h_idx, sel]
            s_past = jnp.einsum('bhqd,bhqjkd->bhqjk', qb, kg) * scale
            m_past = jnp.broadcast_to(valid[..., None], s_past.shape)
            n_past = kk * MOBA_BLOCK
            s_all = jnp.concatenate([s_past.reshape(b, h, Q_BLOCK, n_past), s_own], axis=-1)
            m_all = jnp.concatenate([m_past.reshape(b, h, Q_BLOCK, n_past), m_own], axis=-1)
            p = masked_softmax(s_all, m_all).astype(v.dtype)
            p_past = p[..., :n_past].reshape(b, h, Q_BLOCK, kk, MOBA_BLOCK)
            o = (jnp.einsum('bhqjk,bhqjkd->bhqd', p_past, vg)
                 + jnp.einsum('bhqk,bhkd->bhqd', p[..., n_past:], v_own))
        return o.transpose(0, 2, 1, 3)

    out = lax.map(one_block, jnp.arange(s // Q_BLOCK))
    return out.transpose(1, 0, 2, 3, 4).reshape(b, s, h, d)

def dsa_attention(q, k, v, qi, ki, wi):
    b, s, h, d = q.shape
    n_sel = min(IDX_TOPK_MAX, s // 4)
    scale = d ** -0.5
    kpos = jnp.arange(s)
    b_idx = jnp.arange(b)[:, None, None]

    def one_block(blk):
        start = blk * Q_BLOCK
        qpos = start + jnp.arange(Q_BLOCK)
        q_b = lax.dynamic_slice_in_dim(q, start, Q_BLOCK, axis=1)
        qi_b = lax.dynamic_slice_in_dim(qi, start, Q_BLOCK, axis=1)
        wi_b = lax.dynamic_slice_in_dim(wi, start, Q_BLOCK, axis=1)
        rel = jax.nn.relu(jnp.einsum('bqhd,bsd->bqhs', qi_b, ki))
        idx_score = jnp.einsum('bqhs,bqh->bqs', rel, wi_b).astype(jnp.float32)
        idx_score = jnp.where(kpos[None, :] <= qpos[:, None], idx_score, -jnp.inf)
        _, sel = lax.top_k(idx_score, n_sel)
        valid = sel <= qpos[None, :, None]
        kg = k[b_idx, sel]
        vg = v[b_idx, sel]
        sc = jnp.einsum('bqhd,bqnhd->bqhn', q_b, kg) * scale
        p = masked_softmax(sc, valid[:, :, None, :]).astype(v.dtype)
        return jnp.einsum('bqhn,bqnhd->bqhd', p, vg)

    out = lax.map(one_block, jnp.arange(s // Q_BLOCK))
    return out.transpose(1, 0, 2, 3, 4).reshape(b, s, h, d)

def memory_attention(qm, km, vm):
    sc = jnp.einsum('bshd,bmhd->bhsm', qm, km) * (qm.shape[-1] ** -0.5)
    p = jax.nn.softmax(sc.astype(jnp.float32), axis=-1).astype(vm.dtype)
    return jnp.einsum('bhsm,bmhd->bshd', p, vm)

def hybrid_layer(x, mem, pos, norm_g, w_in, mem_norm_g, w_mem_kv, w_branch, w_out):
    b, s, _ = x.shape
    h = rmsnorm(x, norm_g)
    proj = jnp.einsum('bsd,dc->bsc', h, w_in)
    offs = np.cumsum(IN_WIDTHS)[:-1].tolist()
    (a_q, a_k, a_v, a_g, b_q, b_k, b_v, b_g,
     i_q, i_k, i_w, m_q, m_g, mix) = jnp.split(proj, offs, axis=-1)

    qa = partial_rope(a_q.reshape(b, s, A_HEADS, HEAD_DIM), pos)
    ka = partial_rope(a_k.reshape(b, s, A_HEADS, HEAD_DIM), pos)
    va = a_v.reshape(b, s, A_HEADS, HEAD_DIM)
    ya = moba_attention(qa, ka, va).reshape(b, s, BRANCH_WIDTH) * jax.nn.silu(a_g)

    qb = partial_rope(b_q.reshape(b, s, B_HEADS, HEAD_DIM), pos)
    kb = partial_rope(b_k.reshape(b, s, B_HEADS, HEAD_DIM), pos)
    vb = b_v.reshape(b, s, B_HEADS, HEAD_DIM)
    qi = partial_rope(i_q.reshape(b, s, IDX_HEADS, IDX_DIM), pos) * (IDX_DIM ** -0.5)
    ki = partial_rope(i_k[:, :, None, :], pos)[:, :, 0, :]
    wi = i_w * (IDX_HEADS ** -0.5)
    yb = dsa_attention(qb, kb, vb, qi, ki, wi).reshape(b, s, BRANCH_WIDTH) * jax.nn.silu(b_g)

    mn = rmsnorm(mem, mem_norm_g)
    km, vm = jnp.split(jnp.einsum('bmd,dc->bmc', mn, w_mem_kv), 2, axis=-1)
    km = km.reshape(b, -1, M_HEADS, M_HEAD_DIM)
    vm = vm.reshape(b, -1, M_HEADS, M_HEAD_DIM)
    ym = memory_attention(m_q.reshape(b, s, M_HEADS, M_HEAD_DIM), km, vm)
    ym = ym.reshape(b, s, BRANCH_WIDTH) * jax.nn.silu(m_g)

    ys = jnp.stack([ya, yb, ym], axis=2)
    up = jnp.einsum('bsnw,nwd->bsnd', ys, w_branch)
    gates = jax.nn.sigmoid(mix.reshape(b, s, N_BRANCH, D_MODEL))
    merged = jnp.sum(gates * up, axis=2)
    return x + jnp.einsum('bsd,de->bse', merged, w_out)

def second_inputs(seed: int = 0) -> dict:
    key = jax.random.key(seed)
    ks = jax.random.split(key, 9)
    f32 = jnp.float32
    x = jax.random.normal(ks[0], (BATCH, SEQ, D_MODEL), f32)
    mem = jax.random.normal(ks[1], (BATCH, N_MEM, D_MODEL), f32)
    norm_g = 1.0 + 0.02 * jax.random.normal(ks[2], (DEPTH, D_MODEL), f32)
    w_in = jax.random.normal(ks[3], (DEPTH, D_MODEL, IN_COLS), f32) * (D_MODEL ** -0.5)
    mem_norm_g = 1.0 + 0.02 * jax.random.normal(ks[4], (DEPTH, D_MODEL), f32)
    w_mem_kv = jax.random.normal(ks[5], (DEPTH, D_MODEL, 2 * BRANCH_WIDTH), f32) * (D_MODEL ** -0.5)
    w_branch = jax.random.normal(ks[6], (DEPTH, N_BRANCH, BRANCH_WIDTH, D_MODEL), f32) * (BRANCH_WIDTH ** -0.5)
    w_out = jax.random.normal(ks[7], (DEPTH, D_MODEL, D_MODEL), f32) * (D_MODEL ** -0.5)
    final_g = 1.0 + 0.02 * jax.random.normal(ks[8], (D_MODEL,), f32)
    return {'x': x, 'mem': mem, 'norm_g': norm_g, 'w_in': w_in, 'mem_norm_g': mem_norm_g,
            'w_mem_kv': w_mem_kv, 'w_branch': w_branch, 'w_out': w_out, 'final_g': final_g}

def second_block(x, mem, norm_g, w_in, mem_norm_g, w_mem_kv, w_branch, w_out, final_g):
    pos = jnp.arange(x.shape[1], dtype=jnp.int32)
    for l in range(DEPTH):
        x = hybrid_layer(x, mem, pos, norm_g[l], w_in[l], mem_norm_g[l], w_mem_kv[l],
                         w_branch[l], w_out[l])
    return rmsnorm(x, final_g)


def setup_inputs(seed=0):
    out = dict(first_inputs(seed))
    for name, value in second_inputs(seed + 1).items():
        if name != "x":
            out[name + "_2"] = value
    return out


def reference(
    x, c, ctx, c_ctx, ada_w, ada_b, ln_g, ln_b, ffn_w_gu, ffn_w_down, even_w_in, even_qkv_conv,
    gdn_a_log, gdn_dt_bias, gdn_out_norm, cf_dw_conv, cf_dw_bias, cf_ln_g, cf_ln_b, even_w_out,
    attn_w_in, attn_q_norm, attn_k_norm, attn_w_out, mem_2, norm_g_2, w_in_2, mem_norm_g_2,
    w_mem_kv_2, w_branch_2, w_out_2, final_g_2,
):
    x = first_block(
        x, c, ctx, c_ctx, ada_w, ada_b, ln_g, ln_b, ffn_w_gu, ffn_w_down, even_w_in,
        even_qkv_conv, gdn_a_log, gdn_dt_bias, gdn_out_norm, cf_dw_conv, cf_dw_bias, cf_ln_g,
        cf_ln_b, even_w_out, attn_w_in, attn_q_norm, attn_k_norm, attn_w_out,
    )
    return second_block(
        x, mem_2, norm_g_2, w_in_2, mem_norm_g_2, w_mem_kv_2, w_branch_2, w_out_2, final_g_2,
    )


_drawn_inputs = setup_inputs


def setup_inputs(seed=0):
    import zlib

    import numpy as np

    out = dict(_drawn_inputs(seed))
    spreads = {}
    factors = {'ctx': 4.92,
     'ada_b': 4.662,
     'gdn_a_log': 4.968,
     'gdn_dt_bias': 3.319,
     'gdn_out_norm': 8.0,
     'cf_dw_bias': 8.0,
     'cf_ln_g': 8.0,
     'cf_ln_b': 8.0,
     'attn_q_norm': 8.0,
     'attn_k_norm': 8.0,
     'norm_g_2': 4.277,
     'mem_norm_g_2': 8.0,
     'final_g_2': 2.722}
    for name, (base, spread) in spreads.items():
        noise = np.random.default_rng([zlib.crc32(name.encode()), seed]).standard_normal(out[name].shape)
        drawn = base * np.exp(spread * noise) if base else spread * noise
        out[name] = __import__('jax').numpy.asarray(drawn.astype(out[name].dtype))
    for name, factor in factors.items():
        out[name] = (out[name] * factor).astype(out[name].dtype)
    return out
```

```python
import math
from contextlib import ExitStack

import numpy as np

import concourse.bass as bass
from concourse import mybir

F32 = mybir.dt.float32
ALU = mybir.AluOpType
ACTF = mybir.ActivationFunctionType
AXX = mybir.AxisListType.X

D, T, L = 1024, 512, 256
KD = D // 128
DFF = 2816
KF = DFF // 128
ALPHA = 4.0 ** 0.25
CH = 1024
NSLOT = 6
NCH = 656
NEG = -1.0e30
IN2 = (512,) * 8 + (512, 64, 8, 512, 512, 3072)
OFF2 = [sum(IN2[:i]) for i in range(len(IN2))]


def cols(v, n=None):
    return np.asarray(v).reshape(-1, 128).T


def param_list():
    out = []

    def add(name, n, fn):
        out.append((name, n, fn))

    add("cond", 16, lambda a: np.stack([cols(a["c"][0]), cols(a["c_ctx"])], -1).reshape(128, 16))
    for l in range(2):
        add(f"ada_b{l}", 72, lambda a, l=l: cols(a["ada_b"][l]))
        for j in range(3):
            add(f"ln_g{l}{j}", 8, lambda a, l=l, j=j: cols(a["ln_g"][l, j]))
            add(f"ln_b{l}{j}", 8, lambda a, l=l, j=j: cols(a["ln_b"][l, j]))
        add(f"norm2_{l}", 8, lambda a, l=l: cols(a["norm_g_2"][l]))
        add(f"mnorm2_{l}", 8, lambda a, l=l: cols(a["mem_norm_g_2"][l]))
    add("fin_g", 8, lambda a: cols(a["final_g_2"]))
    add("conv", 60, lambda a: a["even_qkv_conv"][0].reshape(5, 12, 128).transpose(2, 1, 0).reshape(128, 60))
    add("dwc", 124, lambda a: a["cf_dw_conv"][0].reshape(31, 4, 128).transpose(2, 1, 0).reshape(128, 124))
    add("dwb", 4, lambda a: cols(a["cf_dw_bias"][0]))
    add("clg", 4, lambda a: cols(a["cf_ln_g"][0]))
    add("clb", 4, lambda a: cols(a["cf_ln_b"][0]))
    add("onorm", 1, lambda a: cols(a["gdn_out_norm"][0]))
    add("qn", 1, lambda a: cols(a["attn_q_norm"][0]))
    add("kn", 1, lambda a: cols(a["attn_k_norm"][0]))

    def gates(a, name):
        v = np.zeros((128, 1), np.float32)
        v[0:4, 0] = a[name][0, 0]
        v[32:36, 0] = a[name][0, 1]
        return v

    add("alog", 1, lambda a: gates(a, "gdn_a_log"))
    add("dtb", 1, lambda a: gates(a, "gdn_dt_bias"))
    return out


def constant_list():
    out = []
    p = np.arange(128)
    out.append(("ident", np.eye(128)))
    out.append(("ones", np.full((128, 128), 1.0)))
    out.append(("onesD", np.full((128, 128), 1.0 / D)))
    out.append(("ones512", np.full((128, 128), 1.0 / 512)))
    out.append(("ones128", np.full((128, 128), 1.0 / 128)))
    j, i = p[:, None] % 64, np.arange(64)[None, :]
    for n, ok in (("f", i >= j), ("b", i <= j)):
        out.append((f"inc_{n}", ok))
    for n, ok in (("f", i > j), ("b", i < j)):
        out.append((f"str_{n}", ok))
    r, c = p[:, None] % 64, np.arange(64)[None, :]
    for b in (1, 2, 4, 8, 16, 32):
        same = r // (2 * b) == c // (2 * b)
        low = same & ((r // b) % 2 == 1) & ((c // b) % 2 == 0)
        up = same & ((r // b) % 2 == 0) & ((c // b) % 2 == 1)
        if b == 1:
            out.append(("u1_f", -1.0 * up))
            out.append(("u1_b", -1.0 * low))
        else:
            out.append((f"lv{b}_f", low))
            out.append((f"lv{b}_b", up))
    out.append(("id64", r == c))
    for n, step in (("eps5", 1e-5), ("eps6", 1e-6), ("eps128", 128e-6)):
        out.append((n, np.full((128, 1), step)))
    s = np.ones((128, 64))
    s[:, 0] = 0
    out.append(("sg", s))
    t = np.arange(L)
    inv = np.float32(10000.0) ** (-np.arange(32, dtype=np.float32) / np.float32(32))
    ang = np.concatenate([(t // 64).astype(np.float32)[:, None] * inv, (t % 64).astype(np.float32)[:, None] * inv], -1)
    out.append(("ropeC", np.repeat(np.cos(ang).T, 2, axis=0)))
    out.append(("ropeS", np.repeat(np.sin(ang).T, 2, axis=0)))
    rot = np.zeros((128, 128))
    for k in range(64):
        rot[2 * k, 2 * k + 1] = -1
        rot[2 * k + 1, 2 * k] = 1
    out.append(("rotT", rot.T))
    inv = np.float32(500000.0) ** (-np.arange(8, dtype=np.float32) / np.float32(8))
    ang = t.astype(np.float32)[:, None] * inv[None, :]
    C, S, R = np.ones((128, L)), np.zeros((128, L)), np.zeros((128, 128))
    for h in (0, 64):
        for k in range(8):
            C[h + k] = C[h + 8 + k] = np.cos(ang[:, k])
            S[h + k] = S[h + 8 + k] = np.sin(ang[:, k])
            R[h + k, h + 8 + k] = -1
            R[h + 8 + k, h + k] = 1
    out.append(("prC", C))
    out.append(("prS", S))
    out.append(("prT", R.T))
    q = np.concatenate([p[:, None] + 128 * n >= np.arange(L)[None, :] for n in range(2)], 1)
    out.append(("causal", np.where(q, 0.0, NEG)))
    return [(n, np.ascontiguousarray(a, dtype=np.float32)) for n, a in out]


class Queue:

    def __init__(self, sem):
        self.sem, self.ops, self.n, self.seen = sem, [], 0, {}

    def wait(self, *tokens):
        for t in tokens:
            if t is None:
                continue
            if isinstance(t, list):
                self.wait(*t)
                continue
            assert t != "taken", "a buffer is used again before its last reader is known"
            sem, value = t
            if self.seen.get(id(sem), 0) < value:
                self.seen[id(sem)] = value
                self.ops.append([None, sem, value])

    def quiet(self, fn, *tokens):
        self.wait(*tokens)
        self.ops.append([fn, None, 0])

    def mark(self):
        op = self.ops[-1]
        if op[0] is not None and op[1] is None:
            self.n += 1
            op[1] = self.sem
        elif op[0] is None:
            return (self.sem, self.n) if self.n else None
        return (self.sem, self.n)

    def do(self, fn, *tokens):
        self.quiet(fn, *tokens)
        return self.mark()

    def play(self, eng):
        for fn, sem, value in self.ops:
            if fn is None:
                eng.wait_ge(sem, value)
            else:
                ins = fn(eng)
                if sem is not None:
                    ins.then_inc(sem, 1)


class Rot:

    def __init__(self, bufs):
        self.bufs, self.free, self.i = bufs, [None] * len(bufs), -1

    def get(self):
        self.i = (self.i + 1) % len(self.bufs)
        free, self.free[self.i] = self.free[self.i], ["taken"]
        return self.bufs[self.i], free, self.i


def build(nc, W, PRM, CST, XT, MT, OUT, stage="all"):
    recipes = []
    ctx = ExitStack()
    with ctx:
        def sb(name, n):
            return ctx.enter_context(nc.sbuf_tensor(name, [128, n], F32))

        def sem(name):
            return ctx.enter_context(nc.semaphore(name))

        PE, ACT, DVE, POOL, SP = (Queue(sem(n)) for n in ("s_pe", "s_act", "s_dve", "s_pool", "s_sp"))
        s_prm, s_cst, s_x, s_m, s_out = (sem(n) for n in ("d_prm", "d_cst", "d_x", "d_m", "d_out"))
        s_w = [sem(f"d_w{i}") for i in range(NSLOT)]

        ring = sb("ring", NSLOT * CH)
        X = sb("X", KD * T)
        pl, cl = param_list(), constant_list()
        prm = sb("prm", sum(n for _, n, _ in pl))
        cst = sb("cst", sum(a.shape[1] for _, a in cl))
        small = sb("small", 900)
        BIGN = 31984 + 9 * 512
        big = sb("big", BIGN)
        banks = Rot([ctx.enter_context(nc.psum_tensor(f"ps{i}", [128, 512], F32))[:, :] for i in range(8)])

        at = {}
        o = 0
        for n, w, _ in pl:
            at[n] = (prm, o, w)
            o += w
        o = 0
        for n, a in cl:
            at[n] = (cst, o, a.shape[1])
            o += a.shape[1]

        def P(name, a=0, b=None):
            t, o, w = at[name]
            return t[:, o + a:o + (w if b is None else b)]

        so = [0]

        def sm(n):
            so[0] += n
            assert so[0] <= 900, so
            return small[:, so[0] - n:so[0]]

        def last():
            return [q.mark() if q.ops else None for q in (PE, ACT, DVE, POOL)]

        state = {"chunk": -1, "off": CH, "rel": {}}

        def take(recipe, n=128):
            if state["off"] + n > CH:
                if state["chunk"] >= 0:
                    state["rel"][state["chunk"]] = PE.mark()
                state["chunk"] += 1
                state["off"] = 0
                c = state["chunk"]
                s = c % NSLOT
                SP.wait(state["rel"].get(c - NSLOT))
                SP.ops.append([lambda e, c=c, s=s: e.dma_start(ring[:, s * CH:(s + 1) * CH], W[c]).then_inc(s_w[s], 16), None, 0])
            c = state["chunk"]
            recipes.append((c, state["off"], n, recipe))
            ap = ring[:, (c % NSLOT) * CH + state["off"]:(c % NSLOT) * CH + state["off"] + n]
            state["off"] += n
            return ap, (s_w[c % NSLOT], 16 * (c // NSLOT + 1))

        def mm(out, lhsT, rhs, start, stop, *tokens, **kw):
            PE.quiet(lambda e: e.matmul(out, lhsT, rhs, start=start, stop=stop, **kw), *tokens)

        def transp(out, in_, k, *tokens):
            PE.quiet(lambda e: e.transpose(out, in_, P("ident")[0:k, 0:k]), *tokens)

        def ts(q, out, a, s1, s2, op0, op1, *tokens):
            if op1 is None:
                return q.do(lambda e: e.tensor_scalar(out, a, s1, None, op0), *tokens)
            return q.do(lambda e: e.tensor_scalar(out, a, s1, s2, op0, op1), *tokens)

        def tt(q, out, a, b, op, *tokens):
            return q.do(lambda e: e.tensor_tensor(out, a, b, op), *tokens)

        def stt(q, out, a, s, b, op0, op1, *tokens):
            return q.do(lambda e: e.scalar_tensor_tensor(out, a, s, b, op0, op1), *tokens)

        def act(out, a, fn, *tokens, **kw):
            return ACT.do(lambda e: e.activation(out, a, fn, **kw), *tokens)

        def copy(q, out, a, *tokens):
            if q is ACT:
                return act(out, a, ACTF.Copy, *tokens)
            return q.do(lambda e: e.tensor_copy(out, a), *tokens)

        def memset(q, out, v, *tokens):
            return q.do(lambda e: e.memset(out, v), *tokens)

        MUL, ADD, SUB = ALU.mult, ALU.add, ALU.subtract

        def linear(w, src, n, m=128, toks=None):
            bank, free, bi = banks.get()
            for k, (ap, tok) in enumerate(src):
                wt, wtok = take(w(k))
                mm(bank[0:m, 0:n], wt[:, 0:m], ap, k == 0, k == len(src) - 1, free, wtok, tok)
            return bank, bi, PE.mark()

        def tile_of(name, idx, c0):
            return lambda k: [(name, idx, 128 * k, 128, c0, 128, 0)]

        for dst, src, s in ((prm, PRM, s_prm), (cst, CST, s_cst), (X, XT, s_x)):
            SP.ops.append([lambda e, dst=dst, src=src, s=s: e.dma_start(dst[:, :], src).then_inc(s, 16), None, 0])
        tp, tc, tx = (s_prm, 16), (s_cst, 16), (s_x, 16)
        for q in (PE, ACT, DVE, POOL):
            q.wait(tp, tc)

        def B(a, n):
            return big[:, a:a + n]

        Xt = [X[:, k * T:(k + 1) * T] for k in range(KD)]
        XM = [B(k * T, T) for k in range(KD)]

        nega, colA, colT, colB, colG = sm(1), sm(64), sm(32), sm(32), sm(64)
        wi, mx8 = sm(16), sm(16)

        cs = sm(16)
        t_cs = act(cs, P("cond"), ACTF.Silu)
        mods, t_mod = {}, {}
        arow = sb("arow", 1024)
        arows = Rot([arow[0:2, 0:512], arow[0:2, 512:1024]])

        def ada(l):
            md = sm(144)
            pend = []

            def turn(g, row, t_row, ri):
                bank, free, bi = banks.get()
                for q in range(4):
                    mm(bank[:, 2 * q:2 * q + 2], row[:, q * 128:(q + 1) * 128], P("ident")[0:2, 0:2], True, True, t_row, free)
                t = PE.mark()
                arows.free[ri] = t
                banks.free[bi] = copy(DVE, md[:, 8 * g:8 * g + 8], bank[:, 0:8], t)
                return banks.free[bi]

            for g in range(18):
                bank, free, bi = banks.get()
                for k in range(KD):
                    wt, wtok = take([("ada_w", (l,), 128 * k, 128, 512 * g, 512, 0)], 512)
                    mm(bank[0:2, :], cs[:, 2 * k:2 * k + 2], wt, k == 0, k == KD - 1, free, wtok, t_cs)
                t = PE.mark()
                row, rfree, ri = arows.get()
                t_row = copy(ACT, row, bank[0:2, :], t, rfree)
                banks.free[bi] = t_row
                pend.append((g, row, t_row, ri))
                if len(pend) > 1:
                    tl = turn(*pend.pop(0))
                yield
            tl = turn(*pend.pop(0))
            m3 = md.rearrange("p (a s) -> p a s", s=2)
            t = tt(DVE, m3, m3, P(f"ada_b{l}").unsqueeze(2).broadcast_to([128, 72, 2]), ADD, tl)
            mods[l], t_mod[l] = md.rearrange("p (i m s) -> p i m s", i=9, s=2), t
            yield

        def norm_cols(g, b, l, i_shift, i_scale, tok):
            G = sm(16).rearrange("p (m s) -> p m s", s=2)
            Bc = sm(16).rearrange("p (m s) -> p m s", s=2)
            sc, sh = mods[l][:, i_scale], mods[l][:, i_shift]
            t = ts(DVE, G, sc, 1.0, None, ADD, None, tok, t_mod[l])
            if g is None:
                t2 = copy(DVE, Bc, sh, t)
                return G, Bc, t2
            bb = P(b).unsqueeze(2).broadcast_to([128, 8, 2])
            gg = P(g).unsqueeze(2).broadcast_to([128, 8, 2])
            t = tt(DVE, Bc, G, bb, MUL, t)
            t = tt(DVE, Bc, Bc, sh, ADD, t)
            t = tt(DVE, G, G, gg, MUL, t)
            return G, Bc, t

        def gate_cols(l, i, half, tok=None):
            gt = sm(16).rearrange("p (m s) -> p m s", s=2)
            t = ts(DVE, gt, mods[l][:, i], half, None, MUL, None, t_mod[l])
            return gt, t

        WK = BIGN - 9 * 512
        wk = [B(WK + 512 * i, 512) for i in range(9)]
        tmps = Rot(wk[0:3])
        sqs = Rot(wk[3:5])
        accS, accQ, w_mean, w_rstd = wk[5], wk[6], wk[7], wk[8]

        class Sums:

            def __init__(self, n, both=True, tok=None):
                self.n, self.both, self.first, self.tok = n, both, True, tok
                self.ts = self.tq = tok

            def add(self, ap, tok):
                n = self.n
                sq, free, i = sqs.get()
                t = act(sq[:, 0:n], ap, ACTF.Square, tok, free)
                if self.first:
                    if self.both:
                        self.ts = copy(POOL, accS[:, 0:n], ap, tok, self.ts)
                    self.tq = copy(POOL, accQ[:, 0:n], sq[:, 0:n], t, self.tq)
                else:
                    if self.both:
                        self.ts = tt(POOL, accS[:, 0:n], accS[:, 0:n], ap, ADD, tok, self.ts)
                    self.tq = tt(POOL, accQ[:, 0:n], accQ[:, 0:n], sq[:, 0:n], ADD, t, self.tq)
                sqs.free[i] = self.tq
                self.first = False
                return self.tq

            def finish(self, ones, eps):
                n = self.n
                if self.both:
                    b1, f1, i1 = banks.get()
                    mm(b1[:, 0:n], P(ones), accS[:, 0:n], True, True, f1, self.ts)
                    t1 = PE.mark()
                b2, f2, i2 = banks.get()
                mm(b2[:, 0:n], P(ones), accQ[:, 0:n], True, True, f2, self.tq)
                t2 = PE.mark()
                v = w_rstd[:, 0:n]
                if self.both:
                    tm = copy(ACT, w_mean[:, 0:n], b1[:, 0:n], t1, self.tok)
                    banks.free[i1] = tm
                    t = tt(DVE, v, w_mean[:, 0:n], w_mean[:, 0:n], MUL, tm, self.tok)
                    t = tt(DVE, v, b2[:, 0:n], v, SUB, t, t2)
                    banks.free[i2] = t
                    t = ts(DVE, v, v, 0.0, None, ALU.max, None, t)
                    t = act(v, v, ACTF.Sqrt, t, bias=P(eps))
                else:
                    t = act(v, b2[:, 0:n], ACTF.Sqrt, t2, self.tok, bias=P(eps))
                    banks.free[i2] = t
                return DVE.do(lambda e: e.reciprocal(v, v), t)

        def halves(n):
            return [(0, 0, 256), (1, 256, 512)] if n == T else [(0, 0, n)]

        def layer_norm_x(n, sums, lnp, nxt, out, extra=None):
            t0 = sums.finish("onesD", "eps5")
            G, Bc, tcol = nxt
            xs, ms = [], []
            for k in range(KD):
                x = Xt[k][:, 0:n]
                t, free, i = tmps.get()
                t = t[:, 0:n]
                q = DVE
                t1 = tt(DVE, t, x, w_mean[:, 0:n], SUB, t0, free)
                t1 = tt(POOL if k % 2 else DVE, t, t, w_rstd[:, 0:n], MUL, t1)
                tx_ = act(x, t, ACTF.Identity, t1, scale=P(lnp[0], k, k + 1), bias=P(lnp[1], k, k + 1))
                tm = []
                if G is not None:
                    for s, a, b in halves(n):
                        tm.append(ts(DVE, out[k][:, a:b], t[:, a:b], G[:, k, s:s + 1], Bc[:, k, s:s + 1], MUL, ADD, t1, tcol, extra))
                tmps.free[i] = [tx_] + tm
                xs.append(tx_)
                ms.append(tm[-1] if tm else tx_)
            return xs, ms

        def residual(bank, bi, tk, k, n, gt, tg, sums, xtok):
            t, free, i = tmps.get()
            for s, a, b in halves(n):
                ta = act(t[:, a:b], bank[:, a:b], ACTF.Copy, tk, free, tg, scale=gt[:, k, s:s + 1])
            banks.free[bi] = ta
            x = Xt[k][:, 0:n]
            tr = stt(DVE, x, x, ALPHA, t[:, 0:n], MUL, ADD, ta, xtok)
            tmps.free[i] = tr
            return sums.add(x, tr)

        H0 = KD * T
        Ht = [B(H0 + m * T, T) for m in range(KF)]

        def ffn(l, j, n, xs, ms, lnp, nxt, out_extra=None):
            gt, tg = gate_cols(l, 2 + 6 * j, 0.5)
            hs = []
            for m in range(KF):
                src = [(XM[k][:, 0:n], ms[k]) for k in range(KD)]
                bg, ig, _ = linear(tile_of("ffn_w_gu", (l, j), 128 * m), src, n)
                tg1 = PE.mark()
                bu, iu, tu = linear(tile_of("ffn_w_gu", (l, j), DFF + 128 * m), src, n)
                t, free, i = tmps.get()
                ta = act(t[:, 0:n], bg[:, 0:n], ACTF.Silu, tg1, free)
                banks.free[ig] = ta
                th = tt(DVE, Ht[m][:, 0:n], t[:, 0:n], bu[:, 0:n], MUL, ta, tu)
                banks.free[iu] = th
                tmps.free[i] = th
                hs.append(th)
            sums = Sums(n)
            for k in range(KD):
                b, bi, tk = linear(tile_of("ffn_w_down", (l, j), 128 * k), [(Ht[m][:, 0:n], hs[m]) for m in range(KF)], n)
                residual(b, bi, tk, k, n, gt, tg, sums, xs[k])
            return layer_norm_x(n, sums, lnp, nxt() if nxt else (None, None, None), XM, out_extra)

        gens = []

        def pump(n=1):
            for _ in range(n):
                if gens:
                    try:
                        next(gens[0])
                    except StopIteration:
                        gens.pop(0)

        def drain():
            while gens:
                pump()

        def even_mixer(xs, ms):
            f0 = last()
            QK = [B(4096 + i * 512, 512) for i in range(8)]
            V = [B(8192 + i * 512, 512) for i in range(4)]
            SZ = [B(10240 + i * 512, 512) for i in range(4)]
            YP = [B(12288 + i * 572, 572).rearrange("p (s t) -> p s t", s=2) for i in range(4)]
            CF = [B(14576 + i * 512, 512) for i in range(4)]
            QEF = [B(16624 + i * 512, 512) for i in range(4)]
            WT = [[B(18672 + (4 * d + h) * 512, 512) for h in range(4)] for d in range(2)]
            UST = B(22768, 4096).rearrange("p (s n) -> p s n", s=8)
            AT = [[B(26864 + (4 * d + h) * 256, 256).rearrange("p (t i) -> p t i", t=4) for h in range(4)] for d in range(2)]
            LN0 = 28912
            R1, R2 = B(30960, 512), B(31472, 512)
            CP = Rot([B(22768 + i * 520, 520).rearrange("p (s t) -> p s t", s=2) for i in range(2)])
            for i in range(2):
                CP.free[i] = memset(POOL, CP.bufs[i], 0.0, f0)
            t_yp = [memset(POOL, YP[i], 0.0, f0) for i in range(4)]

            def two(ap):
                return ap.rearrange("p (s t) -> p s t", s=2)

            src = [(XM[k], ms[k]) for k in range(KD)]
            bab, iab, tab = linear(lambda k: [("even_w_in", (0,), 128 * k, 128, 2048 + 4 * r, 4, 32 * r) for r in range(4)], src, T)
            WTf = [B(18672 + i * 512, 512) for i in range(8)]
            xr, mr, er, zr, z2, pr = [w[0:64, :] for w in WTf[0:6]]
            t = ts(DVE, xr, bab[0:64, :], P("dtb")[0:64], None, ADD, None, tab, f0)
            tb = act(R1[64:128, :], bab[64:128, :], ACTF.Sigmoid, tab, f0)
            banks.free[iab] = [t, tb]
            tm = ts(DVE, mr, xr, 0.0, None, ALU.max, None, t)
            t2 = ts(DVE, zr, xr, -1.0, None, MUL, None, t)
            t2 = tt(DVE, zr, zr, xr, ALU.min, t2)
            te = act(er, zr, ACTF.Exp, t2)
            ta = act(nega[0:64], P("alog")[0:64], ACTF.Exp)
            t = ts(DVE, zr, er, 2.0, None, ADD, None, te)
            t = DVE.do(lambda e: e.reciprocal(zr, zr), t)
            t = tt(DVE, zr, zr, er, MUL, t)
            t = tt(DVE, z2, zr, zr, MUL, t)
            t = ts(DVE, pr, z2, 1.0 / 15, None, MUL, None, t)
            for c in (13, 11, 9, 7, 5, 3):
                t = stt(DVE, pr, pr, 1.0 / c, z2, ADD, MUL, t)
            t = stt(DVE, pr, pr, 1.0, zr, ADD, MUL, t)
            t = stt(DVE, pr, pr, 2.0, mr, MUL, ADD, t, tm)
            t = ts(DVE, pr, pr, nega[0:64], -1.0, MUL, MUL, t, ta)
            sgt = WTf[6]
            t1 = memset(DVE, sgt, 1.0, f0)
            t1 = memset(DVE, sgt[:, 0:512:64], 0.0, t1)
            tg1 = DVE.do(lambda e: e.tensor_tensor_scan(R1[0:32, :], sgt[0:32, :], pr[0:32, :], 0.0, MUL, ADD), t, t1)
            tg2 = DVE.do(lambda e: e.tensor_tensor_scan(R1[32:64, ::-1], sgt[32:64, :], pr[32:64, ::-1], 0.0, MUL, ADD), t, t1)
            R1c = R1.rearrange("p (c i) -> p c i", i=64)
            R2c = R2.rearrange("p (c i) -> p c i", i=64)
            t3 = tt(DVE, R2c[0:32], R1c[0:32, :, 63:64].broadcast_to([32, 8, 64]), R1c[0:32], SUB, tg1, f0)
            t4 = tt(DVE, R2c[32:64], R1c[32:64, :, 0:1].broadcast_to([32, 8, 64]), R1c[32:64], SUB, tg2)
            t_r1, t_r2 = [tb, tg1, tg2], [t3, t4]

            t_qkv = []
            for m in range(12):
                b, bi, tk = linear(tile_of("even_w_in", (0,), 128 * m), src, T)
                cp, free, ci = CP.get()
                t = copy(ACT, cp[:, :, 2:258], two(b), tk, free)
                banks.free[bi] = t
                dst = (QK + V)[m]
                ac, afree, ai = tmps.get()
                a3 = two(ac)
                w = lambda j, m=m: P("conv", 5 * m + j, 5 * m + j + 1)
                t = ts(DVE, a3, cp[:, :, 0:256], w(0), None, MUL, None, t, afree)
                for j in range(1, 5):
                    t = stt(DVE, a3, cp[:, :, j:j + 256], w(j), a3, MUL, ADD, t)
                CP.free[ci] = t
                t = act(dst, ac, ACTF.Silu, t, f0)
                tmps.free[ai] = t
                t_qkv.append(t)
            t_y = []
            for m in range(4):
                bv, vi, tv = linear(tile_of("even_w_in", (0,), 2064 + 128 * m), src, T)
                bg, gi, tg = linear(tile_of("even_w_in", (0,), 2576 + 128 * m), src, T)
                g, free, i = tmps.get()
                t = act(g, bg, ACTF.Sigmoid, tg, free)
                banks.free[gi] = t
                t = tt(DVE, YP[m][:, :, 15:271], two(g), two(bv), MUL, t, tv, t_yp[m])
                banks.free[vi] = t
                tmps.free[i] = t
                t_y.append(t)
            t_sz = []
            for m in range(4):
                b, bi, tk = linear(tile_of("even_w_in", (0,), 1536 + 128 * m), src, T)
                t = act(SZ[m], b, ACTF.Silu, tk, f0)
                banks.free[bi] = t
                t_sz.append(t)
            t_xm = PE.mark()

            t_cf = []

            def conformer():
                w = lambda j, m: P("dwc", 31 * m + j, 31 * m + j + 1)
                t = [ts(DVE, two(CF[m]), YP[m][:, :, 0:256], w(0, m), P("dwb", m, m + 1), MUL, ADD, t_y[m], f0) for m in range(4)]
                for j in range(1, 31):
                    for m in range(4):
                        t[m] = stt(DVE, two(CF[m]), YP[m][:, :, j:j + 256], w(j, m), two(CF[m]), MUL, ADD, t[m])
                        if m % 2:
                            yield
                t_cf.extend(t)

            cgen = conformer()

            def cstep(n=1):
                for _ in range(n):
                    next(cgen, None)

            b, free, bi = banks.get()
            for t_ in range(4):
                transp(b[:, t_ * 128:(t_ + 1) * 128], R1[:, t_ * 128:(t_ + 1) * 128], 128, free, t_r1)
            tk = PE.mark()
            cA4 = colA.rearrange("p (t q h) -> p t q h", t=4, q=4)
            t_ca = copy(DVE, cA4, b.rearrange("p (t q r) -> p t q r", t=4, q=4)[:, :, :, 0:4], tk)
            banks.free[bi] = t_ca
            b, free, bi = banks.get()
            for t_ in range(4):
                transp(b[:, t_ * 64:(t_ + 1) * 64], R2[0:64, t_ * 128:(t_ + 1) * 128], 64, free, t_r2)
            tk = PE.mark()
            cT4 = colT.rearrange("p (t q h) -> p t q h", t=4, q=2)
            t_ct = act(cT4, b[:, 0:256].rearrange("p (t q r) -> p t q r", t=4, q=2)[:, :, :, 0:4], ACTF.Exp, tk)
            banks.free[bi] = t_ct
            cB4 = colB.rearrange("p (t q h) -> p t q h", t=4, q=2)
            t = act(cB4, cA4[:, :, 0:2, :], ACTF.Exp, t_ca)
            t_cb = tt(DVE, cB4, cB4, cA4[:, :, 2:4, :], MUL, t)

            t_qk = []
            for m in range(8):
                sq, free, i = sqs.get()
                t = act(sq, QK[m], ACTF.Square, t_qkv[m], free)
                b, bfree, bi = banks.get()
                mm(b, P("ones"), sq, True, True, t, bfree)
                tk = PE.mark()
                r, rfree, ri = tmps.get()
                sqs.free[i] = tk
                t = act(r, b, ACTF.Sqrt, tk, rfree, scale=128.0 if m < 4 else 1.0, bias=P("eps128") if m < 4 else P("eps6"))
                banks.free[bi] = t
                t = DVE.do(lambda e, r=r: e.reciprocal(r, r), t)
                t = tt(DVE, QK[m], QK[m], r, MUL, t)
                tmps.free[ri] = t
                t_qk.append(t)
                cstep()

            KT = [B(t_ * 512, 512) for t_ in range(4)]
            VT = [B(2048 + t_ * 512, 512) for t_ in range(4)]
            t_kt, t_vt = [], []
            for dst, srcs, toks, out in ((KT, QK[4:8], t_qk[4:8], t_kt), (VT, V, t_qkv[8:12], t_vt)):
                for t_ in range(4):
                    b, free, bi = banks.get()
                    for h in range(4):
                        transp(b[:, h * 128:(h + 1) * 128], srcs[h][:, t_ * 128:(t_ + 1) * 128], 128, free, toks[h])
                    tk = PE.mark()
                    t = copy(ACT, dst[t_], b, tk, t_xm)
                    banks.free[bi] = t
                    out.append(t)
                pump()
            t_vT = PE.mark()

            def ch(ap, d3=64):
                return ap.rearrange("p (t i) -> p t i", t=4)

            def bc(ap):
                return ap.unsqueeze(1).broadcast_to([128, 4, 64])

            def halfblocks(c):
                return c % 2, c // 2, slice(64 * (c % 2), 64 * (c % 2) + 64)

            id64 = P("id64")
            egl = colG.rearrange("p (d h c) -> p d h c", d=2, h=4)
            t_at, t_w, t_u, t_qe, t_egl = {}, {}, {}, {}, {}
            lanefree = [f0, f0]
            for h in range(4):
                bG, gfree, gi = banks.get()
                for kind, other in ((0, QK[h]), (1, QK[4 + h])):
                    for c in range(8):
                        p, t_, rows_ = halfblocks(c)
                        mm(bG[rows_, kind * 256 + t_ * 64:kind * 256 + t_ * 64 + 64], QK[4 + h][:, 64 * c:64 * c + 64],
                           other[:, 64 * c:64 * c + 64], True, True, gfree, t_qk[h], t_qk[4 + h])
                t_g = PE.mark()
                gread = []
                lanes = []
                for d in range(2):
                    n = "fb"[d]
                    base = LN0 + d * 1024
                    Mt, TU, Pm = B(base, 256), B(base + 256, 512), B(base + 768, 256)
                    b, free, bi = banks.get()
                    for kind, r in ((0, 32 * d + h), (1, 64 + 32 * d + h)):
                        for p in range(2):
                            mm(b[64 * p:64 * p + 64, kind * 256:kind * 256 + 256].rearrange("p (t i) -> p t i", t=4),
                               P("ident")[:, r:r + 1].broadcast_to([128, 64]),
                               R1.rearrange("r (t p i) -> r t p i", p=2, i=64)[:, :, p, :], True, True, free, t_r1)
                    tk = PE.mark()
                    E = Pm
                    t = tt(DVE, ch(E), ch(b[:, 0:256]), cA4[:, :, d, h:h + 1].broadcast_to([128, 4, 64]), SUB, tk, t_ca, lanefree[d])
                    tbm = tt(DVE, ch(Mt), ch(b[:, 256:512]), bc(P(f"str_{n}")), MUL, lanefree[d])
                    banks.free[bi] = [t, tbm]
                    t = ts(POOL, E, E, 0.0, None, ALU.min, None, t)
                    t = act(E, E, ACTF.Exp, t)
                    t = tt(POOL, ch(E), ch(E), bc(P(f"inc_{n}")), MUL, t)
                    ta = tt(DVE, AT[d][h], ch(E), ch(bG[:, 0:256]), MUL, t, t_g)
                    t_at[d, h] = ta
                    tmm = tt(POOL, Mt, Mt, E, MUL, t, tbm)
                    tmm = tt(DVE, Mt, Mt, bG[:, 256:512], MUL, tmm)
                    gread += [ta, tmm]
                    U = TU[:, 256:512]
                    t = tt(POOL, ch(U), ch(Mt), bc(P(f"u1_{n}")), MUL, tmm, lanefree[d])
                    t = tt(POOL, ch(U), ch(U), bc(id64), ADD, t)
                    b, free, bi = banks.get()
                    for c in range(8):
                        p, t_, rows_ = halfblocks(c)
                        mm(b[rows_, t_ * 64:t_ * 64 + 64], U[rows_, t_ * 64:t_ * 64 + 64], id64[rows_, :], True, True, free, t)
                    tk = PE.mark()
                    tT = copy(ACT, TU[:, 0:256], b[:, 0:256], tk, lanefree[d])
                    banks.free[bi] = tT
                    lanes.append([Mt, TU, Pm, [t, tT], ta, tmm])
                    cstep()
                banks.free[gi] = gread
                for d in range(2):
                    b, free, bi = banks.get()
                    r = 32 * d + h
                    mm(b, P("ident")[:, r:r + 1].broadcast_to([128, 128]), R1, True, True, free, t_r1)
                    tk = PE.mark()
                    if d == 0:
                        e_, efree = QEF[h], f0
                    else:
                        e_, efree, ei = tmps.get()
                    t = act(e_, b, ACTF.Exp, tk, efree)
                    banks.free[bi] = t
                    o_ = 63 if d == 0 else 0
                    t_egl[d, h] = copy(POOL, egl[:, d, h, :], e_[:, o_:512:64], t)
                    dst = QEF[h] if d == 0 else QK[h]
                    t = tt(DVE, dst, QK[h], e_, MUL, t, t_g, t_egl[d, h], t_qe.get((0, h)))
                    t_qe[d, h] = t
                    if d:
                        tmps.free[ei] = t
                for lv in (2, 4, 8, 16, 32):
                    for d in range(2):
                        Mt, TU, Pm, tTU, ta, tmm = lanes[d]
                        b, free, bi = banks.get()
                        for c in range(8):
                            p, t_, rows_ = halfblocks(c)
                            cs_ = slice(t_ * 64, t_ * 64 + 64)
                            mm(b[rows_, cs_], Mt[rows_, cs_], TU[rows_, cs_], True, True, free, tTU, tmm)
                        tk = PE.mark()
                        tP = tt(DVE, ch(Pm), ch(b[:, 0:256]), bc(P(f"lv{lv}_{'fb'[d]}")), MUL, tk, ta, tmm)
                        banks.free[bi] = tP
                        lanes[d].append(tP)
                    for d in range(2):
                        Mt, TU, Pm, tTU, ta, tmm, tP = lanes[d]
                        b, free, bi = banks.get()
                        for c in range(8):
                            p, t_, rows_ = halfblocks(c)
                            cs_ = slice(t_ * 64, t_ * 64 + 64)
                            us_ = slice(256 + t_ * 64, 256 + t_ * 64 + 64)
                            if lv < 32:
                                mm(b[rows_, cs_], TU[rows_, us_], Pm[rows_, cs_], True, True, free, tP)
                            mm(b[rows_, us_], Pm[rows_, cs_], TU[rows_, us_], True, True, free, tP)
                        tk = PE.mark()
                        a = 0 if lv < 32 else 256
                        t = tt(DVE, TU[:, a:512], TU[:, a:512], b[:, a:512], SUB, tk)
                        banks.free[bi] = t
                        lanes[d] = [Mt, TU, Pm, t, ta, tmm]
                    cstep()
                pump()
                for d in range(2):
                    Mt, TU, Pm, tU, ta, tmm = lanes[d]
                    U = TU[:, 256:512]
                    Ub, Uw = TU[:, 0:256], Pm
                    t1 = tt(DVE, ch(Ub), ch(U), cA4[:, :, 2 + d, h:h + 1].broadcast_to([128, 4, 64]), MUL, tU)
                    t2 = tt(DVE, ch(Uw), ch(U), cB4[:, :, d, h:h + 1].broadcast_to([128, 4, 64]), MUL, tU, t_cb)
                    b, free, bi = banks.get()
                    for c in range(8):
                        p, t_, rows_ = halfblocks(c)
                        sl = (t_ ^ 2) if d == 0 else 3 - t_
                        mm(b[rows_, sl * 128:sl * 128 + 128], Ub[rows_, t_ * 64:t_ * 64 + 64], VT[t_][rows_, h * 128:(h + 1) * 128],
                           True, True, free, t1, t_vt)
                    tk = PE.mark()
                    tu = []
                    for p in range(2):
                        sp_ = p if d == 0 else 1 - p
                        rows_ = slice(64 * p, 64 * p + 64)
                        tu.append(copy(ACT, UST[rows_, sp_:8:2, h * 128:(h + 1) * 128], b[rows_, :].rearrange("p (s n) -> p s n", s=4), tk, t_qkv))
                    banks.free[bi] = tu
                    t_u[d, h] = tu
                    bb_ = [banks.get() for _ in range(2)]
                    for c in range(8):
                        p, t_, rows_ = halfblocks(c)
                        mm(bb_[p][0][:, 64 * t_:64 * t_ + 64], KT[t_][rows_, h * 128:(h + 1) * 128], Uw[rows_, t_ * 64:t_ * 64 + 64],
                           True, True, bb_[p][1], t2, t_kt)
                    tk = PE.mark()
                    for p in range(2):
                        t_w[d, h] = copy(ACT, WT[d][h].rearrange("p (t s i) -> p t s i", t=4, s=2)[:, :, p, :], ch(bb_[p][0][:, 0:256]), tk, tg1, tg2)
                        banks.free[bb_[p][2]] = t_w[d, h]
                    lanefree[d] = [tk, tu[0]]
                pump()

            fs = last()
            S = [B(6144 + d * 512, 512) for d in range(2)]
            SD = [B(7168 + d * 512, 512) for d in range(2)]
            KTL = Rot([B(LN0 + i * 512, 512) for i in range(2)])
            VN = Rot([B(LN0 + 1024 + i * 512, 512) for i in range(2)])
            oT = B(8192, 2048).rearrange("p (h t) -> p h t", h=4)
            tS = [memset(POOL, S[d], 0.0, fs) for d in range(2)]
            order = [[4, 5, 6, 7, 0, 1, 2, 3], [7, 6, 5, 4, 3, 2, 1, 0]]
            seen, t_o = set(), {}
            for s in range(8):
                cc = [order[d][s] for d in range(2)]
                kt_, kfree, ki = KTL.get()
                if s < 7:
                    tkt = []
                    for d in range(2):
                        p, t_, rows_ = halfblocks(cc[d])
                        tkt.append(tt(DVE, kt_[rows_, :].rearrange("p (h n) -> p h n", h=4), KT[t_][rows_, :].rearrange("p (h n) -> p h n", h=4),
                                      cT4[rows_, t_, d, :].unsqueeze(2).broadcast_to([64, 4, 128]), MUL, kfree, fs, t_ct))
                b, free, bi = banks.get()
                for d in range(2):
                    p, t_, rows_ = halfblocks(cc[d])
                    for h in range(4):
                        mm(b[rows_, h * 128:(h + 1) * 128], WT[d][h][:, 64 * cc[d]:64 * cc[d] + 64], S[d][:, h * 128:(h + 1) * 128],
                           True, True, free, tS[d], t_w[d, h])
                tk = PE.mark()
                vn, vfree, vi = VN.get()
                tv = tt(DVE, vn, UST[:, s, :], b, SUB, tk, vfree, fs)
                banks.free[bi] = tv
                if s < 7:
                    tsd = []
                    for d in range(2):
                        g3 = egl[:, d, :, cc[d]:cc[d] + 1].broadcast_to([128, 4, 128])
                        tsd.append(tt(POOL, SD[d].rearrange("p (h n) -> p h n", h=4), S[d].rearrange("p (h n) -> p h n", h=4), g3, MUL, tS[d], [t_egl[d, h] for h in range(4)]))
                bo = [banks.get() for _ in range(2)]
                b4 = [x_[0][:, 0:256].rearrange("p (h i) -> p h i", h=4) for x_ in bo]
                for d in range(2):
                    p, t_, rows_ = halfblocks(cc[d])
                    for h in range(4):
                        qe = QEF[h] if d == 0 else QK[h]
                        mm(b4[d][:, h, :], S[d][:, h * 128:(h + 1) * 128], qe[:, 64 * cc[d]:64 * cc[d] + 64], True, False, bo[d][1], t_qe[d, h])
                        mm(b4[d][:, h, :], vn[rows_, h * 128:(h + 1) * 128], AT[d][h][rows_, t_, :], False, True, tv, t_at[d, h])
                tok = PE.mark()
                upd = []
                if s < 7:
                    for d in range(2):
                        p, t_, rows_ = halfblocks(cc[d])
                        b, free, bi = banks.get()
                        for h in range(4):
                            mm(b[:, h * 128:(h + 1) * 128], kt_[rows_, h * 128:(h + 1) * 128], vn[rows_, h * 128:(h + 1) * 128], True, True, free, tkt, tv)
                        tk = PE.mark()
                        tS[d] = tt(DVE, S[d], SD[d], b, ADD, tk, tsd[d], tok)
                        banks.free[bi] = tS[d]
                    KTL.free[ki] = tk
                else:
                    KTL.free[ki] = tok
                VN.free[vi] = PE.mark()
                for d in range(2):
                    c = cc[d]
                    dst = oT[:, :, 64 * c:64 * c + 64]
                    if c not in seen:
                        t = copy(ACT, dst, b4[d], tok, t_vT)
                    else:
                        t = tt(DVE, dst, dst, b4[d], ADD, tok, t_o[c])
                    seen.add(c)
                    t_o[c] = t
                    banks.free[bo[d][2]] = t
                cstep(2)
                pump()
            cstep(100)
            t_ox = list(t_o.values())

            fm = last()
            HM = [B(i * 512, 512) for i in range(8)]
            thm = []
            for h in range(4):
                o_ = B(8192 + h * 512, 512)
                sq, free, i = sqs.get()
                t = act(sq, o_, ACTF.Square, t_ox, free)
                b, bfree, bi = banks.get()
                mm(b, P("ones128"), sq, True, True, t, bfree)
                tk = PE.mark()
                sqs.free[i] = tk
                r, rfree, ri = tmps.get()
                t = act(r, b, ACTF.Sqrt, tk, rfree, bias=P("eps6"))
                banks.free[bi] = t
                t = DVE.do(lambda e, r=r: e.reciprocal(r, r), t)
                t = tt(DVE, r, r, o_, MUL, t)
                t = stt(DVE, HM[h], r, P("onorm"), SZ[h], MUL, MUL, t, t_sz[h], fm)
                tmps.free[ri] = t
                thm.append(t)
            b1, f1, i1 = banks.get()
            for m in range(4):
                mm(b1, P("ones512"), CF[m], m == 0, m == 3, f1, t_cf[m])
            tk1 = PE.mark()
            b2, f2, i2 = banks.get()
            for m in range(4):
                sq, free, i = sqs.get()
                t = act(sq, CF[m], ACTF.Square, t_cf[m], free)
                mm(b2, P("ones512"), sq, m == 0, m == 3, f2, t)
                sqs.free[i] = PE.mark()
            tk2 = PE.mark()
            mean, rstd = w_mean, w_rstd
            tm = copy(ACT, mean, b1, tk1, fm)
            banks.free[i1] = tm
            t = tt(DVE, rstd, mean, mean, MUL, tm, fm)
            t = tt(DVE, rstd, b2, rstd, SUB, t, tk2)
            banks.free[i2] = t
            t = ts(DVE, rstd, rstd, 0.0, None, ALU.max, None, t)
            t = act(rstd, rstd, ACTF.Sqrt, t, bias=P("eps5"))
            tr = DVE.do(lambda e: e.reciprocal(rstd, rstd), t)
            for m in range(4):
                t = tt(DVE, CF[m], CF[m], mean, SUB, tr, tk2)
                t = tt(DVE, CF[m], CF[m], rstd, MUL, t)
                t = act(HM[4 + m], CF[m], ACTF.Silu, t, fm, scale=P("clg", m, m + 1), bias=P("clb", m, m + 1))
                thm.append(t)

            gt, tg = gate_cols(0, 5, 1.0)
            sums = Sums(T, tok=[t, tr])
            srcs = [(HM[k], thm[k]) for k in range(8)]
            for k in range(KD):
                b, bi, tk = linear(tile_of("even_w_out", (0,), 128 * k), srcs, T)
                residual(b, bi, tk, k, T, gt, tg, sums, xs[k])
            return layer_norm_x(T, sums, ("ln_g01", "ln_b01"), norm_cols("ln_g01", "ln_b01", 0, 6, 7, None), XM, last())

        def attend(items, PB, PT, stat):

            def scores(it):
                qs, (k, tk_), scale, mask, v, rows_, sink = it
                nq = len(qs)
                nk = 512 // nq
                b, free, bi = banks.get()
                for i, (q, tq) in enumerate(qs):
                    mm(b[:, i * nk:(i + 1) * nk], q, k, True, True, free, tq, tk_)
                t = PE.mark()
                p, pfree, pi = PB.get()
                st, sfree, si = stat.get()
                src = b
                if mask is not None:
                    t = tt(DVE, p, b, mask[0], ADD, t, pfree, mask[1])
                    banks.free[bi] = t
                    src = p
                mx, nb, sm_, rc = (st[:, 2 * j:2 * j + nq] for j in range(4))
                t = DVE.do(lambda e: e.tensor_reduce(mx, src.rearrange("p (i k) -> p i k", i=nq), AXX, ALU.max), t, sfree)
                t = ts(DVE, nb, mx, -scale, None, MUL, None, t)
                for i in range(nq):
                    te = act(p[:, i * nk:(i + 1) * nk], src[:, i * nk:(i + 1) * nk], ACTF.Exp, t, pfree,
                             bias=nb[:, i:i + 1], scale=scale, accum_out=sm_[:, i:i + 1])
                if mask is None:
                    banks.free[bi] = te
                t = DVE.do(lambda e: e.reciprocal(rc, sm_), te)
                for i in range(nq):
                    t2 = ts(DVE, p[:, i * nk:(i + 1) * nk], p[:, i * nk:(i + 1) * nk], rc[:, i:i + 1], None, MUL, None, t)
                stat.free[si] = t2
                return p, pi, t2, nq, nk

            def turn(it, sc):
                p, pi, tp_, nq, nk = sc
                b, free, bi = banks.get()
                for i in range(nq):
                    for k in range(nk // 128):
                        transp(b[:, (k * nq + i) * 128:(k * nq + i + 1) * 128], p[:, i * nk + k * 128:i * nk + (k + 1) * 128], 128, free, tp_)
                t = PE.mark()
                PB.free[pi] = t
                pt, ptfree, pti = PT.get()
                t = copy(ACT, pt, b, t, ptfree)
                banks.free[bi] = t
                return pt, pti, t, nq, nk

            def values(it, tr):
                pt, pti, tp_, nq, nk = tr
                v, rows_, sink = it[4:7]
                b, free, bi = banks.get()
                o = b[rows_, 0:nq * 128]
                for k in range(nk // 128):
                    va, vt = v(k)
                    mm(o, va, pt[:, k * nq * 128:(k + 1) * nq * 128], k == 0, k == nk // 128 - 1, free, tp_, vt)
                t = PE.mark()
                PT.free[pti] = t
                banks.free[bi] = sink(o, t)

            a, c = [], []
            for it in list(items) + [None, None]:
                if c:
                    values(*c.pop(0))
                if a:
                    i0, sc = a.pop(0)
                    c.append((i0, turn(i0, sc)))
                if it is not None:
                    a.append((it, scores(it)))
                yield

        stats = Rot([sm(8) for _ in range(4)])

        def rope(raw, traw, n, rt, C, S, out, ofree):
            b, free, bi = banks.get()
            mm(b[:, 0:256], P(rt), raw[:, 0:256], True, True, free, traw)
            tk = PE.mark()
            t, tfree, ti = tmps.get()
            t1 = tt(DVE, t[:, 0:256], b[:, 0:256], P(S), MUL, tk, tfree)
            banks.free[bi] = t1
            t2 = tt(POOL, out[:, 0:256], raw[:, 0:256], P(C), MUL, traw, ofree, tk)
            t3 = tt(DVE, out[:, 0:256], out[:, 0:256], t[:, 0:256], ADD, t1, t2)
            tmps.free[ti] = t3
            return t3

        def odd_mixer(xs, ms):
            f0 = last()
            Q = [B(4096 + h * 256, 256) for h in range(8)]
            K = [B(6144 + h * 512, 512) for h in range(2)]
            VK = [B(7168 + k * 256, 256) for k in range(4)]
            O = [B(8192 + h * 256, 256) for h in range(8)]
            PB = Rot([B(10240 + i * 512, 512) for i in range(3)])
            PT = Rot([B(11776 + i * 512, 512) for i in range(3)])
            raws = Rot([B(13312 + i * 512, 512) for i in range(3)])
            scale = 128.0 ** -0.5

            def headnorm(m, n, g, dst):
                b, bi, tk = linear(tile_of("attn_w_in", (0,), 128 * m), [(XM[k][:, 0:n], ms[k]) for k in range(KD)], n)
                sq, free, i = sqs.get()
                t = act(sq[:, 0:n], b[:, 0:n], ACTF.Square, tk, free)
                b2, f2, i2 = banks.get()
                mm(b2[:, 0:n], P("ones128"), sq[:, 0:n], True, True, f2, t)
                tk2 = PE.mark()
                sqs.free[i] = tk2
                r, rfree, ri = tmps.get()
                t = act(r[:, 0:n], b2[:, 0:n], ACTF.Sqrt, tk2, rfree, bias=P("eps6"))
                banks.free[i2] = t
                t = DVE.do(lambda e: e.reciprocal(r[:, 0:n], r[:, 0:n]), t)
                raw, wfree, wi = raws.get()
                t = stt(DVE, raw[:, 0:n], b[:, 0:n], P(g), r[:, 0:n], MUL, MUL, t, wfree, f0)
                banks.free[bi] = t
                tmps.free[ri] = t
                if n > 256:
                    t = [t, copy(POOL, dst[:, 256:n], raw[:, 256:n], t, f0)]
                t3 = [rope(raw, t, n, "rotT", "ropeC", "ropeS", dst, f0)] + (t[1:] if n > 256 else [])
                raws.free[wi] = t3
                return t3

            tK = [headnorm(8 + h, T, "kn", K[h]) for h in range(2)]
            bs = [banks.get() for _ in range(4)]
            for k in range(KD):
                wt, wtok = take([("attn_w_in", (0,), 128 * k, 128, 1280, 256, 0)], 256)
                for i in range(4):
                    mm(bs[i][0][:, 0:256], XM[k][:, i * 128:(i + 1) * 128], wt, k == 0, k == KD - 1, bs[i][1], wtok, ms[k])
            tk = PE.mark()
            tV = []
            for i in range(4):
                t = copy(ACT, VK[i], bs[i][0][:, 0:256], tk, f0)
                banks.free[bs[i][2]] = t
                tV.append(t)
            tO = {}
            for h in range(8):
                tq = headnorm(h, 256, "qn", Q[h])

                def items(h=h, tq=tq):
                    for i in range(2):
                        g = h // 4

                        def sink(o, t, h=h, i=i):
                            tO[h, i] = copy(ACT, O[h][:, i * 128:(i + 1) * 128], o, t, f0)
                            return tO[h, i]

                        yield ([(Q[h][:, i * 128:(i + 1) * 128], tq)], (K[g], tK[g]), scale, None,
                               lambda k, g=g: (VK[k][:, g * 128:(g + 1) * 128], tV[k]), slice(0, 128), sink)

                gens.append(attend(items(), PB, PT, stats))
                pump(3)
            drain()
            gt, tg = gate_cols(1, 5, 1.0)
            sums = Sums(L)
            srcs = [(O[h], [tO[h, 0], tO[h, 1]]) for h in range(8)]
            for k in range(KD):
                b, bi, tk = linear(tile_of("attn_w_out", (0,), 128 * k), srcs, L)
                residual(b, bi, tk, k, L, gt, tg, sums, xs[k])
            return layer_norm_x(L, sums, ("ln_g11", "ln_b11"), norm_cols("ln_g11", "ln_b11", 1, 6, 7, None), XM, last())

        def second_block(xs, depth):
            f0 = last()
            MX = [X[:, k * T + 256:(k + 1) * T] for k in range(KD)]
            SP.wait(f0)
            SP.ops.append([lambda e: e.dma_start(X.rearrange("p (k t) -> p k t", k=KD)[:, :, 256:512], MT.rearrange("p (k t) -> p k t", k=KD)).then_inc(s_m, 16), None, 0])
            sums = Sums(L, both=False)
            for k in range(KD):
                sums.add(MX[k], (s_m, 16))
            tr = sums.finish("onesD", "eps6")
            t_mx = [tt(DVE, MX[k], MX[k], w_rstd[:, 0:L], MUL, tr) for k in range(KD)]

            def tiles(a, n=4, w=256):
                return [B(a + i * w, w) for i in range(n)]

            HH, MN, MG = tiles(0, 8), tiles(2048, 8), tiles(2048, 8)
            QA, KA, QB, KB = (tiles(4096 + 1024 * i) for i in range(4))
            VA, VB = tiles(8192, 2, 512), tiles(9216, 2, 512)
            GA, GB, GM = (tiles(10240 + 1024 * i) for i in range(3))
            QI, KI = tiles(13312), B(14336, 256)
            MQ = tiles(14592)
            MIX = tiles(15616, 24)
            KM, VM = tiles(21760), tiles(22784, 2, 512)
            YA, YB, YM = (tiles(23808 + 1024 * i) for i in range(3))
            PT = Rot(tiles(26880, 2, 512))
            IDX, SEL = B(28928, 512), B(29440, 512)
            WKI = B(27904, 512)
            PB = Rot(tiles(29952, 3, 512))
            tsum = None
            for l in range(depth):
                fl = last()
                t_mn = [ts(DVE, MN[k], MX[k], P(f"mnorm2_{l}", k, k + 1), None, MUL, None, t_mx[k], fl) for k in range(KD)]
                srcm = [(MN[k], t_mn[k]) for k in range(KD)]
                if tsum is None:
                    sums = Sums(L, both=False)
                    for k in range(KD):
                        sums.add(Xt[k][:, 0:L], xs[k])
                else:
                    sums = tsum
                tKM, tVM = [], []
                for m in range(4):
                    b, bi, tk = linear(tile_of("w_mem_kv_2", (l,), 128 * m), srcm, L)
                    tKM.append(copy(ACT, KM[m], b[:, 0:L], tk, fl))
                    banks.free[bi] = tKM[-1]
                tr = sums.finish("onesD", "eps6")
                t_h = [stt(DVE, HH[k], Xt[k][:, 0:L], P(f"norm2_{l}", k, k + 1), w_rstd[:, 0:L], MUL, MUL, tr, fl) for k in range(KD)]

                def by_token(name, idx, c0, src, out, fr):
                    bs = [banks.get() for _ in range(2)]
                    for k in range(KD):
                        wt, wtok = take([(name, idx, 128 * k, 128, c0, 512, 0)], 512)
                        for i in range(2):
                            mm(bs[i][0], src[k][0][:, i * 128:(i + 1) * 128], wt, k == 0, k == KD - 1, bs[i][1], wtok, src[k][1])
                    tk = PE.mark()
                    res = []
                    for i in range(2):
                        res.append(copy(ACT, out[i], bs[i][0], tk, fr))
                        banks.free[bs[i][2]] = res[-1]
                    return res

                tVM = by_token("w_mem_kv_2", (l,), 512, srcm, VM, fl)
                src = [(HH[k], t_h[k]) for k in range(KD)]

                def proj(piece, m):
                    r = linear(tile_of("w_in_2", (l,), OFF2[piece] + 128 * m), src, L)
                    return r

                def roped(r, dst):
                    b, bi, tk = r
                    raw, free, i = sqs.get()
                    t = copy(ACT, raw[:, 0:256], b[:, 0:256], tk, free)
                    banks.free[bi] = t
                    t = rope(raw, t, L, "prT", "prC", "prS", dst, fl)
                    sqs.free[i] = t
                    return t

                def gated(piece, m, dst, fn):
                    b, bi, tk = proj(piece, m)
                    t = act(dst, b[:, 0:L], fn, tk, fl)
                    banks.free[bi] = t
                    return t

                r = linear(lambda k: [("w_in_2", (l,), 128 * k, 128, OFF2[9], 64, 0), ("w_in_2", (l,), 128 * k, 128, OFF2[9], 64, 64)], src, L)
                tKI = roped(r, KI)
                wt, wtok = take([("w_in_2", (l,), 128 * k, 128, OFF2[10], 8, 8 * k) for k in range(KD)], 64)
                b, free, bi = banks.get()
                for i in range(2):
                    for k in range(KD):
                        mm(b[:, 8 * i:8 * i + 8], HH[k][:, i * 128:(i + 1) * 128], wt[:, 8 * k:8 * k + 8], k == 0, k == KD - 1, free, wtok, t_h[k])
                tk = PE.mark()
                t_wi = ts(DVE, wi, b[:, 0:16], 8 ** -0.5, 0.125, MUL, MUL, tk, fl)
                banks.free[bi] = t_wi
                tQI = [roped(proj(8, m), QI[m]) for m in range(4)]
                selt = []

                def index():
                    ta = copy(POOL, IDX, P("causal"), fl)
                    for h in range(8):
                        rows_ = slice(64 * (h % 2), 64 * (h % 2) + 64)
                        b, free, bi = banks.get()
                        for i in range(2):
                            mm(b[:, 256 * i:256 * i + 256], QI[h // 2][rows_, i * 128:(i + 1) * 128], KI[rows_, :], True, True, free, tQI[h // 2], tKI)
                        tk = PE.mark()
                        rl, rfree, ri = tmps.get()
                        t = act(rl, b, ACTF.Relu, tk, rfree)
                        banks.free[bi] = t
                        for i in range(2):
                            ta2 = stt(DVE, IDX[:, 256 * i:256 * i + 256], rl[:, 256 * i:256 * i + 256], wi[:, 8 * i + h:8 * i + h + 1],
                                      IDX[:, 256 * i:256 * i + 256], MUL, ADD, t, ta, t_wi)
                        ta = ta2
                        tmps.free[ri] = ta
                        yield
                    tm = [ta, ta]
                    for r_ in range(8):
                        a, o = (IDX, WKI) if r_ % 2 == 0 else (WKI, IDX)
                        for i in range(2):
                            s_ = slice(256 * i, 256 * i + 256)
                            tm[i] = DVE.do(lambda e, a=a, s_=s_, i=i: e.max(mx8[:, 8 * i:8 * i + 8], a[:, s_]), tm[i], fl)
                        for i in range(2):
                            s_ = slice(256 * i, 256 * i + 256)
                            tm[i] = DVE.do(lambda e, a=a, o=o, s_=s_, i=i: e.match_replace(o[:, s_], mx8[:, 8 * i:8 * i + 8], a[:, s_], -2.0 ** 127), tm[i])
                        if r_ % 2:
                            yield
                    t = tm
                    t = ts(DVE, SEL, IDX, -2.0 ** 127, NEG, ALU.not_equal, MUL, t)
                    t = tt(DVE, SEL, SEL, P("causal"), ALU.min, t)
                    selt.append(t)
                    yield

                gens.append(index())

                def branch_heads(Q, tQ, K, tK, V, tV, G, tG, Y, tY, mask):
                    for h in range(8):
                        rows_ = slice(64 * (h % 2), 64 * (h % 2) + 64)
                        m = h // 2

                        def sink(o, t, h=h, m=m, rows_=rows_):
                            tY.append(tt(DVE, Y[m][rows_, :], o, G[m][rows_, :], MUL, t, tG[m], fl))
                            return tY[-1]

                        yield ([(Q[m][rows_, i * 128:(i + 1) * 128], tQ[m]) for i in range(2)], (K[m][rows_, :], tK[m]), 0.125,
                               mask(), lambda k, h=h: (V[k][:, h * 64:(h + 1) * 64], tV[k]), rows_, sink)

                tY = [[], [], []]

                def qkvg(p0, Q, K, V, G):
                    tQ, tK, tG = [], [], []
                    for m in range(4):
                        tQ.append(roped(proj(p0, m), Q[m]))
                        pump()
                        tK.append(roped(proj(p0 + 1, m), K[m]))
                        pump()
                    tV = by_token("w_in_2", (l,), OFF2[p0 + 2], src, V, fl)
                    pump()
                    for m in range(4):
                        tG.append(gated(p0 + 3, m, G[m], ACTF.Silu))
                        pump()
                    return tQ, tK, tV, tG

                tQ, tK, tV, tG = qkvg(0, QA, KA, VA, GA)
                gens.append(attend(branch_heads(QA, tQ, KA, tK, VA, tV, GA, tG, YA, tY[0], lambda: (P("causal"), None)), PB, PT, stats))
                tQ, tK, tV, tG = qkvg(4, QB, KB, VB, GB)
                gens.append(attend(branch_heads(QB, tQ, KB, tK, VB, tV, GB, tG, YB, tY[1], lambda: (SEL, selt[0])), PB, PT, stats))
                tMQ, tGM = [], []
                for m in range(4):
                    tMQ.append(gated(11, m, MQ[m], ACTF.Copy))
                    pump()
                    tGM.append(gated(12, m, GM[m], ACTF.Silu))
                    pump()

                def memory_heads():
                    for h in range(4):
                        def sink(o, t, h=h):
                            tY[2].append(tt(DVE, YM[h], o, GM[h], MUL, t, tGM[h], fl))
                            return tY[2][-1]

                        yield ([(MQ[h][:, i * 128:(i + 1) * 128], tMQ[h]) for i in range(2)], (KM[h], tKM[h]), 128.0 ** -0.5, None,
                               lambda k, h=h: (VM[k][:, h * 128:(h + 1) * 128], tVM[k]), slice(0, 128), sink)

                gens.append(attend(memory_heads(), PB, PT, stats))
                tX = []
                for m in range(24):
                    tX.append(gated(13, m, MIX[m], ACTF.Sigmoid))
                    pump()
                drain()
                t_mg = []
                fmg = last()
                for m in range(KD):
                    prev = None
                    for n, Y in enumerate((YA, YB, YM)):
                        b, bi, tk = linear(tile_of("w_branch_2", (l, n), 128 * m), [(Y[k], tY[n]) for k in range(4)], L)
                        t, free, i = tmps.get()
                        dst = MG[m] if n == 0 else t[:, 0:L]
                        t1 = tt(DVE, dst, b[:, 0:L], MIX[8 * n + m], MUL, tk, tX[8 * n + m], free, fmg)
                        banks.free[bi] = t1
                        if n:
                            t1 = tt(DVE, MG[m], MG[m], t[:, 0:L], ADD, t1, prev)
                        tmps.free[i] = t1
                        prev = t1
                    t_mg.append(prev)
                tsum = Sums(L, both=False)
                nxs = []
                for k in range(KD):
                    b, bi, tk = linear(tile_of("w_out_2", (l,), 128 * k), [(MG[m], t_mg[m]) for m in range(KD)], L)
                    x = Xt[k][:, 0:L]
                    t = tt(DVE, x, x, b[:, 0:L], ADD, tk)
                    banks.free[bi] = t
                    tsum.add(x, t)
                    nxs.append(t)
                xs = nxs
            if depth == 2:
                tr = tsum.finish("onesD", "eps6")
                xs = [stt(DVE, Xt[k][:, 0:L], Xt[k][:, 0:L], P("fin_g", k, k + 1), w_rstd[:, 0:L], MUL, MUL, tr) for k in range(KD)]
            return xs

        gens.append(ada(0))
        drain()
        G, Bc, tcol = norm_cols(None, None, 0, 0, 1, None)
        ms = []
        for k in range(KD):
            for s, a, b in halves(T):
                t = ts(DVE, XM[k][:, a:b], Xt[k][:, a:b], G[:, k, s:s + 1], Bc[:, k, s:s + 1], MUL, ADD, tx, tcol)
            ms.append(t)
        xs = [tx] * KD
        xs, ms = ffn(0, 0, T, xs, ms, ("ln_g00", "ln_b00"), lambda: norm_cols("ln_g00", "ln_b00", 0, 3, 4, None))

        if stage != "ffn0":
            gens.append(ada(1))
            xs, ms = even_mixer(xs, ms)
        if stage not in ("ffn0", "even"):
            drain()
            xs, ms = ffn(0, 1, T, xs, ms, ("ln_g02", "ln_b02"), lambda: norm_cols("ln_g02", "ln_b02", 1, 0, 1, None))
            xs, ms = ffn(1, 0, T, xs, ms, ("ln_g10", "ln_b10"), lambda: norm_cols("ln_g10", "ln_b10", 1, 3, 4, None))
        if stage not in ("ffn0", "even", "l1f"):
            xs, ms = odd_mixer(xs, ms)
        if stage not in ("ffn0", "even", "l1f", "odd"):
            xs, ms = ffn(1, 1, L, xs, ms, ("ln_g12", "ln_b12"), None)
        if stage not in ("ffn0", "even", "l1f", "odd", "first"):
            xs = second_block(xs, 1 if stage == "second0" else 2)
        drain()
        no = T if stage in ("ffn0", "even", "l1f") else L
        for k in range(KD):
            SP.wait(xs[k])
            SP.ops.append([lambda e, k=k: e.dma_start(OUT[:, k, 0:no], Xt[k][:, 0:no]).then_inc(s_out, 16), None, 0])
        SP.ops.append([None, s_out, 16 * KD])

        block = ctx.enter_context(nc.Block())

        @block.sync
        def _(eng):
            SP.play(eng)

        @block.tensor
        def _(eng):
            PE.play(eng)

        @block.scalar
        def _(eng):
            ACT.play(eng)

        @block.vector
        def _(eng):
            DVE.play(eng)

        @block.gpsimd
        def _(eng):
            POOL.play(eng)
    return recipes


def program(nc, nch, stage="all"):
    pn = sum(n for _, n, _ in param_list())
    cn = sum(a.shape[1] for _, a in constant_list())

    def dram(name, shape, kind="ExternalInput"):
        return nc.dram_tensor(name, shape, F32, kind=kind).ap()

    args = [dram("w_stream", [nch, 128, CH]), dram("params", [128, pn]), dram("consts", [128, cn]),
            dram("x_t", [128, KD * T]), dram("mem_t", [128, KD * L]), dram("out_t", [128, KD, T if stage in ("ffn0", "even", "l1f") else L], "ExternalOutput")]
    return build(nc, *args, stage=stage)


def lay_out(a, recipes):
    nch = recipes[-1][0] + 1
    w = np.zeros((nch, 128, CH), np.float32)
    for c, off, n, parts in recipes:
        for name, idx, r0, nr, c0, ncol, at in parts:
            w[c, 0:nr, off + at:off + at + ncol] = a[name][idx][r0:r0 + nr, c0:c0 + ncol]
    x = np.concatenate([a["x"][0], a["ctx"][0]], 0)
    return {
        "w_stream": w,
        "params": np.concatenate([fn(a) for _, _, fn in param_list()], 1),
        "consts": np.concatenate([c for _, c in constant_list()], 1),
        "x_t": np.ascontiguousarray(x.T.reshape(KD, 128, T).transpose(1, 0, 2).reshape(128, KD * T)),
        "mem_t": np.ascontiguousarray(a["mem_2"][0].T.reshape(KD, 128, L).transpose(1, 0, 2).reshape(128, KD * L)),
    }


def kernel(**inputs):
    import concourse.bacc as bacc
    from concourse.bass_utils import run_bass_kernel_spmd

    a = {k: np.asarray(v) for k, v in inputs.items()}
    nc = bacc.Bacc("TRN2", target_bir_lowering=False, num_devices=1)
    recipes = program(nc, NCH)
    assert recipes[-1][0] + 1 == NCH
    r = run_bass_kernel_spmd(nc, [lay_out(a, recipes)], core_ids=[0])
    y = r.results[0]["out_t"]
    return np.ascontiguousarray(y.transpose(2, 1, 0)).reshape(1, L, D)
```

```python
import math
from contextlib import ExitStack
from itertools import chain

import numpy as np

import concourse.bass as bass
from concourse import mybir

F32 = mybir.dt.float32
F32R = mybir.dt.float32r
ALU = mybir.AluOpType
ACTF = mybir.ActivationFunctionType
AXX = mybir.AxisListType.X

D, T, L = 1024, 512, 256
KD = D // 128
DFF = 2816
KF = DFF // 128
ALPHA = 4.0 ** 0.25
CH = 1024
NSLOT = 3
NSPL = 4
HC = CH // 2
NCH = 658
NEG = -1.0e30
IN2 = (512,) * 8 + (512, 64, 8, 512, 512, 3072)
OFF2 = [sum(IN2[:i]) for i in range(len(IN2))]


def cols(v, n=None):
    return np.asarray(v).reshape(-1, 128).T


def param_list():
    out = []

    def add(name, n, fn):
        out.append((name, n, fn))

    add("cond", 16, lambda a: np.stack([cols(a["c"][0]), cols(a["c_ctx"])], -1).reshape(128, 16))
    for l in range(2):
        add(f"ada_b{l}", 72, lambda a, l=l: cols(a["ada_b"][l]))
        for j in range(3):
            add(f"ln_g{l}{j}", 8, lambda a, l=l, j=j: cols(a["ln_g"][l, j]))
            add(f"ln_b{l}{j}", 8, lambda a, l=l, j=j: cols(a["ln_b"][l, j]))
        add(f"norm2_{l}", 8, lambda a, l=l: cols(a["norm_g_2"][l]))
        add(f"mnorm2_{l}", 8, lambda a, l=l: cols(a["mem_norm_g_2"][l]))
    add("fin_g", 8, lambda a: cols(a["final_g_2"]))
    add("conv", 60, lambda a: a["even_qkv_conv"][0].reshape(5, 12, 128).transpose(2, 1, 0).reshape(128, 60))
    add("dwc", 124, lambda a: a["cf_dw_conv"][0].reshape(31, 4, 128).transpose(2, 1, 0).reshape(128, 124))
    add("dwb", 4, lambda a: cols(a["cf_dw_bias"][0]))
    add("clg", 4, lambda a: cols(a["cf_ln_g"][0]))
    add("clb", 4, lambda a: cols(a["cf_ln_b"][0]))
    add("onorm", 1, lambda a: cols(a["gdn_out_norm"][0]))
    add("qn", 1, lambda a: cols(a["attn_q_norm"][0]))
    add("kn", 1, lambda a: cols(a["attn_k_norm"][0]))

    def gates(a, name):
        v = np.zeros((128, 1), np.float32)
        v[0:4, 0] = a[name][0, 0]
        v[32:36, 0] = a[name][0, 1]
        return v

    add("alog", 1, lambda a: gates(a, "gdn_a_log"))
    add("dtb", 1, lambda a: gates(a, "gdn_dt_bias"))
    return out


def constant_list():
    out = []
    p = np.arange(128)
    out.append(("ident", np.eye(128)))
    out.append(("ones", np.full((128, 128), 1.0)))
    out.append(("sel4", np.concatenate([np.eye(2), np.eye(2), np.zeros((124, 2))])))
    j, i = p[:, None] % 64, np.arange(64)[None, :]
    for n, ok in (("f", i >= j), ("b", i <= j)):
        out.append((f"inc_{n}", ok))
    for n, ok in (("f", i > j), ("b", i < j)):
        out.append((f"str_{n}", ok))
    r, c = p[:, None] % 64, np.arange(64)[None, :]
    for b in (1, 2, 4, 8, 16, 32):
        same = r // (2 * b) == c // (2 * b)
        low = same & ((r // b) % 2 == 1) & ((c // b) % 2 == 0)
        up = same & ((r // b) % 2 == 0) & ((c // b) % 2 == 1)
        if b == 1:
            out.append(("u1_f", -1.0 * up))
            out.append(("u1_b", -1.0 * low))
        else:
            out.append((f"lv{b}_f", low))
            out.append((f"lv{b}_b", up))
    out.append(("id64", r == c))
    for n, step in (("eps5", 1e-5), ("eps6", 1e-6), ("eps128", 128e-6)):
        out.append((n, np.full((128, 1), step)))
    s = np.ones((128, 64))
    s[:, 0] = 0
    out.append(("sg", s))
    t = np.arange(L)
    inv = np.float32(10000.0) ** (-np.arange(32, dtype=np.float32) / np.float32(32))
    ang = np.concatenate([(t // 64).astype(np.float32)[:, None] * inv, (t % 64).astype(np.float32)[:, None] * inv], -1)
    out.append(("ropeC", np.repeat(np.cos(ang).T, 2, axis=0)))
    out.append(("ropeS", np.repeat(np.sin(ang).T, 2, axis=0)))
    rot = np.zeros((128, 128))
    for k in range(64):
        rot[2 * k, 2 * k + 1] = -1
        rot[2 * k + 1, 2 * k] = 1
    out.append(("rotT", rot.T))
    inv = np.float32(500000.0) ** (-np.arange(8, dtype=np.float32) / np.float32(8))
    ang = t.astype(np.float32)[:, None] * inv[None, :]
    C, S, R = np.ones((128, L)), np.zeros((128, L)), np.zeros((128, 128))
    for h in (0, 64):
        for k in range(8):
            C[h + k] = C[h + 8 + k] = np.cos(ang[:, k])
            S[h + k] = S[h + 8 + k] = np.sin(ang[:, k])
            R[h + k, h + 8 + k] = -1
            R[h + 8 + k, h + k] = 1
    out.append(("prC", C))
    out.append(("prS", S))
    out.append(("prT", R.T))
    q = np.concatenate([p[:, None] + 128 * n >= np.arange(L)[None, :] for n in range(2)], 1)
    out.append(("causal", np.where(q, 0.0, NEG)))
    return [(n, np.ascontiguousarray(a, dtype=np.float32)) for n, a in out]


class Queue:

    def __init__(self, sem):
        self.sem, self.ops, self.n, self.seen = sem, [], 0, {}

    def wait(self, *tokens):
        for t in tokens:
            if t is None:
                continue
            if isinstance(t, list):
                self.wait(*t)
                continue
            assert t != "taken", "a buffer is used again before its last reader is known"
            sem, value = t
            if self.seen.get(id(sem), 0) < value:
                self.seen[id(sem)] = value
                self.ops.append([None, sem, value])

    def quiet(self, fn, *tokens):
        self.wait(*tokens)
        self.ops.append([fn, None, 0])

    def mark(self):
        op = self.ops[-1]
        if op[0] is not None and op[1] is None:
            self.n += 1
            op[1] = self.sem
        elif op[0] is None:
            return (self.sem, self.n) if self.n else None
        return (self.sem, self.n)

    def do(self, fn, *tokens):
        self.quiet(fn, *tokens)
        return self.mark()

    def play(self, eng):
        for fn, sem, value in self.ops:
            if fn is None:
                eng.wait_ge(sem, value)
            else:
                ins = fn(eng)
                if sem is not None:
                    ins.then_inc(sem, 1)


class Rot:

    def __init__(self, bufs):
        self.bufs, self.free, self.i = bufs, [None] * len(bufs), -1

    def get(self):
        n = len(self.bufs)
        self.i = next(i % n for i in range(self.i + 1, self.i + 1 + n) if self.free[i % n] != ["taken"])
        free, self.free[self.i] = self.free[self.i], ["taken"]
        return self.bufs[self.i], free, self.i


def build(nc, nch, W, PRM, CST, XT, MT, OUT, stage="all"):
    recipes = []
    ctx = ExitStack()
    with ctx:
        def sb(name, n):
            return ctx.enter_context(nc.sbuf_tensor(name, [128, n], F32))

        def sem(name):
            return ctx.enter_context(nc.semaphore(name))

        PE, ACT, DVE, POOL, SP = (Queue(sem(n)) for n in ("s_pe", "s_act", "s_dve", "s_pool", "s_sp"))
        s_prm, s_cst, s_x, s_m, s_out = (sem(n) for n in ("d_prm", "d_cst", "d_x", "d_m", "d_out"))
        s_w = [sem(f"d_w{i}") for i in range(NSLOT)]

        ring = sb("ring", NSLOT * CH)
        X = sb("X", KD * T)
        pl, cl = param_list(), constant_list()
        prm = sb("prm", sum(n for _, n, _ in pl))
        cst = sb("cst", sum(a.shape[1] for _, a in cl))
        small = sb("small", 900)
        WK = 30720
        BIGN = WK
        with nc.sbuf_tensor("big", [128, BIGN], F32) as big:
            pass
        bigr = ctx.enter_context(nc.sbuf_tensor("bigr", [128, BIGN], F32R))
        work = sb("work", 9 * 512)
        spl = ctx.enter_context(nc.sbuf_tensor("spl", [128, NSPL * 2 * HC], F32R))
        csr = ctx.enter_context(nc.sbuf_tensor("csr", [128, 160], F32R))
        banks = Rot([ctx.enter_context(nc.psum_tensor(f"ps{i}", [128, 512], F32))[:, :] for i in range(8)])

        at = {}
        o = 0
        for n, w, _ in pl:
            at[n] = (prm, o, w)
            o += w
        o = 0
        for n, a in cl:
            at[n] = (cst, o, a.shape[1])
            o += a.shape[1]

        def P(name, a=0, b=None):
            t, o, w = at[name]
            return t[:, o + a:o + (w if b is None else b)]

        so = [0]

        def sm(n):
            so[0] += n
            assert so[0] <= 900, so
            return small[:, so[0] - n:so[0]]

        def last():
            return [q.mark() if q.ops else None for q in (PE, ACT, DVE, POOL)]

        state = {"half": -1, "off": HC, "split": {}, "used": {}, "pool": False, "auto": False}

        def load(c):
            s = c % NSLOT
            SP.wait(state["split"].get(2 * (c - NSLOT)), state["split"].get(2 * (c - NSLOT) + 1))
            SP.ops.append([lambda e: e.dma_start(ring[:, s * CH:(s + 1) * CH], W[c]).then_inc(s_w[s], 16), None, 0])

        def split(h):
            c = h // 2
            if c >= nch:
                return
            if h % 2 == 0:
                if h == 0:
                    for i in range(NSLOT):
                        load(i)
                    for dst, src, s in ((cst, CST, s_cst), (X, XT, s_x)):
                        SP.ops.append([lambda e, dst=dst, src=src, s=s: e.dma_start(dst[:, :], src).then_inc(s, 16), None, 0])
                elif c + NSLOT - 1 < nch:
                    load(c + NSLOT - 1)
            a = (c % NSLOT) * CH + (h % 2) * HC
            raw = ring[:, a:a + HC]
            base = (h % NSPL) * 2 * HC
            hi, lo = spl[:, base:base + HC], spl[:, base + HC:base + 2 * HC]
            arrived = (s_w[c % NSLOT], 16 * (c // NSLOT + 1))
            t = ACT.do(lambda e: e.activation(hi, raw, ACTF.Copy), arrived, state["used"].get(h - NSPL))
            q = POOL if state["pool"] and h % 2 else DVE
            state["split"][h] = q.do(lambda e: e.tensor_tensor(lo, raw, hi, ALU.subtract), t)

        def take(recipe, n=128):
            if state["off"] + n > HC:
                h = state["half"]
                if h >= 0:
                    state["used"][h] = PE.mark()
                    split(h + NSPL)
                else:
                    for i in range(NSPL):
                        split(i)
                state["half"] += 1
                state["off"] = 0
            h = state["half"]
            recipes.append((h // 2, (h % 2) * HC + state["off"], n, recipe))
            a = (h % NSPL) * 2 * HC + state["off"]
            state["off"] += n
            return spl[:, a:a + n], spl[:, a + HC:a + HC + n], state["split"].get(h)

        def mm(out, lhsT, rhs, start, stop, *tokens, **kw):
            PE.quiet(lambda e: e.matmul(out, lhsT, rhs, start=start, stop=stop, **kw), *tokens)

        def transp(out, in_, k, *tokens):
            PE.quiet(lambda e: e.transpose(out, in_, P("ident")[0:k, 0:k]), *tokens)

        def ts(q, out, a, s1, s2, op0, op1, *tokens):
            if op1 is None:
                return q.do(lambda e: e.tensor_scalar(out, a, s1, None, op0), *tokens)
            return q.do(lambda e: e.tensor_scalar(out, a, s1, s2, op0, op1), *tokens)

        def tt(q, out, a, b, op, *tokens):
            return q.do(lambda e: e.tensor_tensor(out, a, b, op), *tokens)

        def stt(q, out, a, s, b, op0, op1, *tokens):
            return q.do(lambda e: e.scalar_tensor_tensor(out, a, s, b, op0, op1), *tokens)

        def act(out, a, fn, *tokens, **kw):
            return ACT.do(lambda e: e.activation(out, a, fn, **kw), *tokens)

        def copy(q, out, a, *tokens):
            if q is ACT:
                return act(out, a, ACTF.Copy, *tokens)
            return q.do(lambda e: e.tensor_copy(out, a), *tokens)

        def memset(q, out, v, *tokens):
            return q.do(lambda e: e.memset(out, v), *tokens)

        MUL, ADD, SUB = ALU.mult, ALU.add, ALU.subtract

        def mm3(out, st, mv, start, stop, *tokens):
            mm(out, st[0], mv[0], start, False, *tokens)
            mm(out, st[0], mv[1], False, False)
            mm(out, st[1], mv[0], False, stop)

        def linear(w, src, n):
            bank, free, bi = banks.get()
            for k, (hi, lo, tok) in enumerate(src):
                whi, wlo, wtok = take(w(k))
                mm3(bank[:, 0:n], (whi, wlo), (hi, lo), k == 0, k == len(src) - 1, free, wtok, tok)
                t = PE.mark() if k == len(src) - 1 else None
                if k % 4 == 3 and state["auto"]:
                    pump()
            old, later[:] = list(later), []
            for fn in old:
                fn()
            return bank, bi, t

        later = []

        def flush():
            while later:
                later.pop(0)()

        def dual(raw, hi, lo, tok, *more, q=None):
            t = copy(ACT, hi, raw, tok, *more)
            return tt(q or POOL, lo, raw, hi, SUB, t)

        def tile_of(name, idx, c0):
            return lambda k: [(name, idx, 128 * k, 128, c0, 128, 0)]

        for dst, src, s in ((prm, PRM, s_prm),):
            SP.ops.append([lambda e, dst=dst, src=src, s=s: e.dma_start(dst[:, :], src).then_inc(s, 16), None, 0])
        tp, tc, tx = (s_prm, 16), (s_cst, 16), (s_x, 16)
        for q in (PE, ACT, DVE, POOL):
            q.wait(tp)

        def B(a, n):
            return big[:, a:a + n]

        def R(a, n):
            return bigr[:, a:a + n]

        Xt = [X[:, k * T:(k + 1) * T] for k in range(KD)]
        XM = [(R(k * T, T), R((KD + k) * T, T)) for k in range(KD)]

        nega, colA, colT, colB, colG = sm(1), sm(64), sm(32), sm(32), sm(64)
        wi, mx8 = sm(16), sm(16)

        cs = sm(16)
        t_cs = act(cs, P("cond"), ACTF.Silu)
        cs3, c3 = cs.rearrange("p (k s) -> p k s", s=2), csr[:, 0:32].rearrange("p (k s) -> p k s", s=4)
        t = memset(DVE, csr[:, 32:160].bitcast(F32), 0.0)
        t1 = copy(DVE, c3[:, :, 0:2], cs3, t_cs)
        t_cs = tt(DVE, c3[:, :, 2:4], cs3, c3[:, :, 0:2], SUB, t1)
        mods, t_mod, md_ = {}, {}, {}
        arow = sb("arow", 1024)
        arows = Rot([arow[0:4, 0:512], arow[0:4, 512:1024]])

        def ada(l, groups):
            if l not in mods:
                md_[l] = sm(144)
                mods[l], t_mod[l] = md_[l].rearrange("p (i m s) -> p i m s", i=9, s=2), {}
            md = md_[l]

            def turn(g, row, t_row, ri):
                bank, free, bi = banks.get()
                for q in range(4):
                    mm(bank[:, 2 * q:2 * q + 2], row[:, q * 128:(q + 1) * 128], P("sel4")[0:4, :], True, True, t_row, free, tc)
                t = PE.mark()
                arows.free[ri] = t
                t = tt(DVE, md[:, 8 * g:8 * g + 8].rearrange("p (a s) -> p a s", s=2), bank[:, 0:8].rearrange("p (a s) -> p a s", s=2),
                       P(f"ada_b{l}", 4 * g, 4 * g + 4).unsqueeze(2).broadcast_to([128, 4, 2]), ADD, t)
                banks.free[bi] = t
                t_mod[l][g] = t

            prev = None
            for g in groups:
                bank, free, bi = banks.get()
                for k in range(KD):
                    whi, wlo, wtok = take([("ada_w", (l,), 128 * k, 128, 512 * g, 512, 0)], 512)
                    mm(bank, csr[:, 4 * k:4 * k + 128], whi, k == 0, False, free, wtok, t_cs)
                    mm(bank, csr[:, 4 * k:4 * k + 128], wlo, False, k == KD - 1)
                    if k == 1 and prev:
                        turn(*prev)
                    if k < KD - 1:
                        yield
                t = PE.mark()
                row, rfree, ri = arows.get()
                t_row = copy(ACT, row, bank[0:4, :], t, rfree)
                banks.free[bi] = t_row
                prev = (g, row, t_row, ri)
                yield
            turn(*prev)

        def mod_ready(l, *i):
            return [t_mod[l][2 * j + e] for j in i for e in (0, 1)]

        def norm_cols(g, b, l, i_shift, i_scale, tok):
            G = sm(16).rearrange("p (m s) -> p m s", s=2)
            Bc = sm(16).rearrange("p (m s) -> p m s", s=2)
            sc, sh = mods[l][:, i_scale], mods[l][:, i_shift]
            t = ts(DVE, G, sc, 1.0, None, ADD, None, tok, mod_ready(l, i_shift, i_scale))
            if g is None:
                t2 = copy(DVE, Bc, sh, t)
                return G, Bc, t2
            bb = P(b).unsqueeze(2).broadcast_to([128, 8, 2])
            gg = P(g).unsqueeze(2).broadcast_to([128, 8, 2])
            t = tt(DVE, Bc, G, bb, MUL, t)
            t = tt(DVE, Bc, Bc, sh, ADD, t)
            t = tt(DVE, G, G, gg, MUL, t)
            return G, Bc, t

        def gate_cols(l, i, half, tok=None):
            gt = sm(16).rearrange("p (m s) -> p m s", s=2)
            t = ts(DVE, gt, mods[l][:, i], half, None, MUL, None, mod_ready(l, i))
            return gt, t

        wk = [work[:, 512 * i:512 * i + 512] for i in range(9)]
        tmps = Rot(wk[0:3])
        sqs = Rot(wk[3:5])
        accS, accQ, w_mean, w_rstd = wk[5], wk[6], wk[7], wk[8]

        class Sums:

            def __init__(self, n, both=True, tok=None):
                self.n, self.both, self.first, self.tok = n, both, True, tok
                self.ts = self.tq = tok

            def add(self, ap, tok):
                n = self.n
                sq, free, i = sqs.get()
                t = act(sq[:, 0:n], ap, ACTF.Square, tok, free)
                if self.first:
                    if self.both:
                        self.ts = copy(POOL, accS[:, 0:n], ap, tok, self.ts)
                    self.tq = copy(POOL, accQ[:, 0:n], sq[:, 0:n], t, self.tq)
                else:
                    if self.both:
                        self.ts = tt(POOL, accS[:, 0:n], accS[:, 0:n], ap, ADD, tok, self.ts)
                    self.tq = tt(POOL, accQ[:, 0:n], accQ[:, 0:n], sq[:, 0:n], ADD, t, self.tq)
                sqs.free[i] = self.tq
                self.first = False
                return self.tq

            def finish(self, count, eps):
                n = self.n
                if self.both:
                    b1, f1, i1 = banks.get()
                    mm(b1[:, 0:n], P("ones"), accS[:, 0:n], True, True, f1, self.ts)
                    t1 = PE.mark()
                b2, f2, i2 = banks.get()
                mm(b2[:, 0:n], P("ones"), accQ[:, 0:n], True, True, f2, self.tq)
                t2 = PE.mark()
                v = w_rstd[:, 0:n]
                if self.both:
                    tm = act(w_mean[:, 0:n], b1[:, 0:n], ACTF.Copy, t1, self.tok, scale=1.0 / count)
                    banks.free[i1] = tm
                    t = tt(DVE, v, w_mean[:, 0:n], w_mean[:, 0:n], MUL, tm, self.tok)
                    t = stt(DVE, v, b2[:, 0:n], 1.0 / count, v, MUL, SUB, t, t2)
                    banks.free[i2] = t
                    t = ts(DVE, v, v, 0.0, None, ALU.max, None, t)
                    t = act(v, v, ACTF.Sqrt, t, bias=P(eps))
                else:
                    t = act(v, b2[:, 0:n], ACTF.Sqrt, t2, self.tok, scale=1.0 / count, bias=P(eps))
                    banks.free[i2] = t
                return DVE.do(lambda e: e.reciprocal(v, v), t)

        def halves(n):
            return [(0, 0, 256), (1, 256, 512)] if n == T else [(0, 0, n)]

        def layer_norm_x(n, sums, lnp, nxt, out, extra=None):
            t0 = sums.finish(D, "eps5")
            G, Bc, tcol = nxt
            xs, ms = [], []
            for k in range(KD):
                x = Xt[k][:, 0:n]
                t, free, i = tmps.get()
                t = t[:, 0:n]
                q = DVE
                t1 = tt(DVE, t, x, w_mean[:, 0:n], SUB, t0, free)
                t1 = tt(POOL if k % 2 else DVE, t, t, w_rstd[:, 0:n], MUL, t1)
                if G is None:
                    tx_ = act(x, t, ACTF.Identity, t1, scale=P(lnp[0], k, k + 1), bias=P(lnp[1], k, k + 1))
                    tmps.free[i] = tx_
                    xs.append(tx_)
                    continue
                m, mfree, mi = sqs.get()
                for s, a, b in halves(n):
                    tm = ts(DVE, m[:, a:b], t[:, a:b], G[:, k, s:s + 1], Bc[:, k, s:s + 1], MUL, ADD, t1, tcol, mfree)
                hi, lo = out[k][0][:, 0:n], out[k][1][:, 0:n]
                td = dual(m[:, 0:n], hi, lo, tm, extra)
                sqs.free[mi] = td
                tx_ = act(x, t, ACTF.Identity, t1, scale=P(lnp[0], k, k + 1), bias=P(lnp[1], k, k + 1))
                tmps.free[i] = [tx_, tm]
                xs.append(tx_)
                ms.append(td)
            return xs, ms

        def residual(bank, bi, tk, k, n, gt, tg, sums, xtok):
            t, free, i = tmps.get()
            for s, a, b in halves(n):
                ta = act(t[:, a:b], bank[:, a:b], ACTF.Copy, tk, free, tg, scale=gt[:, k, s:s + 1])
            banks.free[bi] = ta
            x = Xt[k][:, 0:n]
            tr = stt(DVE, x, x, ALPHA, t[:, 0:n], MUL, ADD, ta, xtok)
            tmps.free[i] = tr
            return sums.add(x, tr)

        def ffn(l, j, n, xs, ms, lnp, nxt, out_extra=None):
            Ht = [(R(2 * KD * T + m * n, n), R(2 * KD * T + (KF + m) * n, n)) for m in range(KF)]
            hs = []
            state["auto"] = bool(gens)
            for m in range(KF):
                src = [(XM[k][0][:, 0:n], XM[k][1][:, 0:n], ms[k]) for k in range(KD)]
                bg, ig, _ = linear(tile_of("ffn_w_gu", (l, j), 128 * m), src, n)
                tg1 = PE.mark()
                bu, iu, tu = linear(tile_of("ffn_w_gu", (l, j), DFF + 128 * m), src, n)
                t, free, i = tmps.get()
                ta = act(t[:, 0:n], bg[:, 0:n], ACTF.Silu, tg1, free)
                banks.free[ig] = ta
                th = tt(DVE, t[:, 0:n], t[:, 0:n], bu[:, 0:n], MUL, ta, tu)
                banks.free[iu] = th
                th = dual(t[:, 0:n], Ht[m][0][:, 0:n], Ht[m][1][:, 0:n], th)
                tmps.free[i] = th
                hs.append(th)
            gt, tg = gate_cols(l, 2 + 6 * j, 0.5)
            sums = Sums(n)
            for k in range(KD):
                b, bi, tk = linear(tile_of("ffn_w_down", (l, j), 128 * k), [(Ht[m][0][:, 0:n], Ht[m][1][:, 0:n], hs[m]) for m in range(KF)], n)
                residual(b, bi, tk, k, n, gt, tg, sums, xs[k])
            state["auto"] = False
            drain()
            return layer_norm_x(n, sums, lnp, nxt() if nxt else (None, None, None), XM, out_extra)

        gens = []

        def pump(n=1):
            for _ in range(n):
                if gens:
                    try:
                        next(gens[0])
                    except StopIteration:
                        gens.pop(0)

        def drain():
            flush()
            while gens:
                pump()

        def even_mixer(xs, ms):
            f0 = last()
            QK = [B(16624 + i * 512, 512) for i in range(8)]
            V = [B(8192 + i * 512, 512) for i in range(4)]
            SZ = [B(10240 + i * 512, 512) for i in range(4)]
            YP = [B(12288 + i * 572, 572).rearrange("p (s t) -> p s t", s=2) for i in range(4)]
            CF = [B(14576 + i * 512, 512) for i in range(4)]
            QEF = [B(20720 + i * 512, 512) for i in range(4)]
            WT = [[B(4096 + (4 * d + h) * 512, 512) for h in range(4)] for d in range(2)]
            UST = B(22768, 4096).rearrange("p (s n) -> p s n", s=8)
            AT = [[B(26864 + (4 * d + h) * 256, 256).rearrange("p (t i) -> p t i", t=4) for h in range(4)] for d in range(2)]
            LN0 = 28912
            R1, R2 = accS, B(20720, 512)
            CP = Rot([B(26864 + i * 520, 520).rearrange("p (s t) -> p s t", s=2) for i in range(2)])
            for i in range(2):
                CP.free[i] = memset(POOL, CP.bufs[i], 0.0, f0)
            t_yp = [memset(POOL, YP[i], 0.0, f0) for i in range(4)]

            def two(ap):
                return ap.rearrange("p (s t) -> p s t", s=2)

            src = [(XM[k][0], XM[k][1], ms[k]) for k in range(KD)]
            bab, iab, tab = linear(lambda k: [("even_w_in", (0,), 128 * k, 128, 2048 + 4 * r, 4, 32 * r) for r in range(4)], src, T)
            WTf = [B(22768 + i * 512, 512) for i in range(8)]
            xr, mr, er, zr, z2, pr = [w[0:64, :] for w in WTf[0:6]]
            t = ts(DVE, xr, bab[0:64, :], P("dtb")[0:64], None, ADD, None, tab, f0)
            tb = act(R1[64:128, :], bab[64:128, :], ACTF.Sigmoid, tab, f0)
            banks.free[iab] = [t, tb]
            tm = ts(DVE, mr, xr, 0.0, None, ALU.max, None, t)
            t2 = ts(DVE, zr, xr, -1.0, None, MUL, None, t)
            t2 = tt(DVE, zr, zr, xr, ALU.min, t2)
            te = act(er, zr, ACTF.Exp, t2)
            ta = act(nega[0:64], P("alog")[0:64], ACTF.Exp)
            t = ts(DVE, zr, er, 2.0, None, ADD, None, te)
            t = DVE.do(lambda e: e.reciprocal(zr, zr), t)
            t = tt(DVE, zr, zr, er, MUL, t)
            t = tt(DVE, z2, zr, zr, MUL, t)
            t = ts(DVE, pr, z2, 1.0 / 15, None, MUL, None, t)
            for c in (13, 11, 9, 7, 5, 3):
                t = stt(DVE, pr, pr, 1.0 / c, z2, ADD, MUL, t)
            t = stt(DVE, pr, pr, 1.0, zr, ADD, MUL, t)
            t = stt(DVE, pr, pr, 2.0, mr, MUL, ADD, t, tm)
            t = ts(DVE, pr, pr, nega[0:64], -1.0, MUL, MUL, t, ta)
            sgt = WTf[6]
            t1 = memset(DVE, sgt, 1.0, f0)
            t1 = memset(DVE, sgt[:, 0:512:64], 0.0, t1)
            tg1 = DVE.do(lambda e: e.tensor_tensor_scan(R1[0:32, :], sgt[0:32, :], pr[0:32, :], 0.0, MUL, ADD), t, t1)
            tg2 = DVE.do(lambda e: e.tensor_tensor_scan(R1[32:64, ::-1], sgt[32:64, :], pr[32:64, ::-1], 0.0, MUL, ADD), t, t1)
            R1c = R1.rearrange("p (c i) -> p c i", i=64)
            R2c = R2.rearrange("p (c i) -> p c i", i=64)
            t3 = tt(DVE, R2c[0:32], R1c[0:32, :, 63:64].broadcast_to([32, 8, 64]), R1c[0:32], SUB, tg1, f0)
            t4 = tt(DVE, R2c[32:64], R1c[32:64, :, 0:1].broadcast_to([32, 8, 64]), R1c[32:64], SUB, tg2)
            t_r1, t_r2 = [tb, tg1, tg2], [t3, t4]

            t_qkv = []
            t_qk = {}

            def l2norm(m):
                sq, free, i = sqs.get()
                t = act(sq, QK[m], ACTF.Square, t_qkv[m], free)

                def product():
                    b, bfree, bi = banks.get()
                    mm(b, P("ones"), sq, True, True, t, bfree)
                    tk = PE.mark()
                    r, rfree, ri = tmps.get()
                    sqs.free[i] = tk
                    t_ = act(r, b, ACTF.Sqrt, tk, rfree, scale=128.0 if m < 4 else 1.0, bias=P("eps128") if m < 4 else P("eps6"))
                    banks.free[bi] = t_
                    t_ = DVE.do(lambda e: e.reciprocal(r, r), t_)
                    t_ = tt(DVE, QK[m], QK[m], r, MUL, t_)
                    tmps.free[ri] = t_
                    t_qk[m] = t_

                later.append(product)

            for m in range(12):
                b, bi, tk = linear(tile_of("even_w_in", (0,), 128 * m), src, T)
                cp, free, ci = CP.get()
                t = copy(ACT, cp[:, :, 2:258], two(b), tk, free)
                banks.free[bi] = t
                dst = (QK + V)[m]
                ac, afree, ai = tmps.get()
                a3 = two(ac)
                w = lambda j, m=m: P("conv", 5 * m + j, 5 * m + j + 1)
                t = ts(DVE, a3, cp[:, :, 0:256], w(0), None, MUL, None, t, afree)
                for j in range(1, 5):
                    t = stt(DVE, a3, cp[:, :, j:j + 256], w(j), a3, MUL, ADD, t)
                CP.free[ci] = t
                t = act(dst, ac, ACTF.Silu, t, f0)
                tmps.free[ai] = t
                t_qkv.append(t)
                if 2 <= m < 10:
                    l2norm(m - 2)
            t_y = []
            for m in range(4):
                bv, vi, tv = linear(tile_of("even_w_in", (0,), 2064 + 128 * m), src, T)
                bg, gi, tg = linear(tile_of("even_w_in", (0,), 2576 + 128 * m), src, T)
                g, free, i = tmps.get()
                t = act(g, bg, ACTF.Sigmoid, tg, free)
                banks.free[gi] = t
                t = tt(DVE, YP[m][:, :, 15:271], two(g), two(bv), MUL, t, tv, t_yp[m])
                banks.free[vi] = t
                tmps.free[i] = t
                t_y.append(t)
            t_sz = []
            for m in range(4):
                b, bi, tk = linear(tile_of("even_w_in", (0,), 1536 + 128 * m), src, T)
                t = act(SZ[m], b, ACTF.Silu, tk, f0)
                banks.free[bi] = t
                t_sz.append(t)
            t_xm = PE.mark()

            t_cf = []

            def conformer():
                w = lambda j, m: P("dwc", 31 * m + j, 31 * m + j + 1)
                t = [ts(DVE, two(CF[m]), YP[m][:, :, 0:256], w(0, m), P("dwb", m, m + 1), MUL, ADD, t_y[m], f0) for m in range(4)]
                for j in range(1, 31):
                    for m in range(4):
                        t[m] = stt(DVE, two(CF[m]), YP[m][:, :, j:j + 256], w(j, m), two(CF[m]), MUL, ADD, t[m])
                        if m % 2:
                            yield
                t_cf.extend(t)

            cgen = conformer()

            def cstep(n=1):
                for _ in range(n):
                    next(cgen, None)

            def conformer_norm():
                b1, f1, i1 = banks.get()
                for m in range(4):
                    mm(b1, P("ones"), CF[m], m == 0, m == 3, f1, t_cf[m])
                tk1 = PE.mark()
                yield
                b2, f2, i2 = banks.get()
                for m in range(4):
                    sq, free, i = sqs.get()
                    t = act(sq, CF[m], ACTF.Square, t_cf[m], free)
                    mm(b2, P("ones"), sq, m == 0, m == 3, f2, t)
                    sqs.free[i] = PE.mark()
                    if m == 1:
                        yield
                tk2 = PE.mark()
                fc = last()
                mean, rstd = w_mean, w_rstd
                tm = act(mean, b1, ACTF.Copy, tk1, fc, scale=1.0 / 512)
                banks.free[i1] = tm
                t = tt(DVE, rstd, mean, mean, MUL, tm, fc)
                yield
                t = stt(DVE, rstd, b2, 1.0 / 512, rstd, MUL, SUB, t, tk2)
                banks.free[i2] = t
                t = ts(DVE, rstd, rstd, 0.0, None, ALU.max, None, t)
                t = act(rstd, rstd, ACTF.Sqrt, t, bias=P("eps5"))
                yield
                tr = DVE.do(lambda e: e.reciprocal(rstd, rstd), t)
                yield
                for m in range(4):
                    t = tt(POOL, CF[m], CF[m], mean, SUB, tr, tk2)
                    t = tt(POOL, CF[m], CF[m], rstd, MUL, t)
                    t_cf[m] = t

            b, free, bi = banks.get()
            for t_ in range(4):
                transp(b[:, t_ * 128:(t_ + 1) * 128], R1[:, t_ * 128:(t_ + 1) * 128], 128, free, t_r1)
            tk = PE.mark()
            cA4 = colA.rearrange("p (t q h) -> p t q h", t=4, q=4)
            t_ca = copy(DVE, cA4, b.rearrange("p (t q r) -> p t q r", t=4, q=4)[:, :, :, 0:4], tk)
            banks.free[bi] = t_ca
            b, free, bi = banks.get()
            for t_ in range(4):
                transp(b[:, t_ * 64:(t_ + 1) * 64], R2[0:64, t_ * 128:(t_ + 1) * 128], 64, free, t_r2)
            tk = PE.mark()
            cT4 = colT.rearrange("p (t q h) -> p t q h", t=4, q=2)
            t_ct = act(cT4, b[:, 0:256].rearrange("p (t q r) -> p t q r", t=4, q=2)[:, :, :, 0:4], ACTF.Exp, tk)
            banks.free[bi] = t_ct
            cB4 = colB.rearrange("p (t q h) -> p t q h", t=4, q=2)
            t = act(cB4, cA4[:, :, 0:2, :], ACTF.Exp, t_ca)
            t_cb = tt(DVE, cB4, cB4, cA4[:, :, 2:4, :], MUL, t)

            KT = [B(t_ * 512, 512) for t_ in range(4)]
            VT = [B(2048 + t_ * 512, 512) for t_ in range(4)]
            t_kt, t_vt = [], []
            for dst, srcs, toks, out in ((KT, QK[4:8], [t_qk[m] for m in range(4, 8)], t_kt), (VT, V, t_qkv[8:12], t_vt)):
                for t_ in range(4):
                    b, free, bi = banks.get()
                    for h in range(4):
                        transp(b[:, h * 128:(h + 1) * 128], srcs[h][:, t_ * 128:(t_ + 1) * 128], 128, free, toks[h])
                    tk = PE.mark()
                    t = copy(ACT, dst[t_], b, tk, t_xm)
                    banks.free[bi] = t
                    out.append(t)
                pump()
            t_vT = PE.mark()

            def ch(ap, d3=64):
                return ap.rearrange("p (t i) -> p t i", t=4)

            def bc(ap):
                return ap.unsqueeze(1).broadcast_to([128, 4, 64])

            def halfblocks(c):
                return c % 2, c // 2, slice(64 * (c % 2), 64 * (c % 2) + 64)

            id64 = P("id64")
            state["pool"] = True
            egl = colG.rearrange("p (d h c) -> p d h c", d=2, h=4)
            t_at, t_w, t_u, t_qe, t_egl = {}, {}, {}, {}, {}
            sets = [[(B(LN0 + d * 1024, 256), B(LN0 + d * 1024 + 256, 512), accQ[:, 0:256] if d else B(LN0 + 768, 256)) for d in range(2)],
                    [(w_[:, 0:256], WT[d][3], w_[:, 256:512]) for d, w_ in enumerate((w_mean, w_rstd))]]
            setfree = [[f0, f0], [f0, f0]]
            lanes = {}

            def prep(h):
                bufs, bfree = sets[h % 2], setfree[h % 2]
                bG, gfree, gi = banks.get()
                for kind, other in ((0, QK[h]), (1, QK[4 + h])):
                    for c in range(8):
                        p, t_, rows_ = halfblocks(c)
                        mm(bG[rows_, kind * 256 + t_ * 64:kind * 256 + t_ * 64 + 64], QK[4 + h][:, 64 * c:64 * c + 64],
                           other[:, 64 * c:64 * c + 64], True, True, gfree, t_qk[h], t_qk[4 + h])
                t_g = PE.mark()
                yield
                bb, tE, tbm = [], [], []
                for d in range(2):
                    b, free, bi = banks.get()
                    for kind, r in ((0, 32 * d + h), (1, 64 + 32 * d + h)):
                        for p in range(2):
                            mm(b[64 * p:64 * p + 64, kind * 256:kind * 256 + 256].rearrange("p (t i) -> p t i", t=4),
                               P("ident")[:, r:r + 1].broadcast_to([128, 64]),
                               R1.rearrange("r (t p i) -> r t p i", p=2, i=64)[:, :, p, :], True, True, free, t_r1)
                    bb.append((b, bi, PE.mark()))
                for d in range(2):
                    Mt, TU, E = bufs[d]
                    b, bi, tk = bb[d]
                    t = tt(DVE, ch(E), ch(b[:, 0:256]), cA4[:, :, d, h:h + 1].broadcast_to([128, 4, 64]), SUB, tk, t_ca, bfree[d])
                    tbm.append(tt(DVE, ch(Mt), ch(b[:, 256:512]), bc(P(f"str_{'fb'[d]}")), MUL, bfree[d]))
                    banks.free[bi] = [t, tbm[d]]
                    t = ts(DVE, E, E, 0.0, None, ALU.min, None, t)
                    t = act(E, E, ACTF.Exp, t)
                    tE.append(tt(POOL, ch(E), ch(E), bc(P(f"inc_{'fb'[d]}")), MUL, t))
                yield
                ta, tmm = [], []
                for d in range(2):
                    Mt, TU, E = bufs[d]
                    tmm.append(tt(POOL, Mt, Mt, E, MUL, tE[d], tbm[d]))
                    ta.append(tt(DVE, AT[d][h], ch(E), ch(bG[:, 0:256]), MUL, tE[d], t_g))
                    t_at[d, h] = ta[d]
                yield
                tU = []
                for d in range(2):
                    Mt, TU, E = bufs[d]
                    tmm[d] = tt(DVE, Mt, Mt, bG[:, 256:512], MUL, tmm[d])
                    U = TU[:, 256:512]
                    t = tt(POOL, ch(U), ch(Mt), bc(P(f"u1_{'fb'[d]}")), MUL, tmm[d], bfree[d])
                    tU.append(tt(POOL, ch(U), ch(U), bc(id64), ADD, t))
                banks.free[gi] = ta + tmm
                yield
                for d in range(2):
                    Mt, TU, E = bufs[d]
                    U = TU[:, 256:512]
                    b, free, bi = banks.get()
                    for c in range(8):
                        p, t_, rows_ = halfblocks(c)
                        mm(b[rows_, t_ * 64:t_ * 64 + 64], U[rows_, t_ * 64:t_ * 64 + 64], id64[rows_, :], True, True, free, tU[d])
                    tk = PE.mark()
                    tT = copy(ACT, TU[:, 0:256], b[:, 0:256], tk, bfree[d])
                    banks.free[bi] = tT
                    lanes[h, d] = [Mt, TU, E, [tU[d], tT], ta[d], tmm[d]]
                for d in range(2):
                    yield
                    b, free, bi = banks.get()
                    r = 32 * d + h
                    mm(b, P("ident")[:, r:r + 1].broadcast_to([128, 128]), R1, True, True, free, t_r1)
                    tk = PE.mark()
                    if d == 0:
                        e_, efree = QEF[h], f0
                    else:
                        e_, efree, ei = tmps.get()
                    t = act(e_, b, ACTF.Exp, tk, efree)
                    banks.free[bi] = t
                    o_ = 63 if d == 0 else 0
                    t_egl[d, h] = copy(POOL, egl[:, d, h, :], e_[:, o_:512:64], t)
                    dst = QEF[h] if d == 0 else QK[h]
                    t = tt(POOL, dst, QK[h], e_, MUL, t, t_g, t_egl[d, h], t_qe.get((0, h)))
                    t_qe[d, h] = t
                    if d:
                        tmps.free[ei] = t
                yield

            def ending(h):
                tt_ = []
                for d in range(2):
                    Mt, TU, Pm, tU, ta, tmm = lanes[h, d]
                    U = TU[:, 256:512]
                    t1 = tt(DVE, ch(TU[:, 0:256]), ch(U), cA4[:, :, 2 + d, h:h + 1].broadcast_to([128, 4, 64]), MUL, tU)
                    t2 = tt(DVE, ch(Pm), ch(U), cB4[:, :, d, h:h + 1].broadcast_to([128, 4, 64]), MUL, tU, t_cb)
                    tt_.append((t1, t2))
                yield
                for d in range(2):
                    Ub, t1 = lanes[h, d][1][:, 0:256], tt_[d][0]
                    b, free, bi = banks.get()
                    for c in range(8):
                        p, t_, rows_ = halfblocks(c)
                        sl = (t_ ^ 2) if d == 0 else 3 - t_
                        mm(b[rows_, sl * 128:sl * 128 + 128], Ub[rows_, t_ * 64:t_ * 64 + 64], VT[t_][rows_, h * 128:(h + 1) * 128],
                           True, True, free, t1, t_vt)
                    tk = PE.mark()
                    tu = []
                    for p in range(2):
                        sp_ = p if d == 0 else 1 - p
                        rows_ = slice(64 * p, 64 * p + 64)
                        tu.append(copy(ACT, UST[rows_, sp_:8:2, h * 128:(h + 1) * 128], b[rows_, :].rearrange("p (s n) -> p s n", s=4), tk, t_qkv))
                    banks.free[bi] = tu
                    t_u[d, h] = tu
                yield
                for d in range(2):
                    Uw, t2 = lanes[h, d][2], tt_[d][1]
                    bb_ = [banks.get() for _ in range(2)]
                    for c in range(8):
                        p, t_, rows_ = halfblocks(c)
                        mm(bb_[p][0][:, 64 * t_:64 * t_ + 64], KT[t_][rows_, h * 128:(h + 1) * 128], Uw[rows_, t_ * 64:t_ * 64 + 64],
                           True, True, bb_[p][1], t2, t_kt)
                    tk = PE.mark()
                    for p in range(2):
                        t_w[d, h] = copy(ACT, WT[d][h].rearrange("p (t s i) -> p t s i", t=4, s=2)[:, :, p, :], ch(bb_[p][0][:, 0:256]), tk, t_xm)
                        banks.free[bb_[p][2]] = t_w[d, h]
                    setfree[h % 2][d] = tk
                yield

            for _ in prep(0):
                pump()
            for h in range(4):
                side = chain(ending(h - 1) if h else (), prep(h + 1) if h < 3 else ())
                for lv in (2, 4, 8, 16, 32):
                    for d in range(2):
                        Mt, TU, Pm, tTU, ta, tmm = lanes[h, d]
                        b, free, bi = banks.get()
                        for c in range(8):
                            p, t_, rows_ = halfblocks(c)
                            cs_ = slice(t_ * 64, t_ * 64 + 64)
                            mm(b[rows_, cs_], Mt[rows_, cs_], TU[rows_, cs_], True, True, free, tTU, tmm)
                        tk = PE.mark()
                        tP = tt(DVE, ch(Pm), ch(b[:, 0:256]), bc(P(f"lv{lv}_{'fb'[d]}")), MUL, tk, ta, tmm)
                        banks.free[bi] = tP
                        lanes[h, d].append(tP)
                    next(side, None)
                    cstep()
                    for d in range(2):
                        Mt, TU, Pm, tTU, ta, tmm, tP = lanes[h, d]
                        b, free, bi = banks.get()
                        for c in range(8):
                            p, t_, rows_ = halfblocks(c)
                            cs_ = slice(t_ * 64, t_ * 64 + 64)
                            us_ = slice(256 + t_ * 64, 256 + t_ * 64 + 64)
                            if lv < 32:
                                mm(b[rows_, cs_], TU[rows_, us_], Pm[rows_, cs_], True, True, free, tP)
                            mm(b[rows_, us_], Pm[rows_, cs_], TU[rows_, us_], True, True, free, tP)
                        tk = PE.mark()
                        a = 0 if lv < 32 else 256
                        t = tt(DVE, TU[:, a:512], TU[:, a:512], b[:, a:512], SUB, tk)
                        banks.free[bi] = t
                        lanes[h, d] = [Mt, TU, Pm, t, ta, tmm]
                    next(side, None)
                    pump()
                    cstep(2)
                for _ in side:
                    pass
            for _ in ending(3):
                pump(2)
            cstep(100)

            fs = last()
            S = [B(18672 + d * 512, 512) for d in range(2)]
            SD = [B(19696 + d * 512, 512) for d in range(2)]
            KTL = Rot([B(LN0 + i * 512, 512) for i in range(2)])
            VN = Rot([B(LN0 + 1024, 512), accQ])
            oT = B(8192, 2048).rearrange("p (h t) -> p h t", h=4)
            tS = [memset(POOL, S[d], 0.0, fs) for d in range(2)]
            order = [[4, 5, 6, 7, 0, 1, 2, 3], [7, 6, 5, 4, 3, 2, 1, 0]]
            seen, t_o = set(), {}

            def decayed_keys(s):
                kt_, kfree, ki = KTL.get()
                tkt = []
                for d in range(2):
                    p, t_, rows_ = halfblocks(order[d][s])
                    tkt.append(tt(DVE, kt_[rows_, :].rearrange("p (h n) -> p h n", h=4), KT[t_][rows_, :].rearrange("p (h n) -> p h n", h=4),
                                  cT4[rows_, t_, d, :].unsqueeze(2).broadcast_to([64, 4, 128]), MUL, kfree, fs, t_ct))
                return kt_, ki, tkt

            keys = decayed_keys(0)
            cln = conformer_norm()
            for s in range(8):
                cc = [order[d][s] for d in range(2)]
                hb = [halfblocks(c) for c in cc]
                bw = [banks.get() for _ in range(2)]
                bo = [banks.get() for _ in range(2)]
                b4 = [x_[0][:, 0:256].rearrange("p (h i) -> p h i", h=4) for x_ in bo]
                vn, vfree, vi = VN.get()
                tv, tsd = [], []
                for d in range(2):
                    p, t_, rows_ = hb[d]
                    b, free, bi = bw[d]
                    for h in range(4):
                        mm(b[rows_, h * 128:(h + 1) * 128], WT[d][h][:, 64 * cc[d]:64 * cc[d] + 64], S[d][:, h * 128:(h + 1) * 128],
                           True, True, free, tS[d], t_w[d, h])
                    tk = PE.mark()
                    tv.append(tt(DVE, vn[rows_, :], UST[rows_, s, :], b[rows_, :], SUB, tk, vfree, fs))
                    banks.free[bi] = tv[d]
                    if s < 7:
                        g3 = egl[:, d, :, cc[d]:cc[d] + 1].broadcast_to([128, 4, 128])
                        tsd.append(tt(POOL, SD[d].rearrange("p (h n) -> p h n", h=4), S[d].rearrange("p (h n) -> p h n", h=4), g3, MUL, tS[d], [t_egl[d, h] for h in range(4)]))
                    for h in range(4):
                        qe = QEF[h] if d == 0 else QK[h]
                        mm(b4[d][:, h, :], S[d][:, h * 128:(h + 1) * 128], qe[:, 64 * cc[d]:64 * cc[d] + 64], h == 0, False, bo[d][1], t_qe[d, h])
                    tqs = PE.mark()
                kt_, ki, tkt = keys
                for d in range(2):
                    p, t_, rows_ = hb[d]
                    if s < 7:
                        b, free, bi = banks.get()
                        for h in range(4):
                            mm(b[:, h * 128:(h + 1) * 128], kt_[rows_, h * 128:(h + 1) * 128], vn[rows_, h * 128:(h + 1) * 128], True, True, free, tkt[d], tv[d])
                        tk = PE.mark()
                        tS[d] = tt(DVE, S[d], SD[d], b, ADD, tk, tsd[d], tqs)
                        banks.free[bi] = tS[d]
                    for h in range(4):
                        mm(b4[d][:, h, :], vn[rows_, h * 128:(h + 1) * 128], AT[d][h][rows_, t_, :], False, h == 3, tv[d], t_at[d, h])
                    tok = PE.mark()
                    c = cc[d]
                    dst = oT[:, :, 64 * c:64 * c + 64]
                    if c not in seen:
                        t = copy(ACT, dst, b4[d], tok, t_vT, fs)
                    else:
                        t = tt(DVE, dst, dst, b4[d], ADD, tok, t_o[c])
                    seen.add(c)
                    t_o[c] = t
                    banks.free[bo[d][2]] = t
                KTL.free[ki] = tok
                VN.free[vi] = tok
                if s < 6:
                    keys = decayed_keys(s + 1)
                next(cln, None)
                pump()
            for _ in cln:
                pass
            state["pool"] = False
            t_ox = list(t_o.values())

            fm = last()
            HM = [(R(16624 + i * 512, 512), R(20720 + i * 512, 512)) for i in range(8)]
            thm = []
            for h in range(4):
                o_ = B(8192 + h * 512, 512)
                sq, free, i = sqs.get()
                t = act(sq, o_, ACTF.Square, t_ox, free)
                b, bfree, bi = banks.get()
                mm(b, P("ones"), sq, True, True, t, bfree)
                tk = PE.mark()
                sqs.free[i] = tk
                r, rfree, ri = tmps.get()
                t = act(r, b, ACTF.Sqrt, tk, rfree, scale=1.0 / 128, bias=P("eps6"))
                banks.free[bi] = t
                t = DVE.do(lambda e, r=r: e.reciprocal(r, r), t)
                t = tt(DVE, r, r, o_, MUL, t)
                t = stt(DVE, r, r, P("onorm"), SZ[h], MUL, MUL, t, t_sz[h])
                t = dual(r, HM[h][0], HM[h][1], t, fm)
                tmps.free[ri] = t
                thm.append(t)
            for m in range(4):
                w, free, i = tmps.get()
                t = act(w, CF[m], ACTF.Silu, t_cf[m], free, scale=P("clg", m, m + 1), bias=P("clb", m, m + 1))
                t = dual(w, HM[4 + m][0], HM[4 + m][1], t, fm)
                tmps.free[i] = t
                thm.append(t)

            gt, tg = gate_cols(0, 5, 1.0)
            sums = Sums(T, tok=last())
            srcs = [(HM[k][0], HM[k][1], thm[k]) for k in range(8)]
            for k in range(KD):
                b, bi, tk = linear(tile_of("even_w_out", (0,), 128 * k), srcs, T)
                residual(b, bi, tk, k, T, gt, tg, sums, xs[k])
            return layer_norm_x(T, sums, ("ln_g01", "ln_b01"), norm_cols("ln_g01", "ln_b01", 0, 6, 7, None), XM, last())

        def attend(items, PB, PT, stat):

            def scores(it):
                qs, (k, tk_), scale, mask, v, rows_, sink = it
                nq = len(qs)
                nk = 512 // nq
                b, free, bi = banks.get()
                for i, (q, tq) in enumerate(qs):
                    assert tq != [] and tk_ != []
                    mm(b[:, i * nk:(i + 1) * nk], q, k, True, True, free, tq, tk_)
                t = PE.mark()
                p, pfree, pi = PB.get()
                st, sfree, si = stat.get()
                src = b
                if mask is not None:
                    t = tt(DVE, p, b, mask[0], ADD, t, pfree, mask[1])
                    banks.free[bi] = t
                    src = p
                mx, nb, sm_, rc = (st[:, 2 * j:2 * j + nq] for j in range(4))
                t = DVE.do(lambda e: e.tensor_reduce(mx, src.rearrange("p (i k) -> p i k", i=nq), AXX, ALU.max), t, sfree)
                t = ts(DVE, nb, mx, -scale, None, MUL, None, t)
                for i in range(nq):
                    te = act(p[:, i * nk:(i + 1) * nk], src[:, i * nk:(i + 1) * nk], ACTF.Exp, t, pfree,
                             bias=nb[:, i:i + 1], scale=scale, accum_out=sm_[:, i:i + 1])
                if mask is None:
                    banks.free[bi] = te
                t = DVE.do(lambda e: e.reciprocal(rc, sm_), te)
                for i in range(nq):
                    t2 = ts(DVE, p[:, i * nk:(i + 1) * nk], p[:, i * nk:(i + 1) * nk], rc[:, i:i + 1], None, MUL, None, t)
                stat.free[si] = t2
                return p, pi, t2, nq, nk

            def turn(it, sc):
                p, pi, tp_, nq, nk = sc
                b, free, bi = banks.get()
                for i in range(nq):
                    for k in range(nk // 128):
                        transp(b[:, (k * nq + i) * 128:(k * nq + i + 1) * 128], p[:, i * nk + k * 128:i * nk + (k + 1) * 128], 128, free, tp_)
                t = PE.mark()
                PB.free[pi] = t
                pt, ptfree, pti = PT.get()
                t = copy(ACT, pt, b, t, ptfree)
                banks.free[bi] = t
                return pt, pti, t, nq, nk

            def values(it, tr):
                pt, pti, tp_, nq, nk = tr
                v, rows_, sink = it[4:7]
                b, free, bi = banks.get()
                o = b[rows_, 0:nq * 128]
                for k in range(nk // 128):
                    va, vt = v(k)
                    mm(o, va, pt[:, k * nq * 128:(k + 1) * nq * 128], k == 0, k == nk // 128 - 1, free, tp_, vt)
                t = PE.mark()
                PT.free[pti] = t
                banks.free[bi] = sink(o, t)

            a, c = [], []
            for it in list(items) + [None, None]:
                if c:
                    values(*c.pop(0))
                if a:
                    i0, sc = a.pop(0)
                    c.append((i0, turn(i0, sc)))
                if it is not None:
                    a.append((it, scores(it)))
                yield

        stats = Rot([sm(8) for _ in range(4)])

        def rope(raw, traw, n, rt, C, S, out, ofree, done):
            later.append(lambda: done(rope_now(raw, traw, n, rt, C, S, out, ofree)))

        def rope_now(raw, traw, n, rt, C, S, out, ofree):
            b, free, bi = banks.get()
            mm(b[:, 0:256], P(rt), raw[:, 0:256], True, True, free, traw)
            tk = PE.mark()
            t, tfree, ti = tmps.get()
            t1 = tt(DVE, t[:, 0:256], b[:, 0:256], P(S), MUL, tk, tfree)
            banks.free[bi] = t1
            t2 = tt(POOL, out[:, 0:256], raw[:, 0:256], P(C), MUL, traw, ofree, tk)
            t3 = tt(DVE, out[:, 0:256], out[:, 0:256], t[:, 0:256], ADD, t1, t2)
            tmps.free[ti] = t3
            return t3

        def tiles(a, n=4, w=256):
            return [B(a + i * w, w) for i in range(n)]

        def by_token(name, idx, c0, src, out, fr, between=None):
            bs = [banks.get() for _ in range(2)]
            for k in range(KD):
                whi, wlo, wtok = take([(name, idx, 128 * k, 128, c0, 512, 0)], 512)
                for i in range(2):
                    mm3(bs[i][0], [x_[:, i * 128:(i + 1) * 128] for x_ in src[k][0:2]], (whi, wlo), k == 0, k == KD - 1, bs[i][1], wtok, src[k][2])
                if k < KD - 1 and between:
                    between()
            tk = PE.mark()
            res = []
            for i in range(2):
                res.append(copy(ACT, out[i], bs[i][0], tk, fr))
                banks.free[bs[i][2]] = res[-1]
            return res

        MX = [X[:, k * T + 256:(k + 1) * T] for k in range(KD)]
        KM, VM = tiles(21760), tiles(22784, 2, 512)
        t_mx, t_km, t_vm = [], [[], []], [[], []]

        def scaled_memory(l, MN, fl):
            srcm = []
            for k in range(KD):
                t_, free, i = sqs.get()
                t = ts(DVE, t_[:, 0:L], MX[k], P(f"mnorm2_{l}", k, k + 1), None, MUL, None, t_mx[k], free)
                sqs.free[i] = dual(t_[:, 0:L], MN[k][0], MN[k][1], t, fl)
                srcm.append((MN[k][0], MN[k][1], sqs.free[i]))
            return srcm

        def memory_keys(l, m, srcm, fl):
            b, bi, tk = linear(tile_of("w_mem_kv_2", (l,), 128 * m), srcm, L)
            t_km[l].append(copy(ACT, KM[m], b[:, 0:L], tk, fl))
            banks.free[bi] = t_km[l][-1]

        def memory_values(l, srcm, fl, between=None):
            t_vm[l].extend(by_token("w_mem_kv_2", (l,), 512, srcm, VM, fl, between))

        def odd_mixer(xs, ms):
            f0 = last()
            Q = [B(8192 + h * 256, 256) for h in range(8)]
            K = [B(10240 + h * 512, 512) for h in range(2)]
            VK = [B(11264 + k * 256, 256) for k in range(4)]
            O = [(R(12288 + h * 256, 256), R(14336 + h * 256, 256)) for h in range(8)]
            PB = Rot([B(16384 + i * 512, 512) for i in range(3)])
            PT = Rot([B(17920 + i * 512, 512) for i in range(3)])
            raws = Rot([B(19456 + i * 512, 512) for i in range(3)])
            scale = 128.0 ** -0.5
            MN = [(R(23808 + i * 256, 256), R(25856 + i * 256, 256)) for i in range(8)]
            SP.wait(f0)
            SP.ops.append([lambda e: e.dma_start(X.rearrange("p (k t) -> p k t", k=KD)[:, :, 256:512], MT.rearrange("p (k t) -> p k t", k=KD)).then_inc(s_m, 16), None, 0])

            def headnorm(m, n, g, dst, res):
                b, bi, tk = linear(tile_of("attn_w_in", (0,), 128 * m), [(XM[k][0][:, 0:n], XM[k][1][:, 0:n], ms[k]) for k in range(KD)], n)
                sq, free, i = sqs.get()
                t = act(sq[:, 0:n], b[:, 0:n], ACTF.Square, tk, free)
                def product():
                    b2, f2, i2 = banks.get()
                    mm(b2[:, 0:n], P("ones"), sq[:, 0:n], True, True, f2, t)
                    tk2 = PE.mark()
                    sqs.free[i] = tk2
                    r, rfree, ri = tmps.get()
                    t_ = act(r[:, 0:n], b2[:, 0:n], ACTF.Sqrt, tk2, rfree, scale=1.0 / 128, bias=P("eps6"))
                    banks.free[i2] = t_
                    t_ = DVE.do(lambda e: e.reciprocal(r[:, 0:n], r[:, 0:n]), t_)
                    raw, wfree, wi_ = raws.get()
                    t_ = stt(DVE, raw[:, 0:n], b[:, 0:n], P(g), r[:, 0:n], MUL, MUL, t_, wfree, f0)
                    banks.free[bi] = t_
                    tmps.free[ri] = t_
                    if n > 256:
                        res.append(copy(POOL, dst[:, 256:n], raw[:, 256:n], t_, f0))

                    def done(t3):
                        res.append(t3)
                        raws.free[wi_] = list(res)

                    rope(raw, t_, n, "rotT", "ropeC", "ropeS", dst, f0, done)

                later.append(product)
                return res

            tK = [headnorm(8 + h, T, "kn", K[h], []) for h in range(2)]
            sums = Sums(L, both=False, tok=f0)
            for k in range(KD):
                sums.add(MX[k], (s_m, 16))
            bs = [banks.get() for _ in range(4)]
            for k in range(KD):
                whi, wlo, wtok = take([("attn_w_in", (0,), 128 * k, 128, 1280, 256, 0)], 256)
                for i in range(4):
                    mm3(bs[i][0][:, 0:256], [x_[:, i * 128:(i + 1) * 128] for x_ in XM[k]], (whi, wlo), k == 0, k == KD - 1, bs[i][1], wtok, ms[k])
            tk = PE.mark()
            flush()
            tV = []
            for i in range(4):
                t = copy(ACT, VK[i], bs[i][0][:, 0:256], tk, f0)
                banks.free[bs[i][2]] = t
                tV.append(t)
            tr = sums.finish(D, "eps6")
            t_mx.extend(tt(DVE, MX[k], MX[k], w_rstd[:, 0:L], MUL, tr) for k in range(KD))
            tO = {}
            tQ = [[] for _ in range(8)]

            def items():
                for h in range(8):
                    for i in range(2):
                        g = h // 4

                        def sink(o, t, h=h, i=i):
                            hi, lo = (x_[:, i * 128:(i + 1) * 128] for x_ in O[h])
                            tO[h, i] = dual(o, hi, lo, t, f0, q=DVE)
                            return tO[h, i]

                        yield ([(Q[h][:, i * 128:(i + 1) * 128], tQ[h])], (K[g], tK[g]), scale, None,
                               lambda k, g=g: (VK[k][:, g * 128:(g + 1) * 128], tV[k]), slice(0, 128), sink)

            gens.append(attend(items(), PB, PT, stats))
            srcm = scaled_memory(0, MN, f0)
            headnorm(0, 256, "qn", Q[0], tQ[0])
            headnorm(1, 256, "qn", Q[1], tQ[1])
            for h in range(2, 8):
                headnorm(h, 256, "qn", Q[h], tQ[h])
                pump()
                if h < 6:
                    memory_keys(0, h - 2, srcm, f0)
                    pump()
            flush()
            memory_values(0, srcm, f0, pump)
            drain()
            gt, tg = gate_cols(1, 5, 1.0)
            sums = Sums(L)
            srcs = [(O[h][0], O[h][1], [tO[h, 0], tO[h, 1]]) for h in range(8)]
            for k in range(KD):
                b, bi, tk = linear(tile_of("attn_w_out", (0,), 128 * k), srcs, L)
                residual(b, bi, tk, k, L, gt, tg, sums, xs[k])
            return layer_norm_x(L, sums, ("ln_g11", "ln_b11"), norm_cols("ln_g11", "ln_b11", 1, 6, 7, None), XM, last())

        def second_block(xs, depth):
            f0 = last()

            def duals(a, n):
                return [(R(a + i * 256, 256), R(a + (n + i) * 256, 256)) for i in range(n)]

            HH, MN, MG = duals(0, 8), duals(4096, 8), duals(4096, 8)
            PT = Rot(tiles(4096, 2, 512))
            WKI, IDX, SEL = (B(5120 + 512 * i, 512) for i in range(3))
            PB = Rot(tiles(6656, 3, 512))
            QA, KA, VA, GA = tiles(8192), tiles(9216), tiles(10240, 2, 512), tiles(11264)
            QB, GB, KB, VB = tiles(12288), tiles(13312), tiles(14336), tiles(15360, 2, 512)
            MQ, GM = QB, GB
            QI, KI = tiles(16384), B(17408, 256)
            MIX = tiles(17664, 24)
            YA, YB, YM = (duals(23808 + 2048 * i, 4) for i in range(3))
            tsum = None
            for l in range(depth):
                fl = last()
                if l:
                    srcm = scaled_memory(l, MN, fl)
                if tsum is None:
                    sums = Sums(L, both=False)
                    for k in range(KD):
                        sums.add(Xt[k][:, 0:L], xs[k])
                else:
                    sums = tsum
                if l:
                    for m in range(4):
                        memory_keys(l, m, srcm, fl)
                tr = sums.finish(D, "eps6")
                src = []
                for k in range(KD):
                    t_, free, i = tmps.get()
                    t = stt(DVE, t_[:, 0:L], Xt[k][:, 0:L], P(f"norm2_{l}", k, k + 1), w_rstd[:, 0:L], MUL, MUL, tr, free)
                    tmps.free[i] = dual(t_[:, 0:L], HH[k][0], HH[k][1], t, fl)
                    src.append((HH[k][0], HH[k][1], tmps.free[i]))

                if l:
                    memory_values(l, srcm, fl)
                tKM, tVM = t_km[l], t_vm[l]
                f_mn = last()

                def proj(piece, m):
                    r = linear(tile_of("w_in_2", (l,), OFF2[piece] + 128 * m), src, L)
                    return r

                def roped(r, dst, fl=fl):
                    res = []
                    b, bi, tk = r
                    raw, free, i = sqs.get()
                    t = copy(ACT, raw[:, 0:256], b[:, 0:256], tk, free)
                    banks.free[bi] = t

                    def done(t3):
                        res.append(t3)
                        sqs.free[i] = t3

                    rope(raw, t, L, "prT", "prC", "prS", dst, fl, done)
                    return res

                def gated(piece, m, dst, fn, fl=fl):
                    b, bi, tk = proj(piece, m)
                    t = act(dst, b[:, 0:L], fn, tk, fl)
                    banks.free[bi] = t
                    return t

                r = linear(lambda k: [("w_in_2", (l,), 128 * k, 128, OFF2[9], 64, 0), ("w_in_2", (l,), 128 * k, 128, OFF2[9], 64, 64)], src, L)
                tKI = roped(r, KI)
                whi, wlo, wtok = take([("w_in_2", (l,), 128 * k, 128, OFF2[10], 8, 8 * k) for k in range(KD)], 64)
                flush()
                b, free, bi = banks.get()
                for i in range(2):
                    for k in range(KD):
                        mm3(b[:, 8 * i:8 * i + 8], [x_[:, i * 128:(i + 1) * 128] for x_ in HH[k]], (whi[:, 8 * k:8 * k + 8], wlo[:, 8 * k:8 * k + 8]),
                            k == 0, k == KD - 1, free, wtok, src[k][2])
                tk = PE.mark()
                t_wi = ts(DVE, wi, b[:, 0:16], 8 ** -0.5, 0.125, MUL, MUL, tk, fl)
                banks.free[bi] = t_wi
                tQI = [roped(proj(8, m), QI[m]) for m in range(4)]
                selt = []

                def index():
                    ta = copy(POOL, IDX, P("causal"), f_mn)
                    for h in range(8):
                        rows_ = slice(64 * (h % 2), 64 * (h % 2) + 64)
                        b, free, bi = banks.get()
                        for i in range(2):
                            mm(b[:, 256 * i:256 * i + 256], QI[h // 2][rows_, i * 128:(i + 1) * 128], KI[rows_, :], True, True, free, tQI[h // 2], tKI)
                        tk = PE.mark()
                        rl, rfree, ri = tmps.get()
                        t = act(rl, b, ACTF.Relu, tk, rfree)
                        banks.free[bi] = t
                        for i in range(2):
                            ta2 = stt(DVE, IDX[:, 256 * i:256 * i + 256], rl[:, 256 * i:256 * i + 256], wi[:, 8 * i + h:8 * i + h + 1],
                                      IDX[:, 256 * i:256 * i + 256], MUL, ADD, t, ta, t_wi)
                        ta = ta2
                        tmps.free[ri] = ta
                        yield
                    tm = [ta, ta]
                    for r_ in range(8):
                        a, o = (IDX, WKI) if r_ % 2 == 0 else (WKI, IDX)
                        for i in range(2):
                            s_ = slice(256 * i, 256 * i + 256)
                            tm[i] = DVE.do(lambda e, a=a, s_=s_, i=i: e.max(mx8[:, 8 * i:8 * i + 8], a[:, s_]), tm[i], f_mn)
                        for i in range(2):
                            s_ = slice(256 * i, 256 * i + 256)
                            tm[i] = DVE.do(lambda e, a=a, o=o, s_=s_, i=i: e.match_replace(o[:, s_], mx8[:, 8 * i:8 * i + 8], a[:, s_], -2.0 ** 127), tm[i])
                        if r_ % 2:
                            yield
                    t = tm
                    t = ts(DVE, SEL, IDX, -2.0 ** 127, NEG, ALU.not_equal, MUL, t)
                    t = tt(DVE, SEL, SEL, P("causal"), ALU.min, t)
                    selt.append(t)
                    yield

                
                def branch_heads(Q, tQ, K, tK, V, tV, G, tG, Y, tY, mask):
                    for h in range(8):
                        rows_ = slice(64 * (h % 2), 64 * (h % 2) + 64)
                        m = h // 2

                        def sink(o, t, h=h, m=m, rows_=rows_):
                            w, free, i = tmps.get()
                            t1 = tt(DVE, w[rows_, 0:L], o, G[m][rows_, :], MUL, t, tG[m], free)
                            tmps.free[i] = dual(w[rows_, 0:L], Y[m][0][rows_, :], Y[m][1][rows_, :], t1, fl, q=DVE)
                            tY.append(tmps.free[i])
                            return t1

                        yield ([(Q[m][rows_, i * 128:(i + 1) * 128], tQ[m]) for i in range(2)], (K[m][rows_, :], tK[m]), 0.125,
                               mask(), lambda k, h=h: (V[k][:, h * 64:(h + 1) * 64], tV[k]), rows_, sink)

                tY = [[], [], []]

                def qkvg(p0, Q, K, V, G, fl):
                    tQ, tK, tG = [], [], []
                    for m in range(4):
                        tQ.append(roped(proj(p0, m), Q[m], fl))
                        pump()
                        tK.append(roped(proj(p0 + 1, m), K[m], fl))
                        pump()
                    tV = by_token("w_in_2", (l,), OFF2[p0 + 2], src, V, fl)
                    flush()
                    pump()
                    for m in range(4):
                        tG.append(gated(p0 + 3, m, G[m], ACTF.Silu, fl))
                        pump()
                    return tQ, tK, tV, tG

                tMQ, tGM = [], []
                for m in range(4):
                    tMQ.append(gated(11, m, MQ[m], ACTF.Copy))
                    pump()
                    tGM.append(gated(12, m, GM[m], ACTF.Silu))
                    pump()

                def memory_heads():
                    for h in range(4):
                        def sink(o, t, h=h):
                            w, free, i = tmps.get()
                            t1 = tt(DVE, w[:, 0:L], o, GM[h], MUL, t, tGM[h], free)
                            tmps.free[i] = dual(w[:, 0:L], YM[h][0], YM[h][1], t1, fl)
                            tY[2].append(tmps.free[i])
                            return t1

                        yield ([(MQ[h][:, i * 128:(i + 1) * 128], tMQ[h]) for i in range(2)], (KM[h], tKM[h]), 128.0 ** -0.5, None,
                               lambda k, h=h: (VM[k][:, h * 128:(h + 1) * 128], tVM[k]), slice(0, 128), sink)

                gens.append(attend(memory_heads(), PB, PT, stats))
                gens.append(index())
                tQ, tK, tV, tG = qkvg(0, QA, KA, VA, GA, fl)
                gens.append(attend(branch_heads(QA, tQ, KA, tK, VA, tV, GA, tG, YA, tY[0], lambda: (P("causal"), None)), PB, PT, stats))
                while len(gens) > 1:
                    pump()
                f_b = last()
                tQ, tK, tV, tG = qkvg(4, QB, KB, VB, GB, f_b)
                gens.append(attend(branch_heads(QB, tQ, KB, tK, VB, tV, GB, tG, YB, tY[1], lambda: (SEL, selt[0])), PB, PT, stats))
                tX = []
                for m in range(24):
                    tX.append(gated(13, m, MIX[m], ACTF.Sigmoid))
                    pump()
                drain()
                t_mg = []
                fmg = last()
                for m in range(KD):
                    acc, afree, ai = sqs.get()
                    acc, prev = acc[:, 0:L], afree
                    for n, Y in enumerate((YA, YB, YM)):
                        b, bi, tk = linear(tile_of("w_branch_2", (l, n), 128 * m), [(Y[k][0], Y[k][1], tY[n]) for k in range(4)], L)
                        t, free, i = tmps.get()
                        dst = acc if n == 0 else t[:, 0:L]
                        t1 = tt(DVE, dst, b[:, 0:L], MIX[8 * n + m], MUL, tk, tX[8 * n + m], free, prev if n == 0 else None)
                        banks.free[bi] = t1
                        if n:
                            t1 = tt(DVE, acc, acc, t[:, 0:L], ADD, t1, prev)
                        tmps.free[i] = t1
                        prev = t1
                    sqs.free[ai] = dual(acc, MG[m][0], MG[m][1], prev, fmg)
                    t_mg.append(sqs.free[ai])
                tsum = Sums(L, both=False)
                nxs = []
                for k in range(KD):
                    b, bi, tk = linear(tile_of("w_out_2", (l,), 128 * k), [(MG[m][0], MG[m][1], t_mg[m]) for m in range(KD)], L)
                    x = Xt[k][:, 0:L]
                    t = tt(DVE, x, x, b[:, 0:L], ADD, tk)
                    banks.free[bi] = t
                    tsum.add(x, t)
                    nxs.append(t)
                xs = nxs
            if depth == 2:
                tr = tsum.finish(D, "eps6")
                xs = [stt(DVE, Xt[k][:, 0:L], Xt[k][:, 0:L], P("fin_g", k, k + 1), w_rstd[:, 0:L], MUL, MUL, tr) for k in range(KD)]
            return xs

        gens.append(ada(0, range(4)))
        drain()
        for q in (PE, ACT, DVE, POOL):
            q.wait(tc)
        G, Bc, tcol = norm_cols(None, None, 0, 0, 1, None)
        ms = []
        for k in range(KD):
            m, mfree, mi = sqs.get()
            for s, a, b in halves(T):
                t = ts(DVE, m[:, a:b], Xt[k][:, a:b], G[:, k, s:s + 1], Bc[:, k, s:s + 1], MUL, ADD, tx, tcol, mfree)
            sqs.free[mi] = dual(m, XM[k][0], XM[k][1], t)
            ms.append(sqs.free[mi])
        xs = [tx] * KD
        gens.append(ada(0, range(4, 18)))
        xs, ms = ffn(0, 0, T, xs, ms, ("ln_g00", "ln_b00"), lambda: norm_cols("ln_g00", "ln_b00", 0, 3, 4, None))

        if stage != "ffn0":
            gens.append(ada(1, range(18)))
            xs, ms = even_mixer(xs, ms)
        if stage not in ("ffn0", "even"):
            xs, ms = ffn(0, 1, T, xs, ms, ("ln_g02", "ln_b02"), lambda: norm_cols("ln_g02", "ln_b02", 1, 0, 1, None))
            xs, ms = ffn(1, 0, T, xs, ms, ("ln_g10", "ln_b10"), lambda: norm_cols("ln_g10", "ln_b10", 1, 3, 4, None))
        if stage not in ("ffn0", "even", "l1f"):
            xs, ms = odd_mixer(xs, ms)
        if stage not in ("ffn0", "even", "l1f", "odd"):
            xs, ms = ffn(1, 1, L, xs, ms, ("ln_g12", "ln_b12"), None)
        if stage not in ("ffn0", "even", "l1f", "odd", "first"):
            xs = second_block(xs, 1 if stage == "second0" else 2)
        drain()
        no = T if stage in ("ffn0", "even", "l1f") else L
        for k in range(KD):
            SP.wait(xs[k])
            SP.ops.append([lambda e, k=k: e.dma_start(OUT[:, k, 0:no], Xt[k][:, 0:no]).then_inc(s_out, 16), None, 0])
        SP.ops.append([None, s_out, 16 * KD])

        block = ctx.enter_context(nc.Block())

        @block.sync
        def _(eng):
            SP.play(eng)

        @block.tensor
        def _(eng):
            PE.play(eng)

        @block.scalar
        def _(eng):
            ACT.play(eng)

        @block.vector
        def _(eng):
            DVE.play(eng)

        @block.gpsimd
        def _(eng):
            POOL.play(eng)
    return recipes


def program(nc, nch, stage="all"):
    pn = sum(n for _, n, _ in param_list())
    cn = sum(a.shape[1] for _, a in constant_list())

    def dram(name, shape, kind="ExternalInput"):
        return nc.dram_tensor(name, shape, F32, kind=kind).ap()

    args = [dram("w_stream", [nch, 128, CH]), dram("params", [128, pn]), dram("consts", [128, cn]),
            dram("x_t", [128, KD * T]), dram("mem_t", [128, KD * L]), dram("out_t", [128, KD, T if stage in ("ffn0", "even", "l1f") else L], "ExternalOutput")]
    return build(nc, nch, *args, stage=stage)


def lay_out(a, recipes):
    nch = recipes[-1][0] + 1
    w = np.zeros((nch, 128, CH), np.float32)
    for c, off, n, parts in recipes:
        for name, idx, r0, nr, c0, ncol, at in parts:
            w[c, 0:nr, off + at:off + at + ncol] = a[name][idx][r0:r0 + nr, c0:c0 + ncol]
    x = np.concatenate([a["x"][0], a["ctx"][0]], 0)
    return {
        "w_stream": w,
        "params": np.concatenate([fn(a) for _, _, fn in param_list()], 1),
        "consts": np.concatenate([c for _, c in constant_list()], 1),
        "x_t": np.ascontiguousarray(x.T.reshape(KD, 128, T).transpose(1, 0, 2).reshape(128, KD * T)),
        "mem_t": np.ascontiguousarray(a["mem_2"][0].T.reshape(KD, 128, L).transpose(1, 0, 2).reshape(128, KD * L)),
    }


def kernel(**inputs):
    import concourse.bacc as bacc
    from concourse.bass_utils import run_bass_kernel_spmd

    a = {k: np.asarray(v) for k, v in inputs.items()}
    nc = bacc.Bacc("TRN2", target_bir_lowering=False, num_devices=1)
    recipes = program(nc, NCH)
    assert recipes[-1][0] + 1 == NCH
    r = run_bass_kernel_spmd(nc, [lay_out(a, recipes)], core_ids=[0])
    y = r.results[0]["out_t"]
    return np.ascontiguousarray(y.transpose(2, 1, 0)).reshape(1, L, D)
```

```python
import math
from contextlib import ExitStack
from itertools import chain

import numpy as np

import concourse.bass as bass
from concourse import mybir

F32 = mybir.dt.float32
F32R = mybir.dt.float32r
ALU = mybir.AluOpType
ACTF = mybir.ActivationFunctionType
AXX = mybir.AxisListType.X

D, T, L = 1024, 512, 256
KD = D // 128
DFF = 2816
KF = DFF // 128
ALPHA = 4.0 ** 0.25
CH = 1024
NSLOT = 3
NSPL = 4
HC = CH // 2
NCH = 658
NEG = -1.0e30
IN2 = (512,) * 8 + (512, 64, 8, 512, 512, 3072)
OFF2 = [sum(IN2[:i]) for i in range(len(IN2))]


def cols(v, n=None):
    return np.asarray(v).reshape(-1, 128).T


def param_list():
    out = []

    def add(name, n, fn):
        out.append((name, n, fn))

    add("cond", 16, lambda a: np.stack([cols(a["c"][0]), cols(a["c_ctx"])], -1).reshape(128, 16))
    for l in range(2):
        add(f"ada_b{l}", 72, lambda a, l=l: cols(a["ada_b"][l]))
        for j in range(3):
            add(f"ln_g{l}{j}", 8, lambda a, l=l, j=j: cols(a["ln_g"][l, j]))
            add(f"ln_b{l}{j}", 8, lambda a, l=l, j=j: cols(a["ln_b"][l, j]))
        add(f"norm2_{l}", 8, lambda a, l=l: cols(a["norm_g_2"][l]))
        add(f"mnorm2_{l}", 8, lambda a, l=l: cols(a["mem_norm_g_2"][l]))
    add("fin_g", 8, lambda a: cols(a["final_g_2"]))
    add("conv", 60, lambda a: a["even_qkv_conv"][0].reshape(5, 12, 128).transpose(2, 1, 0).reshape(128, 60))
    add("dwc", 124, lambda a: a["cf_dw_conv"][0].reshape(31, 4, 128).transpose(2, 1, 0).reshape(128, 124))
    add("dwb", 4, lambda a: cols(a["cf_dw_bias"][0]))
    add("clg", 4, lambda a: cols(a["cf_ln_g"][0]))
    add("clb", 4, lambda a: cols(a["cf_ln_b"][0]))
    add("onorm", 1, lambda a: cols(a["gdn_out_norm"][0]))
    add("qn", 1, lambda a: cols(a["attn_q_norm"][0]))
    add("kn", 1, lambda a: cols(a["attn_k_norm"][0]))

    def gates(a, name):
        v = np.zeros((128, 1), np.float32)
        v[0:4, 0] = a[name][0, 0]
        v[32:36, 0] = a[name][0, 1]
        return v

    add("alog", 1, lambda a: gates(a, "gdn_a_log"))
    add("dtb", 1, lambda a: gates(a, "gdn_dt_bias"))
    return out


def constant_list():
    out = []
    p = np.arange(128)
    out.append(("ident", np.eye(128)))
    out.append(("ones", np.full((128, 128), 1.0)))
    out.append(("sel4", np.concatenate([np.eye(2), np.eye(2), np.zeros((124, 2))])))
    j, i = p[:, None] % 64, np.arange(64)[None, :]
    for n, ok in (("f", i >= j), ("b", i <= j)):
        out.append((f"inc_{n}", ok))
    for n, ok in (("f", i > j), ("b", i < j)):
        out.append((f"str_{n}", ok))
    r, c = p[:, None] % 64, np.arange(64)[None, :]
    for b in (1, 2, 4, 8, 16, 32):
        same = r // (2 * b) == c // (2 * b)
        low = same & ((r // b) % 2 == 1) & ((c // b) % 2 == 0)
        up = same & ((r // b) % 2 == 0) & ((c // b) % 2 == 1)
        if b == 1:
            out.append(("u1_f", -1.0 * up))
            out.append(("u1_b", -1.0 * low))
        else:
            out.append((f"lv{b}_f", low))
            out.append((f"lv{b}_b", up))
    out.append(("id64", r == c))
    for n, step in (("eps5", 1e-5), ("eps6", 1e-6), ("eps128", 128e-6)):
        out.append((n, np.full((128, 1), step)))
    s = np.ones((128, 64))
    s[:, 0] = 0
    out.append(("sg", s))
    t = np.arange(L)
    inv = np.float32(10000.0) ** (-np.arange(32, dtype=np.float32) / np.float32(32))
    ang = np.concatenate([(t // 64).astype(np.float32)[:, None] * inv, (t % 64).astype(np.float32)[:, None] * inv], -1)
    out.append(("ropeC", np.repeat(np.cos(ang).T, 2, axis=0)))
    out.append(("ropeS", np.repeat(np.sin(ang).T, 2, axis=0)))
    rot = np.zeros((128, 128))
    for k in range(64):
        rot[2 * k, 2 * k + 1] = -1
        rot[2 * k + 1, 2 * k] = 1
    out.append(("rotT", rot.T))
    inv = np.float32(500000.0) ** (-np.arange(8, dtype=np.float32) / np.float32(8))
    ang = t.astype(np.float32)[:, None] * inv[None, :]
    C, S, R = np.ones((128, L)), np.zeros((128, L)), np.zeros((128, 128))
    for h in (0, 64):
        for k in range(8):
            C[h + k] = C[h + 8 + k] = np.cos(ang[:, k])
            S[h + k] = S[h + 8 + k] = np.sin(ang[:, k])
            R[h + k, h + 8 + k] = -1
            R[h + 8 + k, h + k] = 1
    out.append(("prC", C))
    out.append(("prS", S))
    out.append(("prT", R.T))
    q = np.concatenate([p[:, None] + 128 * n >= np.arange(L)[None, :] for n in range(2)], 1)
    out.append(("causal", np.where(q, 0.0, NEG)))
    return [(n, np.ascontiguousarray(a, dtype=np.float32)) for n, a in out]


class Queue:

    def __init__(self, sem):
        self.sem, self.ops, self.n, self.seen = sem, [], 0, {}

    def wait(self, *tokens):
        for t in tokens:
            if t is None:
                continue
            if isinstance(t, list):
                self.wait(*t)
                continue
            assert t != "taken", "a buffer is used again before its last reader is known"
            sem, value = t
            if self.seen.get(id(sem), 0) < value:
                self.seen[id(sem)] = value
                self.ops.append([None, sem, value])

    def quiet(self, fn, *tokens):
        self.wait(*tokens)
        self.ops.append([fn, None, 0])

    def mark(self):
        op = self.ops[-1]
        if op[0] is not None and op[1] is None:
            self.n += 1
            op[1] = self.sem
        elif op[0] is None:
            return (self.sem, self.n) if self.n else None
        return (self.sem, self.n)

    def do(self, fn, *tokens):
        self.quiet(fn, *tokens)
        return self.mark()

    def play(self, eng):
        for fn, sem, value in self.ops:
            if fn is None:
                eng.wait_ge(sem, value)
            else:
                ins = fn(eng)
                if sem is not None:
                    ins.then_inc(sem, 1)


class Rot:

    def __init__(self, bufs):
        self.bufs, self.free, self.i = bufs, [None] * len(bufs), -1

    def get(self):
        n = len(self.bufs)
        self.i = next(i % n for i in range(self.i + 1, self.i + 1 + n) if self.free[i % n] != ["taken"])
        free, self.free[self.i] = self.free[self.i], ["taken"]
        return self.bufs[self.i], free, self.i


def build(nc, nch, W, PRM, CST, XT, MT, OUT, stage="all"):
    recipes = []
    ctx = ExitStack()
    with ctx:
        def sb(name, n):
            return ctx.enter_context(nc.sbuf_tensor(name, [128, n], F32))

        def sem(name):
            return ctx.enter_context(nc.semaphore(name))

        PE, ACT, DVE, POOL, SP = (Queue(sem(n)) for n in ("s_pe", "s_act", "s_dve", "s_pool", "s_sp"))
        s_prm, s_cst, s_x, s_m, s_out = (sem(n) for n in ("d_prm", "d_cst", "d_x", "d_m", "d_out"))
        s_w = [sem(f"d_w{i}") for i in range(NSLOT)]

        ring = sb("ring", NSLOT * CH)
        X = sb("X", KD * T)
        pl, cl = param_list(), constant_list()
        prm = sb("prm", sum(n for _, n, _ in pl))
        cst = sb("cst", sum(a.shape[1] for _, a in cl))
        small = sb("small", 980)
        WK = 30720
        BIGN = WK
        with nc.sbuf_tensor("big", [128, BIGN], F32) as big:
            pass
        bigr = ctx.enter_context(nc.sbuf_tensor("bigr", [128, BIGN], F32R))
        work = sb("work", 9 * 512)
        spl = ctx.enter_context(nc.sbuf_tensor("spl", [128, NSPL * 2 * HC], F32R))
        csr = ctx.enter_context(nc.sbuf_tensor("csr", [128, 160], F32R))
        banks = Rot([ctx.enter_context(nc.psum_tensor(f"ps{i}", [128, 512], F32))[:, :] for i in range(8)])

        at = {}
        o = 0
        for n, w, _ in pl:
            at[n] = (prm, o, w)
            o += w
        o = 0
        for n, a in cl:
            at[n] = (cst, o, a.shape[1])
            o += a.shape[1]

        def P(name, a=0, b=None):
            t, o, w = at[name]
            return t[:, o + a:o + (w if b is None else b)]

        so = [0]

        def sm(n):
            so[0] += n
            assert so[0] <= 980, so
            return small[:, so[0] - n:so[0]]

        def last():
            return [q.mark() if q.ops else None for q in (PE, ACT, DVE, POOL)]

        state = {"half": -1, "off": HC, "split": {}, "used": {}, "pool": False, "auto": False}

        def load(c):
            s = c % NSLOT
            SP.wait(state["split"].get(2 * (c - NSLOT)), state["split"].get(2 * (c - NSLOT) + 1))
            SP.ops.append([lambda e: e.dma_start(ring[:, s * CH:(s + 1) * CH], W[c]).then_inc(s_w[s], 16), None, 0])

        def split(h):
            c = h // 2
            if c >= nch:
                return
            if h % 2 == 0:
                if h == 0:
                    for i in range(NSLOT):
                        load(i)
                elif c + NSLOT - 1 < nch:
                    load(c + NSLOT - 1)
                for at_, dst, src, s in ((1, cst, CST, s_cst), (4, X, XT, s_x)):
                    if c == at_:
                        SP.ops.append([lambda e, dst=dst, src=src, s=s: e.dma_start(dst[:, :], src).then_inc(s, 16), None, 0])
            a = (c % NSLOT) * CH + (h % 2) * HC
            raw = ring[:, a:a + HC]
            base = (h % NSPL) * 2 * HC
            hi, lo = spl[:, base:base + HC], spl[:, base + HC:base + 2 * HC]
            arrived = (s_w[c % NSLOT], 16 * (c // NSLOT + 1))
            t = ACT.do(lambda e: e.activation(hi, raw, ACTF.Copy), arrived, state["used"].get(h - NSPL))
            q = POOL if state["pool"] and h % 2 else DVE
            state["split"][h] = q.do(lambda e: e.tensor_tensor(lo, raw, hi, ALU.subtract), t)

        def take(recipe, n=128):
            if state["off"] + n > HC:
                h = state["half"]
                if h >= 0:
                    state["used"][h] = PE.mark()
                    split(h + NSPL)
                else:
                    for i in range(NSPL):
                        split(i)
                state["half"] += 1
                state["off"] = 0
            h = state["half"]
            recipes.append((h // 2, (h % 2) * HC + state["off"], n, recipe))
            a = (h % NSPL) * 2 * HC + state["off"]
            state["off"] += n
            return spl[:, a:a + n], spl[:, a + HC:a + HC + n], state["split"].get(h)

        def mm(out, lhsT, rhs, start, stop, *tokens, **kw):
            PE.quiet(lambda e: e.matmul(out, lhsT, rhs, start=start, stop=stop, **kw), *tokens)

        def transp(out, in_, k, *tokens):
            PE.quiet(lambda e: e.transpose(out, in_, P("ident")[0:k, 0:k]), *tokens)

        def ts(q, out, a, s1, s2, op0, op1, *tokens):
            if op1 is None:
                return q.do(lambda e: e.tensor_scalar(out, a, s1, None, op0), *tokens)
            return q.do(lambda e: e.tensor_scalar(out, a, s1, s2, op0, op1), *tokens)

        def tt(q, out, a, b, op, *tokens):
            return q.do(lambda e: e.tensor_tensor(out, a, b, op), *tokens)

        def stt(q, out, a, s, b, op0, op1, *tokens):
            return q.do(lambda e: e.scalar_tensor_tensor(out, a, s, b, op0, op1), *tokens)

        def act(out, a, fn, *tokens, **kw):
            return ACT.do(lambda e: e.activation(out, a, fn, **kw), *tokens)

        def copy(q, out, a, *tokens):
            if q is ACT:
                return act(out, a, ACTF.Copy, *tokens)
            return q.do(lambda e: e.tensor_copy(out, a), *tokens)

        def memset(q, out, v, *tokens):
            return q.do(lambda e: e.memset(out, v), *tokens)

        MUL, ADD, SUB = ALU.mult, ALU.add, ALU.subtract

        def mm3(out, st, mv, start, stop, *tokens):
            mm(out, st[0], mv[0], start, False, *tokens)
            mm(out, st[0], mv[1], False, False)
            mm(out, st[1], mv[0], False, stop)

        def linear(w, src, n):
            bank, free, bi = banks.get()
            for k, (hi, lo, tok) in enumerate(src):
                whi, wlo, wtok = take(w(k))
                mm3(bank[:, 0:n], (whi, wlo), (hi, lo), k == 0, k == len(src) - 1, free, wtok, tok)
                t = PE.mark() if k == len(src) - 1 else None
                if k % 4 == 3 and state["auto"]:
                    pump()
            old, later[:] = list(later), []
            for fn in old:
                fn()
            return bank, bi, t

        def pair(w0, w1, src, n, between=None):
            bs = [banks.get() for _ in range(2)]
            for k in range(len(src)):
                if between:
                    between(k)
                hi, lo, tok = src[k]
                for (bank, free, bi), w in zip(bs, (w0, w1)):
                    whi, wlo, wtok = take(w(k))
                    mm3(bank[:, 0:n], (whi, wlo), (hi, lo), k == 0, k == len(src) - 1, free, wtok, tok)
            t = PE.mark()
            old, later[:] = list(later), []
            for fn in old:
                fn()
            return [(bank, bi, t) for bank, free, bi in bs]

        later = []

        def flush():
            while later:
                later.pop(0)()

        def dual(raw, hi, lo, tok, *more, q=None):
            t = copy(ACT, hi, raw, tok, *more)
            return tt(q or POOL, lo, raw, hi, SUB, t)

        def tile_of(name, idx, c0):
            return lambda k: [(name, idx, 128 * k, 128, c0, 128, 0)]

        for dst, src, s in ((prm, PRM, s_prm),):
            SP.ops.append([lambda e, dst=dst, src=src, s=s: e.dma_start(dst[:, :], src).then_inc(s, 16), None, 0])
        tp, tc, tx = (s_prm, 16), (s_cst, 16), (s_x, 16)
        for q in (PE, ACT, DVE, POOL):
            q.wait(tp)

        def B(a, n):
            return big[:, a:a + n]

        def R(a, n):
            return bigr[:, a:a + n]

        Xt = [X[:, k * T:(k + 1) * T] for k in range(KD)]
        XM = [(R(k * T, T), R((KD + k) * T, T)) for k in range(KD)]

        nega, colA, colT, colB, colG = sm(1), sm(64), sm(32), sm(32), sm(64)
        wi, mx8 = sm(16), sm(16)

        cs = sm(16)
        t_cs = act(cs, P("cond"), ACTF.Silu)
        cs3, c3 = cs.rearrange("p (k s) -> p k s", s=2), csr[:, 0:32].rearrange("p (k s) -> p k s", s=4)
        t = memset(DVE, csr[:, 32:160].bitcast(F32), 0.0)
        t1 = copy(DVE, c3[:, :, 0:2], cs3, t_cs)
        t_cs = tt(DVE, c3[:, :, 2:4], cs3, c3[:, :, 0:2], SUB, t1)
        mods, t_mod, md_ = {}, {}, {}
        arow = sb("arow", 1024)
        arows = Rot([arow[0:4, 0:512], arow[0:4, 512:1024]])

        def ada(l, groups):
            if l not in mods:
                md_[l] = sm(144)
                mods[l], t_mod[l] = md_[l].rearrange("p (i m s) -> p i m s", i=9, s=2), {}
            md = md_[l]

            def turn(g, row, t_row, ri):
                bank, free, bi = banks.get()
                for q in range(4):
                    mm(bank[:, 2 * q:2 * q + 2], row[:, q * 128:(q + 1) * 128], P("sel4")[0:4, :], True, True, t_row, free, tc)
                t = PE.mark()
                arows.free[ri] = t
                t = tt(DVE, md[:, 8 * g:8 * g + 8].rearrange("p (a s) -> p a s", s=2), bank[:, 0:8].rearrange("p (a s) -> p a s", s=2),
                       P(f"ada_b{l}", 4 * g, 4 * g + 4).unsqueeze(2).broadcast_to([128, 4, 2]), ADD, t)
                banks.free[bi] = t
                t_mod[l][g] = t

            prev = None
            for g in groups:
                bank, free, bi = banks.get()
                for k in range(KD):
                    whi, wlo, wtok = take([("ada_w", (l,), 128 * k, 128, 512 * g, 512, 0)], 512)
                    mm(bank, csr[:, 4 * k:4 * k + 128], whi, k == 0, False, free, wtok, t_cs)
                    mm(bank, csr[:, 4 * k:4 * k + 128], wlo, False, k == KD - 1)
                    if k == 1 and prev:
                        turn(*prev)
                    if k < KD - 1:
                        yield
                t = PE.mark()
                row, rfree, ri = arows.get()
                t_row = copy(ACT, row, bank[0:4, :], t, rfree)
                banks.free[bi] = t_row
                prev = (g, row, t_row, ri)
                yield
            turn(*prev)

        def mod_ready(l, *i):
            return [t_mod[l][2 * j + e] for j in i for e in (0, 1)]

        def norm_cols(g, b, l, i_shift, i_scale, tok):
            G = sm(16).rearrange("p (m s) -> p m s", s=2)
            Bc = sm(16).rearrange("p (m s) -> p m s", s=2)
            sc, sh = mods[l][:, i_scale], mods[l][:, i_shift]
            t = ts(DVE, G, sc, 1.0, None, ADD, None, tok, mod_ready(l, i_shift, i_scale))
            if g is None:
                t2 = copy(DVE, Bc, sh, t)
                return G, Bc, t2
            bb = P(b).unsqueeze(2).broadcast_to([128, 8, 2])
            gg = P(g).unsqueeze(2).broadcast_to([128, 8, 2])
            t = tt(DVE, Bc, G, bb, MUL, t)
            t = tt(DVE, Bc, Bc, sh, ADD, t)
            t = tt(DVE, G, G, gg, MUL, t)
            return G, Bc, t

        def gate_cols(l, i, half, tok=None):
            gt = sm(16).rearrange("p (m s) -> p m s", s=2)
            t = ts(DVE, gt, mods[l][:, i], half, None, MUL, None, mod_ready(l, i))
            return gt, t

        wk = [work[:, 512 * i:512 * i + 512] for i in range(9)]
        tmps = Rot(wk[0:3])
        sqs = Rot(wk[3:5])
        accS, accQ, w_mean, w_rstd = wk[5], wk[6], wk[7], wk[8]

        class Sums:

            def __init__(self, n, both=True, tok=None):
                self.n, self.both, self.first, self.tok = n, both, True, tok
                self.ts = self.tq = self.tp = tok
                self.count = 0

            def add(self, ap, tok, last=False):
                n = self.n
                sq, free, i = sqs.get()
                t = act(sq[:, 0:n], ap, ACTF.Square, tok, free)
                pool = DVE if last else POOL
                self.count += 1
                if not self.both and self.count % 2 == 0:
                    if self.count == 2:
                        self.tp = copy(DVE, accS[:, 0:n], sq[:, 0:n], t, self.tp)
                    else:
                        self.tp = tt(DVE, accS[:, 0:n], accS[:, 0:n], sq[:, 0:n], ADD, t, self.tp)
                    sqs.free[i] = self.tp
                    return self.tp
                if self.first:
                    if self.both:
                        self.ts = copy(pool, accS[:, 0:n], ap, tok, self.ts)
                    self.tq = copy(POOL, accQ[:, 0:n], sq[:, 0:n], t, self.tq)
                else:
                    if self.both:
                        self.ts = tt(pool, accS[:, 0:n], accS[:, 0:n], ap, ADD, tok, self.ts)
                    self.tq = tt(pool, accQ[:, 0:n], accQ[:, 0:n], sq[:, 0:n], ADD, t, self.tq)
                sqs.free[i] = self.tq
                self.first = False
                return self.tq

            def finish(self, count, eps):
                n = self.n
                b, col, tk, bi, ci = by_columns(n, [(accQ, self.tq)] + ([] if self.both else [(accS, self.tp)]), [(accS, self.ts)] if self.both else [])
                nb = n // 128
                if not self.both:
                    return root(n, b, col, tk, bi, ci, 1.0 / count, eps)
                m, v = col[:, 0:nb], col[:, 4:4 + nb]
                tm = ts(DVE, m, b[:, 4:4 + nb], 1.0 / count, None, MUL, None, tk)
                t = tt(DVE, v, m, m, MUL, tm)
                t = stt(DVE, v, b[:, 0:nb], 1.0 / count, v, MUL, SUB, t)
                banks.free[bi] = t
                t = ts(DVE, v, v, 0.0, None, ALU.max, None, t)
                t = act(v, v, ACTF.Sqrt, t, bias=P(eps))
                mean = spread(n, m, tm)
                tr = DVE.do(lambda e: e.reciprocal(col[:, 8:8 + nb], v), t)
                r = spread(n, col[:, 8:8 + nb], tr)
                cols_.free[ci] = r[1]
                return mean, r

        cols_ = Rot([sm(16) for _ in range(4)])

        def by_columns(n, squares, plain=()):
            b, free, bi = banks.get()
            col, cfree, ci = cols_.get()
            for at_, lst in ((4, plain), (0, squares)):
                for t_ in range(n // 128 if lst else 0):
                    for i, (ap, tok) in enumerate(lst):
                        mm(b[:, at_ + t_:at_ + t_ + 1], ap[:, 128 * t_:128 * t_ + 128], P("ones")[:, 0:1], i == 0, i == len(lst) - 1, free, tok, cfree)
            return b, col, [PE.mark(), cfree], bi, ci

        def root(n, b, col, tk, bi, ci, scale, eps, defer=False):
            nb = n // 128
            t = act(col[:, 0:nb], b[:, 0:nb], ACTF.Sqrt, tk, scale=scale, bias=P(eps))
            banks.free[bi] = t
            t = DVE.do(lambda e: e.reciprocal(col[:, 8:8 + nb], col[:, 0:nb]), t)

            def rest():
                later_half = spread(n, col[:, 8:8 + nb], t, defer=True)

                def product():
                    r = later_half()
                    cols_.free[ci] = r[1]
                    return r

                return product if defer else product()

            return rest if defer else rest()

        def spread(n, col, tok, defer=False):
            def product():
                b, bfree, bi = banks.get()
                for t_ in range(n // 128):
                    mm(b[:, 128 * t_:128 * t_ + 128], col[:, t_:t_ + 1].broadcast_to([128, 128]), P("ident"), True, True, tok, bfree)
                return b, PE.mark(), bi

            return product if defer else product()

        def halves(n):
            return [(0, 0, 256), (1, 256, 512)] if n == T else [(0, 0, n)]

        def layer_norm_x(n, sums, lnp, nxt, out, extra=None):
            tsub = []

            def subtract(mean, count):
                for k in range(len(tsub), min(KD, len(tsub) + count)):
                    x = Xt[k][:, 0:n]
                    tsub.append(tt(DVE, x, x, mean[0][:, 0:n], SUB, mean[1], sums.tq))

            mean, r = sums.finish(D, "eps5")
            subtract(mean, 1)
            G, Bc, tcol = nxt
            xs, ms, tn = [None] * KD, [], []
            for k in range(KD):
                subtract(mean, 1)
                x = Xt[k][:, 0:n]
                t1 = tt(DVE, x, x, r[0][:, 0:n], MUL, r[1], tsub[k])
                if k == KD - 1:
                    banks.free[mean[2]] = banks.free[r[2]] = t1
                if G is None:
                    if k == 0:
                        following = Sums(n, both=False, tok=last())
                    if k % 2:
                        xs[k] = ts(DVE, x, x, P(lnp[0], k, k + 1), P(lnp[1], k, k + 1), MUL, ADD, t1)
                    else:
                        xs[k] = act(x, x, ACTF.Identity, t1, scale=P(lnp[0], k, k + 1), bias=P(lnp[1], k, k + 1))
                    if k:
                        following.add(Xt[k - 1][:, 0:n], xs[k - 1])
                    if k == KD - 1:
                        following.add(x, xs[k], True)
                    continue
                m, mfree, mi = sqs.get()
                tm = []
                for s, a, b in halves(n):
                    if s:
                        tm.append(act(m[:, a:b], x[:, a:b], ACTF.Identity, t1, tcol, mfree, scale=G[:, k, s:s + 1], bias=Bc[:, k, s:s + 1]))
                    else:
                        tm.append(ts(DVE, m[:, a:b], x[:, a:b], G[:, k, s:s + 1], Bc[:, k, s:s + 1], MUL, ADD, t1, tcol, mfree))
                td = dual(m[:, 0:n], out[k][0][:, 0:n], out[k][1][:, 0:n], tm, extra)
                sqs.free[mi] = td
                tn.append([t1, tm])
                ms.append(td)

            def update():
                for k in range(KD):
                    x = Xt[k][:, 0:n]
                    xs[k] = act(x, x, ACTF.Identity, tn[k], scale=P(lnp[0], k, k + 1), bias=P(lnp[1], k, k + 1))

            if G is None:
                return xs, following
            later.append(update)
            return xs, ms

        def residual(bank, bi, tk, k, n, gt, tg, sums, xtok):
            t, free, i = tmps.get()
            for s, a, b in halves(n):
                ta = act(t[:, a:b], bank[:, a:b], ACTF.Copy, tk, free, tg, scale=gt[:, k, s:s + 1])
            banks.free[bi] = ta
            x = Xt[k][:, 0:n]
            tr = stt(DVE, x, x, ALPHA, t[:, 0:n], MUL, ADD, ta, xtok)
            tmps.free[i] = tr
            return sums.add(x, tr, k == KD - 1)

        def ffn(l, j, n, xs, ms, lnp, nxt, out_extra=None):
            Ht = [(R(2 * KD * T + m * n, n), R(2 * KD * T + (KF + m) * n, n)) for m in range(KF)]
            hs = []
            state["auto"] = bool(gens)
            for m in range(KF):
                src = [(XM[k][0][:, 0:n], XM[k][1][:, 0:n], ms[k]) for k in range(KD)]
                wg, wu = tile_of("ffn_w_gu", (l, j), 128 * m), tile_of("ffn_w_gu", (l, j), DFF + 128 * m)
                if m:
                    bg, ig, tg1 = linear(wg, src, n)
                    bu, iu, tu = linear(wu, src, n)
                else:
                    (bg, ig, tg1), (bu, iu, tu) = pair(wg, wu, src, n)
                t, free, i = tmps.get()
                ta = act(t[:, 0:n], bg[:, 0:n], ACTF.Silu, tg1, free)
                banks.free[ig] = ta
                th = tt(DVE, t[:, 0:n], t[:, 0:n], bu[:, 0:n], MUL, ta, tu)
                banks.free[iu] = th
                th = dual(t[:, 0:n], Ht[m][0][:, 0:n], Ht[m][1][:, 0:n], th)
                tmps.free[i] = th
                hs.append(th)
            gt, tg = gate_cols(l, 2 + 6 * j, 0.5)
            sums = Sums(n)
            for k in range(KD):
                b, bi, tk = linear(tile_of("ffn_w_down", (l, j), 128 * k), [(Ht[m][0][:, 0:n], Ht[m][1][:, 0:n], hs[m]) for m in range(KF)], n)
                residual(b, bi, tk, k, n, gt, tg, sums, xs[k])
            state["auto"] = False
            drain()
            return layer_norm_x(n, sums, lnp, nxt() if nxt else (None, None, None), XM, out_extra)

        gens = []

        def pump(n=1):
            for _ in range(n):
                if gens:
                    try:
                        next(gens[0])
                    except StopIteration:
                        gens.pop(0)

        def drain():
            flush()
            while gens:
                pump()

        def even_mixer(xs, ms):
            f0 = last()
            QK = [B(16624 + i * 512, 512) for i in range(8)]
            V = [B(8192 + i * 512, 512) for i in range(4)]
            SZ = [B(10240 + i * 512, 512) for i in range(4)]
            YP = [B(12288 + i * 572, 572).rearrange("p (s t) -> p s t", s=2) for i in range(4)]
            CF = [B(14576 + i * 512, 512) for i in range(4)]
            QEF = [B(20720 + i * 512, 512) for i in range(4)]
            WT = [[B(4096 + (4 * d + h) * 512, 512) for h in range(4)] for d in range(2)]
            UST = B(22768, 4096).rearrange("p (s n) -> p s n", s=8)
            AT = [[B(26864 + (4 * d + h) * 256, 256).rearrange("p (t i) -> p t i", t=4) for h in range(4)] for d in range(2)]
            LN0 = 28912
            R1, R2 = accS, B(20720, 512)
            CP = Rot([B(26864 + i * 520, 520).rearrange("p (s t) -> p s t", s=2) for i in range(2)])
            for i in range(2):
                CP.free[i] = memset(POOL, CP.bufs[i], 0.0, f0)
            t_yp = [memset(POOL, YP[i], 0.0, f0) for i in range(4)]

            def two(ap):
                return ap.rearrange("p (s t) -> p s t", s=2)

            src = [(XM[k][0], XM[k][1], ms[k]) for k in range(KD)]
            (bab, iab, tab), first = pair(lambda k: [("even_w_in", (0,), 128 * k, 128, 2048 + 4 * r, 4, 32 * r) for r in range(4)],
                                          tile_of("even_w_in", (0,), 0), src, T)
            WTf = [B(22768 + i * 512, 512) for i in range(8)]
            xr, mr, er, zr, z2, pr = [w[0:64, :] for w in WTf[0:6]]
            t = ts(DVE, xr, bab[0:64, :], P("dtb")[0:64], None, ADD, None, tab, f0)
            tb = act(R1[64:128, :], bab[64:128, :], ACTF.Sigmoid, tab, f0)
            banks.free[iab] = [t, tb]
            def gate_chain(t):
                tm = ts(DVE, mr, xr, 0.0, None, ALU.max, None, t)
                t2 = ts(DVE, zr, xr, -1.0, None, MUL, None, t)
                t2 = tt(DVE, zr, zr, xr, ALU.min, t2)
                te = act(er, zr, ACTF.Exp, t2)
                yield
                ta = act(nega[0:64], P("alog")[0:64], ACTF.Exp)
                t = ts(DVE, zr, er, 2.0, None, ADD, None, te)
                t = DVE.do(lambda e: e.reciprocal(zr, zr), t)
                t = tt(DVE, zr, zr, er, MUL, t)
                yield
                t = tt(DVE, z2, zr, zr, MUL, t)
                t = ts(DVE, pr, z2, 1.0 / 15, None, MUL, None, t)
                for c in (13, 11, 9, 7, 5, 3):
                    t = stt(DVE, pr, pr, 1.0 / c, z2, ADD, MUL, t)
                    if c in (11, 7, 3):
                        yield
                t = stt(DVE, pr, pr, 1.0, zr, ADD, MUL, t)
                t = stt(DVE, pr, pr, 2.0, mr, MUL, ADD, t, tm)
                t = ts(DVE, pr, pr, nega[0:64], -1.0, MUL, MUL, t, ta)
                sgt = WTf[6]
                t1 = memset(DVE, sgt, 1.0, f0)
                t1 = memset(DVE, sgt[:, 0:512:64], 0.0, t1)
                tg1 = DVE.do(lambda e: e.tensor_tensor_scan(R1[0:32, :], sgt[0:32, :], pr[0:32, :], 0.0, MUL, ADD), t, t1)
                yield
                tg2 = DVE.do(lambda e: e.tensor_tensor_scan(R1[32:64, ::-1], sgt[32:64, :], pr[32:64, ::-1], 0.0, MUL, ADD), t, t1)
                yield
                R1c = R1.rearrange("p (c i) -> p c i", i=64)
                R2c = R2.rearrange("p (c i) -> p c i", i=64)
                t3 = tt(DVE, R2c[0:32], R1c[0:32, :, 63:64].broadcast_to([32, 8, 64]), R1c[0:32], SUB, tg1, f0)
                t4 = tt(DVE, R2c[32:64], R1c[32:64, :, 0:1].broadcast_to([32, 8, 64]), R1c[32:64], SUB, tg2)
                t_r1.extend([tb, tg1, tg2])
                t_r2.extend([t3, t4])

            t_r1, t_r2 = [], []
            chain_ = gate_chain(t)

            t_qkv = []
            t_qk = {}

            def l2norm(m):
                sq, free, i = sqs.get()
                t = act(sq, QK[m], ACTF.Square, t_qkv[m], free)

                def stats():
                    c_ = by_columns(T, [(sq, t)])
                    sqs.free[i] = c_[2][0]
                    rest = root(T, *c_, 128.0 if m < 4 else 1.0, "eps128" if m < 4 else "eps6", defer=True)

                    def product():
                        r, tr, ri = rest()()
                        t_qk[m] = tt(DVE, QK[m], QK[m], r, MUL, tr)
                        banks.free[ri] = t_qk[m]

                    later.append(product)

                later.append(stats)

            for m in range(12):
                b, bi, tk = linear(tile_of("even_w_in", (0,), 128 * m), src, T) if m else first
                cp, free, ci = CP.get()
                t = copy(ACT, cp[:, :, 2:258], two(b), tk, free)
                banks.free[bi] = t
                dst = (QK + V)[m]
                ac, afree, ai = tmps.get()
                a3 = two(ac)
                w = lambda j, m=m: P("conv", 5 * m + j, 5 * m + j + 1)
                t = ts(DVE, a3, cp[:, :, 0:256], w(0), None, MUL, None, t, afree)
                for j in range(1, 5):
                    t = stt(DVE, a3, cp[:, :, j:j + 256], w(j), a3, MUL, ADD, t)
                CP.free[ci] = t
                t = act(dst, ac, ACTF.Silu, t, f0)
                tmps.free[ai] = t
                t_qkv.append(t)
                next(chain_, None)
                if 2 <= m < 10:
                    l2norm(m - 2)
            flush()
            t_y = []
            for m in range(4):
                bv, vi, tv = linear(tile_of("even_w_in", (0,), 2064 + 128 * m), src, T)
                bg, gi, tg = linear(tile_of("even_w_in", (0,), 2576 + 128 * m), src, T)
                g, free, i = tmps.get()
                t = act(g, bg, ACTF.Sigmoid, tg, free)
                banks.free[gi] = t
                t = tt(DVE, YP[m][:, :, 15:271], two(g), two(bv), MUL, t, tv, t_yp[m])
                banks.free[vi] = t
                tmps.free[i] = t
                t_y.append(t)
            t_sz = []
            for m in range(4):
                b, bi, tk = linear(tile_of("even_w_in", (0,), 1536 + 128 * m), src, T)
                t = act(SZ[m], b, ACTF.Silu, tk, f0)
                banks.free[bi] = t
                t_sz.append(t)
            t_xm = PE.mark()

            t_cf = []

            def conformer():
                w = lambda j, m: P("dwc", 31 * m + j, 31 * m + j + 1)
                t = [ts(DVE, two(CF[m]), YP[m][:, :, 0:256], w(0, m), P("dwb", m, m + 1), MUL, ADD, t_y[m], f0) for m in range(4)]
                for j in range(1, 31):
                    for m in range(4):
                        t[m] = stt(DVE, two(CF[m]), YP[m][:, :, j:j + 256], w(j, m), two(CF[m]), MUL, ADD, t[m])
                        if m % 2:
                            yield
                t_cf.extend(t)

            cgen = conformer()

            def cstep(n=1):
                for _ in range(n):
                    next(cgen, None)

            def conformer_norm():
                bq, free, bi = banks.get()
                col, cfree, ci = cols_.get()
                for t_ in range(4):
                    for m in range(4):
                        mm(bq[:, 4 + t_:5 + t_], CF[m][:, 128 * t_:128 * t_ + 128], P("ones")[:, 0:1], m == 0, m == 3, free, t_cf[m])
                yield
                fc = last()
                sq4 = [tmps.get(), sqs.get()]
                for half in range(2):
                    for e_, (sq, free, i) in enumerate(sq4):
                        m = 2 * half + e_
                        free = [free, fc, tsq] if half else [free, fc]
                        t = act(sq, CF[m], ACTF.Square, t_cf[m], free)
                        for t_ in range(4):
                            mm(bq[:, 8 + 4 * m + t_:9 + 4 * m + t_], sq[:, 128 * t_:128 * t_ + 128], P("ones")[:, 0:1], True, True, t)
                    tsq = PE.mark()
                    yield
                tmps.free[sq4[0][2]] = sqs.free[sq4[1][2]] = tsq
                mc, vc, qc = col[:, 0:4], col[:, 4:8], col[:, 8:12]
                tm = ts(DVE, mc, bq[:, 4:8], 1.0 / 512, None, MUL, None, tsq, cfree)
                t = DVE.do(lambda e: e.tensor_reduce(qc, bq[:, 8:24].rearrange("p (m t) -> p t m", m=4), AXX, ADD), tsq, cfree)
                banks.free[bi] = t
                t1 = tt(DVE, vc, mc, mc, MUL, tm)
                t = stt(DVE, vc, qc, 1.0 / 512, vc, MUL, SUB, t, t1)
                t = ts(DVE, vc, vc, 0.0, None, ALU.max, None, t)
                t = act(vc, vc, ACTF.Sqrt, t, bias=P("eps5"))
                pm = spread(T, mc, tm, defer=True)
                yield
                bm, tbm_, im = pm()
                mean, rstd = w_mean, w_rstd
                tm = copy(ACT, mean, bm, tbm_, fc)
                banks.free[im] = tm
                yield
                t = DVE.do(lambda e: e.reciprocal(qc, vc), t)
                pr_ = spread(T, qc, t, defer=True)
                yield
                br, tbr, ir = pr_()
                cols_.free[ci] = tbr
                tr = copy(ACT, rstd, br, tbr, fc)
                banks.free[ir] = tr
                yield
                for m in range(4):
                    t = tt(POOL, CF[m], CF[m], mean, SUB, tr, tm)
                    t = tt(POOL, CF[m], CF[m], rstd, MUL, t)
                    t_cf[m] = t

            b, free, bi = banks.get()
            for t_ in range(4):
                transp(b[:, t_ * 128:(t_ + 1) * 128], R1[:, t_ * 128:(t_ + 1) * 128], 128, free, t_r1)
            tk = PE.mark()
            cA4 = colA.rearrange("p (t q h) -> p t q h", t=4, q=4)
            t_ca = copy(DVE, cA4, b.rearrange("p (t q r) -> p t q r", t=4, q=4)[:, :, :, 0:4], tk)
            banks.free[bi] = t_ca
            b, free, bi = banks.get()
            for t_ in range(4):
                transp(b[:, t_ * 64:(t_ + 1) * 64], R2[0:64, t_ * 128:(t_ + 1) * 128], 64, free, t_r2)
            tk = PE.mark()
            cT4 = colT.rearrange("p (t q h) -> p t q h", t=4, q=2)
            t_ct = act(cT4, b[:, 0:256].rearrange("p (t q r) -> p t q r", t=4, q=2)[:, :, :, 0:4], ACTF.Exp, tk)
            banks.free[bi] = t_ct
            cB4 = colB.rearrange("p (t q h) -> p t q h", t=4, q=2)
            t = act(cB4, cA4[:, :, 0:2, :], ACTF.Exp, t_ca)
            t_cb = tt(DVE, cB4, cB4, cA4[:, :, 2:4, :], MUL, t)

            KT = [B(t_ * 512, 512) for t_ in range(4)]
            VT = [B(2048 + t_ * 512, 512) for t_ in range(4)]
            t_kt, t_vt = [], []
            for dst, srcs, toks, out in ((KT, QK[4:8], [t_qk[m] for m in range(4, 8)], t_kt), (VT, V, t_qkv[8:12], t_vt)):
                for t_ in range(4):
                    b, free, bi = banks.get()
                    for h in range(4):
                        transp(b[:, h * 128:(h + 1) * 128], srcs[h][:, t_ * 128:(t_ + 1) * 128], 128, free, toks[h])
                    tk = PE.mark()
                    t = copy(ACT, dst[t_], b, tk, t_xm)
                    banks.free[bi] = t
                    out.append(t)
                pump()
            t_vT = PE.mark()

            def ch(ap, d3=64):
                return ap.rearrange("p (t i) -> p t i", t=4)

            def bc(ap):
                return ap.unsqueeze(1).broadcast_to([128, 4, 64])

            def halfblocks(c):
                return c % 2, c // 2, slice(64 * (c % 2), 64 * (c % 2) + 64)

            id64 = P("id64")
            state["pool"] = True
            egl = colG.rearrange("p (d h c) -> p d h c", d=2, h=4)
            t_at, t_w, t_u, t_qe, t_egl = {}, {}, {}, {}, {}
            sets = [[(B(LN0 + d * 1024, 256), B(LN0 + d * 1024 + 256, 512), accQ[:, 0:256] if d else B(LN0 + 768, 256)) for d in range(2)],
                    [(w_[:, 0:256], WT[d][3], w_[:, 256:512]) for d, w_ in enumerate((w_mean, w_rstd))]]
            setfree = [[f0, f0], [f0, f0]]
            lanes = {}

            def prep(h):
                bufs, bfree = sets[h % 2], setfree[h % 2]
                bG, gfree, gi = banks.get()
                for kind, other in ((0, QK[h]), (1, QK[4 + h])):
                    for c in range(8):
                        p, t_, rows_ = halfblocks(c)
                        mm(bG[rows_, kind * 256 + t_ * 64:kind * 256 + t_ * 64 + 64], QK[4 + h][:, 64 * c:64 * c + 64],
                           other[:, 64 * c:64 * c + 64], True, True, gfree, t_qk[h], t_qk[4 + h])
                t_g = PE.mark()
                yield
                bb, tE, tbm = [], [], []
                for d in range(2):
                    b, free, bi = banks.get()
                    for kind, r in ((0, 32 * d + h), (1, 64 + 32 * d + h)):
                        for p in range(2):
                            mm(b[64 * p:64 * p + 64, kind * 256:kind * 256 + 256].rearrange("p (t i) -> p t i", t=4),
                               P("ident")[:, r:r + 1].broadcast_to([128, 64]),
                               R1.rearrange("r (t p i) -> r t p i", p=2, i=64)[:, :, p, :], True, True, free, t_r1)
                    bb.append((b, bi, PE.mark()))
                for d in range(2):
                    Mt, TU, E = bufs[d]
                    b, bi, tk = bb[d]
                    t = tt(DVE, ch(E), ch(b[:, 0:256]), cA4[:, :, d, h:h + 1].broadcast_to([128, 4, 64]), SUB, tk, t_ca, bfree[d])
                    tbm.append(tt(DVE, ch(Mt), ch(b[:, 256:512]), bc(P(f"str_{'fb'[d]}")), MUL, bfree[d]))
                    banks.free[bi] = [t, tbm[d]]
                    t = ts(DVE, E, E, 0.0, None, ALU.min, None, t)
                    t = act(E, E, ACTF.Exp, t)
                    tE.append(tt(POOL, ch(E), ch(E), bc(P(f"inc_{'fb'[d]}")), MUL, t))
                yield
                ta, tmm = [], []
                for d in range(2):
                    Mt, TU, E = bufs[d]
                    tmm.append(tt(POOL, Mt, Mt, E, MUL, tE[d], tbm[d]))
                    ta.append(tt(DVE, AT[d][h], ch(E), ch(bG[:, 0:256]), MUL, tE[d], t_g))
                    t_at[d, h] = ta[d]
                yield
                tU = []
                for d in range(2):
                    Mt, TU, E = bufs[d]
                    tmm[d] = tt(DVE, Mt, Mt, bG[:, 256:512], MUL, tmm[d])
                    U = TU[:, 256:512]
                    t = tt(POOL, ch(U), ch(Mt), bc(P(f"u1_{'fb'[d]}")), MUL, tmm[d], bfree[d])
                    tU.append(tt(POOL, ch(U), ch(U), bc(id64), ADD, t))
                banks.free[gi] = ta + tmm
                yield
                for d in range(2):
                    Mt, TU, E = bufs[d]
                    U = TU[:, 256:512]
                    b, free, bi = banks.get()
                    for c in range(8):
                        p, t_, rows_ = halfblocks(c)
                        mm(b[rows_, t_ * 64:t_ * 64 + 64], U[rows_, t_ * 64:t_ * 64 + 64], id64[rows_, :], True, True, free, tU[d])
                    tk = PE.mark()
                    tT = copy(ACT, TU[:, 0:256], b[:, 0:256], tk, bfree[d])
                    banks.free[bi] = tT
                    lanes[h, d] = [Mt, TU, E, [tU[d], tT], ta[d], tmm[d]]
                for d in range(2):
                    yield
                    b, free, bi = banks.get()
                    r = 32 * d + h
                    mm(b, P("ident")[:, r:r + 1].broadcast_to([128, 128]), R1, True, True, free, t_r1)
                    tk = PE.mark()
                    if d == 0:
                        e_, efree = QEF[h], f0
                    else:
                        e_, efree, ei = tmps.get()
                    t = act(e_, b, ACTF.Exp, tk, efree)
                    banks.free[bi] = t
                    o_ = 63 if d == 0 else 0
                    t_egl[d, h] = copy(POOL, egl[:, d, h, :], e_[:, o_:512:64], t)
                    dst = QEF[h] if d == 0 else QK[h]
                    t = tt(POOL, dst, QK[h], e_, MUL, t, t_g, t_egl[d, h], t_qe.get((0, h)))
                    t_qe[d, h] = t
                    if d:
                        tmps.free[ei] = t
                yield

            def ending(h):
                tt_ = []
                for d in range(2):
                    Mt, TU, Pm, tU, ta, tmm = lanes[h, d]
                    U = TU[:, 256:512]
                    t1 = tt(DVE, ch(TU[:, 0:256]), ch(U), cA4[:, :, 2 + d, h:h + 1].broadcast_to([128, 4, 64]), MUL, tU)
                    t2 = tt(DVE, ch(Pm), ch(U), cB4[:, :, d, h:h + 1].broadcast_to([128, 4, 64]), MUL, tU, t_cb)
                    tt_.append((t1, t2))
                yield
                for d in range(2):
                    Ub, t1 = lanes[h, d][1][:, 0:256], tt_[d][0]
                    b, free, bi = banks.get()
                    for c in range(8):
                        p, t_, rows_ = halfblocks(c)
                        sl = (t_ ^ 2) if d == 0 else 3 - t_
                        mm(b[rows_, sl * 128:sl * 128 + 128], Ub[rows_, t_ * 64:t_ * 64 + 64], VT[t_][rows_, h * 128:(h + 1) * 128],
                           True, True, free, t1, t_vt)
                    tk = PE.mark()
                    tu = []
                    for p in range(2):
                        sp_ = p if d == 0 else 1 - p
                        rows_ = slice(64 * p, 64 * p + 64)
                        tu.append(copy(ACT, UST[rows_, sp_:8:2, h * 128:(h + 1) * 128], b[rows_, :].rearrange("p (s n) -> p s n", s=4), tk, t_qkv))
                    banks.free[bi] = tu
                    t_u[d, h] = tu
                yield
                for d in range(2):
                    Uw, t2 = lanes[h, d][2], tt_[d][1]
                    bb_ = [banks.get() for _ in range(2)]
                    for c in range(8):
                        p, t_, rows_ = halfblocks(c)
                        mm(bb_[p][0][:, 64 * t_:64 * t_ + 64], KT[t_][rows_, h * 128:(h + 1) * 128], Uw[rows_, t_ * 64:t_ * 64 + 64],
                           True, True, bb_[p][1], t2, t_kt)
                    tk = PE.mark()
                    for p in range(2):
                        t_w[d, h] = copy(ACT, WT[d][h].rearrange("p (t s i) -> p t s i", t=4, s=2)[:, :, p, :], ch(bb_[p][0][:, 0:256]), tk, t_xm)
                        banks.free[bb_[p][2]] = t_w[d, h]
                    setfree[h % 2][d] = tk
                yield

            for _ in prep(0):
                pump()
            for h in range(4):
                side = chain(ending(h - 1) if h else (), prep(h + 1) if h < 3 else ())
                for lv in (2, 4, 8, 16, 32):
                    for d in range(2):
                        Mt, TU, Pm, tTU, ta, tmm = lanes[h, d]
                        b, free, bi = banks.get()
                        for c in range(8):
                            p, t_, rows_ = halfblocks(c)
                            cs_ = slice(t_ * 64, t_ * 64 + 64)
                            mm(b[rows_, cs_], Mt[rows_, cs_], TU[rows_, cs_], True, True, free, tTU, tmm)
                        tk = PE.mark()
                        tP = tt(DVE, ch(Pm), ch(b[:, 0:256]), bc(P(f"lv{lv}_{'fb'[d]}")), MUL, tk, ta, tmm)
                        banks.free[bi] = tP
                        lanes[h, d].append(tP)
                    next(side, None)
                    cstep()
                    for d in range(2):
                        Mt, TU, Pm, tTU, ta, tmm, tP = lanes[h, d]
                        b, free, bi = banks.get()
                        for c in range(8):
                            p, t_, rows_ = halfblocks(c)
                            cs_ = slice(t_ * 64, t_ * 64 + 64)
                            us_ = slice(256 + t_ * 64, 256 + t_ * 64 + 64)
                            if lv < 32:
                                mm(b[rows_, cs_], TU[rows_, us_], Pm[rows_, cs_], True, True, free, tP)
                            mm(b[rows_, us_], Pm[rows_, cs_], TU[rows_, us_], True, True, free, tP)
                        tk = PE.mark()
                        a = 0 if lv < 32 else 256
                        t = tt(DVE, TU[:, a:512], TU[:, a:512], b[:, a:512], SUB, tk)
                        banks.free[bi] = t
                        lanes[h, d] = [Mt, TU, Pm, t, ta, tmm]
                    next(side, None)
                    pump()
                    cstep(2)
                for _ in side:
                    pass
            for _ in ending(3):
                pump(2)
            cstep(100)

            state["pool"] = False
            fs = last()
            S = [B(18672 + d * 512, 512) for d in range(2)]
            SD = [B(19696 + d * 512, 512) for d in range(2)]
            KTL = Rot([B(LN0 + i * 512, 512) for i in range(2)])
            VN = Rot([B(LN0 + 1024, 512), accQ])
            oT = B(8192, 2048).rearrange("p (h t) -> p h t", h=4)
            tS = [memset(POOL, S[d], 0.0, fs) for d in range(2)]
            order = [[4, 5, 6, 7, 0, 1, 2, 3], [7, 6, 5, 4, 3, 2, 1, 0]]
            seen, t_o = set(), {}

            def decayed_keys(s):
                kt_, kfree, ki = KTL.get()
                tkt = []
                for d in range(2):
                    p, t_, rows_ = halfblocks(order[d][s])
                    tkt.append(tt(DVE, kt_[rows_, :].rearrange("p (h n) -> p h n", h=4), KT[t_][rows_, :].rearrange("p (h n) -> p h n", h=4),
                                  cT4[rows_, t_, d, :].unsqueeze(2).broadcast_to([64, 4, 128]), MUL, kfree, fs, t_ct))
                return kt_, ki, tkt

            keys = decayed_keys(0)
            cln = conformer_norm()
            for s in range(8):
                cc = [order[d][s] for d in range(2)]
                hb = [halfblocks(c) for c in cc]
                bw = [banks.get() for _ in range(2)]
                bo = [banks.get() for _ in range(2)]
                b4 = [x_[0][:, 0:256].rearrange("p (h i) -> p h i", h=4) for x_ in bo]
                vn, vfree, vi = VN.get()
                tv, tsd = [], []
                for d in range(2):
                    p, t_, rows_ = hb[d]
                    b, free, bi = bw[d]
                    for h in range(4):
                        mm(b[rows_, h * 128:(h + 1) * 128], WT[d][h][:, 64 * cc[d]:64 * cc[d] + 64], S[d][:, h * 128:(h + 1) * 128],
                           True, True, free, tS[d], t_w[d, h])
                    tk = PE.mark()
                    tv.append(tt(DVE, vn[rows_, :], UST[rows_, s, :], b[rows_, :], SUB, tk, vfree, fs))
                    banks.free[bi] = tv[d]
                    if s < 7:
                        g3 = egl[:, d, :, cc[d]:cc[d] + 1].broadcast_to([128, 4, 128])
                        tsd.append(tt(POOL, SD[d].rearrange("p (h n) -> p h n", h=4), S[d].rearrange("p (h n) -> p h n", h=4), g3, MUL, tS[d], [t_egl[d, h] for h in range(4)]))
                    for h in range(4):
                        qe = QEF[h] if d == 0 else QK[h]
                        mm(b4[d][:, h, :], S[d][:, h * 128:(h + 1) * 128], qe[:, 64 * cc[d]:64 * cc[d] + 64], h == 0, False, bo[d][1], t_qe[d, h])
                    tqs = PE.mark()
                kt_, ki, tkt = keys
                for d in range(2):
                    p, t_, rows_ = hb[d]
                    if s < 7:
                        b, free, bi = banks.get()
                        for h in range(4):
                            mm(b[:, h * 128:(h + 1) * 128], kt_[rows_, h * 128:(h + 1) * 128], vn[rows_, h * 128:(h + 1) * 128], True, True, free, tkt[d], tv[d])
                        tk = PE.mark()
                        tS[d] = tt(DVE, S[d], SD[d], b, ADD, tk, tsd[d], tqs)
                        banks.free[bi] = tS[d]
                    for h in range(4):
                        mm(b4[d][:, h, :], vn[rows_, h * 128:(h + 1) * 128], AT[d][h][rows_, t_, :], False, h == 3, tv[d], t_at[d, h])
                    tok = PE.mark()
                    c = cc[d]
                    dst = oT[:, :, 64 * c:64 * c + 64]
                    if c not in seen:
                        t = copy(ACT, dst, b4[d], tok, t_vT, fs)
                    else:
                        t = tt(DVE, dst, dst, b4[d], ADD, tok, t_o[c])
                    seen.add(c)
                    t_o[c] = t
                    banks.free[bo[d][2]] = t
                KTL.free[ki] = tok
                VN.free[vi] = tok
                if s < 6:
                    keys = decayed_keys(s + 1)
                next(cln, None)
                next(cln, None)
                pump(2)
            for _ in cln:
                pass
            state["pool"] = False
            t_ox = list(t_o.values())

            fm = last()
            HM = [(R(16624 + i * 512, 512), R(20720 + i * 512, 512)) for i in range(8)]
            thm = []
            for m in range(4):
                w, free, i = tmps.get()
                t = act(w, CF[m], ACTF.Silu, t_cf[m], free, scale=P("clg", m, m + 1), bias=P("clb", m, m + 1))
                t = dual(w, HM[4 + m][0], HM[4 + m][1], t, fm)
                tmps.free[i] = t
                thm.append(t)
            srcs = [(HM[4 + m][0], HM[4 + m][1], thm[m]) for m in range(4)] + [None] * 4
            bq, free, bi = banks.get()
            col, cfree, ci = cols_.get()
            sq4 = [[sqs.get(), sqs.get()], None]
            tr = {}

            def squares(e_):
                for h, (sq, sfree, i) in zip((2 * e_, 2 * e_ + 1), sq4[e_]):
                    tr[h] = act(sq, B(8192 + h * 512, 512), ACTF.Square, t_ox, sfree)

            def sums_(e_):
                for h, (sq, sfree, i) in zip((2 * e_, 2 * e_ + 1), sq4[e_]):
                    for t_ in range(4):
                        mm(bq[:, 4 * h + t_:4 * h + t_ + 1], sq[:, 128 * t_:128 * t_ + 128], P("ones")[:, 0:1], True, True, free, cfree, tr[h])
                    sqs.free[i] = PE.mark()

            def heads(k):
                if k == 0:
                    squares(0)
                    sums_(0)
                elif k == 1:
                    sq4[1] = [sqs.get(), sqs.get()]
                    squares(1)
                    sums_(1)
                    t = act(col, bq[:, 0:16], ACTF.Sqrt, sqs.free[sq4[1][1][2]], scale=1.0 / 128, bias=P("eps6"))
                    banks.free[bi] = t
                    tr["r"] = DVE.do(lambda e: e.reciprocal(col, col), t)
                    tr[0] = spread(T, col[:, 0:4], tr["r"], defer=True)
                    tr[1] = spread(T, col[:, 4:8], tr["r"], defer=True)
                elif k >= 3 and k < 7:
                    h = k - 3
                    b, tb_, bi_ = tr[h]()
                    if h == 1:
                        tr[2] = spread(T, col[:, 8:12], tr["r"], defer=True)
                    if h == 2:
                        tr[3] = spread(T, col[:, 12:16], tr["r"], defer=True)
                    r, rfree, ri = tmps.get()
                    t = tt(DVE, r, b, B(8192 + h * 512, 512), MUL, tb_, rfree)
                    banks.free[bi_] = t
                    t = stt(DVE, r, r, P("onorm"), SZ[h], MUL, MUL, t, t_sz[h])
                    tmps.free[ri] = dual(r, HM[h][0], HM[h][1], t, fm)
                    srcs[4 + h] = (HM[h][0], HM[h][1], tmps.free[ri])

            def out_tile(k):
                return lambda i: tile_of("even_w_out", (0,), 128 * k)((i + 4) % 8)

            gt, tg = gate_cols(0, 5, 1.0)
            sums = Sums(T, tok=last())
            for k in range(KD):
                if k == 0:
                    two_ = pair(out_tile(0), out_tile(1), srcs, T, heads)
                    cols_.free[ci] = last()
                b, bi, tk = two_[k] if k < 2 else linear(out_tile(k), srcs, T)
                residual(b, bi, tk, k, T, gt, tg, sums, xs[k])
            return layer_norm_x(T, sums, ("ln_g01", "ln_b01"), norm_cols("ln_g01", "ln_b01", 0, 6, 7, None), XM, last())

        def attend(items, PB, PT, stat):

            def scores(it):
                qs, (k, tk_), scale, mask, v, rows_, sink = it
                nq = len(qs)
                nk = 512 // nq
                b, free, bi = banks.get()
                for i, (q, tq) in enumerate(qs):
                    assert tq != [] and tk_ != []
                    mm(b[:, i * nk:(i + 1) * nk], q, k, True, True, free, tq, tk_)
                t = PE.mark()
                p, pfree, pi = PB.get()
                st, sfree, si = stat.get()
                src = b
                if mask is not None:
                    t = tt(DVE, p, b, mask[0], ADD, t, pfree, mask[1])
                    banks.free[bi] = t
                    src = p
                mx, nb, sm_, rc = (st[:, 2 * j:2 * j + nq] for j in range(4))
                t = DVE.do(lambda e: e.tensor_reduce(mx, src.rearrange("p (i k) -> p i k", i=nq), AXX, ALU.max), t, sfree)
                t = ts(DVE, nb, mx, -scale, None, MUL, None, t)
                for i in range(nq):
                    te = act(p[:, i * nk:(i + 1) * nk], src[:, i * nk:(i + 1) * nk], ACTF.Exp, t, pfree,
                             bias=nb[:, i:i + 1], scale=scale, accum_out=sm_[:, i:i + 1])
                if mask is None:
                    banks.free[bi] = te
                t = DVE.do(lambda e: e.reciprocal(rc, sm_), te)
                for i in range(nq):
                    t2 = ts(DVE, p[:, i * nk:(i + 1) * nk], p[:, i * nk:(i + 1) * nk], rc[:, i:i + 1], None, MUL, None, t)
                stat.free[si] = t2
                return p, pi, t2, nq, nk

            def turn(it, sc):
                p, pi, tp_, nq, nk = sc
                b, free, bi = banks.get()
                for i in range(nq):
                    for k in range(nk // 128):
                        transp(b[:, (k * nq + i) * 128:(k * nq + i + 1) * 128], p[:, i * nk + k * 128:i * nk + (k + 1) * 128], 128, free, tp_)
                t = PE.mark()
                PB.free[pi] = t
                pt, ptfree, pti = PT.get()
                t = copy(ACT, pt, b, t, ptfree)
                banks.free[bi] = t
                return pt, pti, t, nq, nk

            def values(it, tr):
                pt, pti, tp_, nq, nk = tr
                v, rows_, sink = it[4:7]
                b, free, bi = banks.get()
                o = b[rows_, 0:nq * 128]
                for k in range(nk // 128):
                    va, vt = v(k)
                    mm(o, va, pt[:, k * nq * 128:(k + 1) * nq * 128], k == 0, k == nk // 128 - 1, free, tp_, vt)
                t = PE.mark()
                PT.free[pti] = t
                banks.free[bi] = sink(o, t)

            a, c = [], []
            for it in list(items) + [None, None, None]:
                if c:
                    values(*c.pop(0))
                if len(a) > 1 or a and it is None:
                    i0, sc = a.pop(0)
                    c.append((i0, turn(i0, sc)))
                if it is not None:
                    a.append((it, scores(it)))
                yield

        stats = Rot([sm(8) for _ in range(4)])

        def rope(raw, traw, n, rt, C, S, out, ofree, done):
            later.append(lambda: done(rope_now(raw, traw, n, rt, C, S, out, ofree)))

        def rope_now(raw, traw, n, rt, C, S, out, ofree):
            b, free, bi = banks.get()
            mm(b[:, 0:256], P(rt), raw[:, 0:256], True, True, free, traw)
            tk = PE.mark()
            t, tfree, ti = tmps.get()
            t1 = tt(DVE, t[:, 0:256], b[:, 0:256], P(S), MUL, tk, tfree)
            banks.free[bi] = t1
            t2 = tt(POOL, out[:, 0:256], raw[:, 0:256], P(C), MUL, traw, ofree, tk)
            t3 = tt(DVE, out[:, 0:256], out[:, 0:256], t[:, 0:256], ADD, t1, t2)
            tmps.free[ti] = t3
            return t3

        def tiles(a, n=4, w=256):
            return [B(a + i * w, w) for i in range(n)]

        def by_token(name, idx, c0, src, out, fr, between=None):
            bs = [banks.get() for _ in range(2)]
            for k in range(KD):
                whi, wlo, wtok = take([(name, idx, 128 * k, 128, c0, 512, 0)], 512)
                for i in range(2):
                    mm3(bs[i][0], [x_[:, i * 128:(i + 1) * 128] for x_ in src[k][0:2]], (whi, wlo), k == 0, k == KD - 1, bs[i][1], wtok, src[k][2])
                if k < KD - 1 and between:
                    between()
            tk = PE.mark()
            res = []
            for i in range(2):
                res.append(copy(ACT, out[i], bs[i][0], tk, fr))
                banks.free[bs[i][2]] = res[-1]
            return res

        MX = [X[:, k * T + 256:(k + 1) * T] for k in range(KD)]
        KM, VM = tiles(21760), tiles(22784, 2, 512)
        t_mx, t_km, t_vm = [], [[], []], [[], []]

        def scaled_memory(l, MN, fl, ks=range(KD)):
            srcm = []
            for k in ks:
                t_, free, i = sqs.get()
                t = ts(DVE, t_[:, 0:L], MX[k], P(f"mnorm2_{l}", k, k + 1), None, MUL, None, t_mx[k], free)
                sqs.free[i] = dual(t_[:, 0:L], MN[k][0], MN[k][1], t, fl)
                srcm.append((MN[k][0], MN[k][1], sqs.free[i]))
            return srcm

        def memory_keys(l, m, srcm, fl):
            b, bi, tk = linear(tile_of("w_mem_kv_2", (l,), 128 * m), srcm, L)
            t_km[l].append(copy(ACT, KM[m], b[:, 0:L], tk, fl))
            banks.free[bi] = t_km[l][-1]

        def memory_values(l, srcm, fl, between=None):
            t_vm[l].extend(by_token("w_mem_kv_2", (l,), 512, srcm, VM, fl, between))

        def odd_mixer(xs, ms):
            flush()
            f0 = last()
            Q = [B(8192 + h * 256, 256) for h in range(8)]
            K = [B(10240 + h * 512, 512) for h in range(2)]
            VK = [B(11264 + k * 256, 256) for k in range(4)]
            O = [(R(12288 + h * 256, 256), R(14336 + h * 256, 256)) for h in range(8)]
            PB = Rot([B(16384 + i * 512, 512) for i in range(3)])
            PT = Rot([B(17920 + i * 512, 512) for i in range(3)])
            raws = Rot([B(19456 + i * 512, 512) for i in range(3)])
            scale = 128.0 ** -0.5
            MN = [(R(23808 + i * 256, 256), R(25856 + i * 256, 256)) for i in range(8)]
            SP.wait(f0)
            SP.ops.append([lambda e: e.dma_start(X.rearrange("p (k t) -> p k t", k=KD)[:, :, 256:512], MT.rearrange("p (k t) -> p k t", k=KD)).then_inc(s_m, 16), None, 0])

            def headnorm(m, n, g, dst, res):
                b, bi, tk = linear(tile_of("attn_w_in", (0,), 128 * m), [(XM[k][0][:, 0:n], XM[k][1][:, 0:n], ms[k]) for k in range(KD)], n)
                sq, free, i = sqs.get()
                t = act(sq[:, 0:n], b[:, 0:n], ACTF.Square, tk, free)
                def stats():
                    c_ = by_columns(n, [(sq, t)])
                    sqs.free[i] = c_[2][0]
                    rest = root(n, *c_, 1.0 / 128, "eps6", defer=True)
                    later.append(lambda: product(rest))

                def product(rest):
                    b2, tk2, i2 = rest()()
                    r, rfree, ri = tmps.get()
                    t_ = copy(ACT, r[:, 0:n], b2[:, 0:n], tk2, rfree)
                    banks.free[i2] = t_
                    raw, wfree, wi_ = raws.get()
                    t_ = stt(DVE, raw[:, 0:n], b[:, 0:n], P(g), r[:, 0:n], MUL, MUL, t_, wfree, f0)
                    banks.free[bi] = t_
                    tmps.free[ri] = t_
                    if n > 256:
                        res.append(copy(POOL, dst[:, 256:n], raw[:, 256:n], t_, f0))

                    def done(t3):
                        res.append(t3)
                        raws.free[wi_] = list(res)

                    rope(raw, t_, n, "rotT", "ropeC", "ropeS", dst, f0, done)

                later.append(stats)
                return res

            tK = [headnorm(8 + h, T, "kn", K[h], []) for h in range(2)]
            sums = Sums(L, both=False, tok=f0)
            for k in range(KD):
                sums.add(MX[k], (s_m, 16), k == KD - 1)
            bs = [banks.get() for _ in range(4)]
            for k in range(KD):
                whi, wlo, wtok = take([("attn_w_in", (0,), 128 * k, 128, 1280, 256, 0)], 256)
                for i in range(4):
                    mm3(bs[i][0][:, 0:256], [x_[:, i * 128:(i + 1) * 128] for x_ in XM[k]], (whi, wlo), k == 0, k == KD - 1, bs[i][1], wtok, ms[k])
            tk = PE.mark()
            flush()
            tV = []
            for i in range(4):
                t = copy(ACT, VK[i], bs[i][0][:, 0:256], tk, f0)
                banks.free[bs[i][2]] = t
                tV.append(t)
            r, tr, ri = sums.finish(D, "eps6")
            t_mx.extend(tt(DVE, MX[k], MX[k], r[:, 0:L], MUL, tr) for k in range(KD))
            banks.free[ri] = t_mx[-1]
            tO = {}
            tQ = [[] for _ in range(8)]

            def items():
                for h in range(8):
                    for i in range(2):
                        g = h // 4

                        def sink(o, t, h=h, i=i):
                            hi, lo = (x_[:, i * 128:(i + 1) * 128] for x_ in O[h])
                            tO[h, i] = dual(o, hi, lo, t, f0, q=DVE)
                            return tO[h, i]

                        yield ([(Q[h][:, i * 128:(i + 1) * 128], tQ[h])], (K[g], tK[g]), scale, None,
                               lambda k, g=g: (VK[k][:, g * 128:(g + 1) * 128], tV[k]), slice(0, 128), sink)

            gens.append(attend(items(), PB, PT, stats))
            srcm = []
            for h, ks in ((0, (0, 1)), (1, (2, 3, 4)), (2, (5, 6, 7))):
                headnorm(h, 256, "qn", Q[h], tQ[h])
                srcm.extend(scaled_memory(0, MN, f0, ks))
            for h in range(3, 8):
                if h < 7:
                    memory_keys(0, h - 3, srcm, f0)
                    pump()
                headnorm(h, 256, "qn", Q[h], tQ[h])
                pump()
            flush()
            memory_values(0, srcm, f0, pump)
            drain()
            gt, tg = gate_cols(1, 5, 1.0)
            sums = Sums(L)
            srcs = [(O[h][0], O[h][1], [tO[h, 0], tO[h, 1]]) for h in range(8)]
            for k in range(KD):
                b, bi, tk = linear(tile_of("attn_w_out", (0,), 128 * k), srcs, L)
                residual(b, bi, tk, k, L, gt, tg, sums, xs[k])
            return layer_norm_x(L, sums, ("ln_g11", "ln_b11"), norm_cols("ln_g11", "ln_b11", 1, 6, 7, None), XM, last())

        def second_block(xs, tsum, depth):
            state["pool"] = True
            f0 = last()

            def duals(a, n):
                return [(R(a + i * 256, 256), R(a + (n + i) * 256, 256)) for i in range(n)]

            HH, MN, MG = duals(0, 8), duals(4096, 8), duals(4096, 8)
            PT = Rot(tiles(4096, 2, 512))
            WKI, IDX, SEL = (B(5120 + 512 * i, 512) for i in range(3))
            PB = Rot(tiles(6656, 3, 512))
            QA, KA, VA, GA = tiles(8192), tiles(9216), tiles(10240, 2, 512), tiles(11264)
            QB, GB, KB, VB = tiles(12288), tiles(13312), tiles(14336), tiles(15360, 2, 512)
            MQ, GM = QB, GB
            QI, KI = tiles(16384), B(17408, 256)
            MIX = tiles(17664, 24)
            YA, YB, YM = (duals(23808 + 2048 * i, 4) for i in range(3))
            for l in range(depth):
                fl = last()
                if l:
                    srcm = scaled_memory(l, MN, fl)
                sums = tsum
                if l:
                    for m in range(4):
                        memory_keys(l, m, srcm, fl)
                r, tr, ri = sums.finish(D, "eps6")
                src = []
                for k in range(KD):
                    t_, free, i = tmps.get()
                    t = stt(DVE, t_[:, 0:L], Xt[k][:, 0:L], P(f"norm2_{l}", k, k + 1), r[:, 0:L], MUL, MUL, tr, free)
                    banks.free[ri] = t
                    tmps.free[i] = dual(t_[:, 0:L], HH[k][0], HH[k][1], t, fl)
                    src.append((HH[k][0], HH[k][1], tmps.free[i]))

                if l:
                    memory_values(l, srcm, fl)
                tKM, tVM = t_km[l], t_vm[l]
                f_mn = last()

                def proj(piece, m):
                    r = linear(tile_of("w_in_2", (l,), OFF2[piece] + 128 * m), src, L)
                    return r

                def roped(r, dst, fl=fl):
                    res = []
                    b, bi, tk = r
                    raw, free, i = sqs.get()
                    t = copy(ACT, raw[:, 0:256], b[:, 0:256], tk, free)
                    banks.free[bi] = t

                    def done(t3):
                        res.append(t3)
                        sqs.free[i] = t3

                    rope(raw, t, L, "prT", "prC", "prS", dst, fl, done)
                    return res

                def gated(piece, m, dst, fn, fl=fl):
                    b, bi, tk = proj(piece, m)
                    t = act(dst, b[:, 0:L], fn, tk, fl)
                    banks.free[bi] = t
                    return t

                def gated_pair(piece, m, dst, fn, fl):
                    r = [proj(piece, m)]
                    pump()
                    r.append(proj(piece, m + 1))
                    res = []
                    for i, (b, bi, tk) in enumerate(r):
                        t = act(dst[m + i], b[:, 0:L], fn, tk, fl)
                        banks.free[bi] = t
                        res.append(t)
                    return res

                r = linear(lambda k: [("w_in_2", (l,), 128 * k, 128, OFF2[9], 64, 0), ("w_in_2", (l,), 128 * k, 128, OFF2[9], 64, 64)], src, L)
                tKI = roped(r, KI)
                whi, wlo, wtok = take([("w_in_2", (l,), 128 * k, 128, OFF2[10], 8, 8 * k) for k in range(KD)], 64)
                flush()
                b, free, bi = banks.get()
                for i in range(2):
                    for k in range(KD):
                        mm3(b[:, 8 * i:8 * i + 8], [x_[:, i * 128:(i + 1) * 128] for x_ in HH[k]], (whi[:, 8 * k:8 * k + 8], wlo[:, 8 * k:8 * k + 8]),
                            k == 0, k == KD - 1, free, wtok, src[k][2])
                tk = PE.mark()
                t_wi = ts(DVE, wi, b[:, 0:16], 8 ** -0.5, 0.125, MUL, MUL, tk, fl)
                banks.free[bi] = t_wi
                tQI = [roped(proj(8, m), QI[m]) for m in range(4)]
                selt = []

                def index():
                    ta = copy(POOL, IDX, P("causal"), f_mn)
                    for h in range(8):
                        rows_ = slice(64 * (h % 2), 64 * (h % 2) + 64)
                        b, free, bi = banks.get()
                        for i in range(2):
                            mm(b[:, 256 * i:256 * i + 256], QI[h // 2][rows_, i * 128:(i + 1) * 128], KI[rows_, :], True, True, free, tQI[h // 2], tKI)
                        tk = PE.mark()
                        rl, rfree, ri = tmps.get()
                        t = act(rl, b, ACTF.Relu, tk, rfree)
                        banks.free[bi] = t
                        for i in range(2):
                            ta2 = stt(DVE, IDX[:, 256 * i:256 * i + 256], rl[:, 256 * i:256 * i + 256], wi[:, 8 * i + h:8 * i + h + 1],
                                      IDX[:, 256 * i:256 * i + 256], MUL, ADD, t, ta, t_wi)
                        ta = ta2
                        tmps.free[ri] = ta
                        yield
                    tm = [ta, ta]
                    for r_ in range(8):
                        a, o = (IDX, WKI) if r_ % 2 == 0 else (WKI, IDX)
                        for i in range(2):
                            s_ = slice(256 * i, 256 * i + 256)
                            tm[i] = DVE.do(lambda e, a=a, s_=s_, i=i: e.max(mx8[:, 8 * i:8 * i + 8], a[:, s_]), tm[i], f_mn)
                        for i in range(2):
                            s_ = slice(256 * i, 256 * i + 256)
                            tm[i] = DVE.do(lambda e, a=a, o=o, s_=s_, i=i: e.match_replace(o[:, s_], mx8[:, 8 * i:8 * i + 8], a[:, s_], -2.0 ** 127), tm[i])
                        yield
                    t = tm
                    t = ts(DVE, SEL, IDX, -2.0 ** 127, NEG, ALU.not_equal, MUL, t)
                    t = tt(DVE, SEL, SEL, P("causal"), ALU.min, t)
                    selt.append(t)
                    yield

                
                def branch_heads(Q, tQ, K, tK, V, tV, G, tG, Y, tY, mask):
                    for h in range(8):
                        rows_ = slice(64 * (h % 2), 64 * (h % 2) + 64)
                        m = h // 2

                        def sink(o, t, h=h, m=m, rows_=rows_):
                            w, free, i = tmps.get()
                            t1 = tt(DVE, w[rows_, 0:L], o, G[m][rows_, :], MUL, t, tG[m], free)
                            tmps.free[i] = dual(w[rows_, 0:L], Y[m][0][rows_, :], Y[m][1][rows_, :], t1, fl, q=DVE)
                            tY.append(tmps.free[i])
                            return t1

                        yield ([(Q[m][rows_, i * 128:(i + 1) * 128], tQ[m]) for i in range(2)], (K[m][rows_, :], tK[m]), 0.125,
                               mask(), lambda k, h=h: (V[k][:, h * 64:(h + 1) * 64], tV[k]), rows_, sink)

                tY = [[], [], []]

                def qkvg(p0, Q, K, V, G, fl):
                    tQ, tK, tG = [], [], []
                    for m in range(4):
                        tQ.append(roped(proj(p0, m), Q[m], fl))
                        pump()
                        tK.append(roped(proj(p0 + 1, m), K[m], fl))
                        pump()
                    tV = by_token("w_in_2", (l,), OFF2[p0 + 2], src, V, fl)
                    flush()
                    pump()
                    for m in range(0, 4, 2):
                        tG.extend(gated_pair(p0 + 3, m, G, ACTF.Silu, fl))
                        pump()
                    return tQ, tK, tV, tG

                tMQ, tGM = [], []
                for m in range(4):
                    tMQ.append(gated(11, m, MQ[m], ACTF.Copy))
                    pump()
                    tGM.append(gated(12, m, GM[m], ACTF.Silu))
                    pump()

                def memory_heads():
                    for h in range(4):
                        def sink(o, t, h=h):
                            w, free, i = tmps.get()
                            t1 = tt(DVE, w[:, 0:L], o, GM[h], MUL, t, tGM[h], free)
                            tmps.free[i] = dual(w[:, 0:L], YM[h][0], YM[h][1], t1, fl)
                            tY[2].append(tmps.free[i])
                            return t1

                        yield ([(MQ[h][:, i * 128:(i + 1) * 128], tMQ[h]) for i in range(2)], (KM[h], tKM[h]), 128.0 ** -0.5, None,
                               lambda k, h=h: (VM[k][:, h * 128:(h + 1) * 128], tVM[k]), slice(0, 128), sink)

                mem_ = attend(memory_heads(), PB, PT, stats)
                gens.append(mem_)
                gens.append(index())
                tQ, tK, tV, tG = qkvg(0, QA, KA, VA, GA, fl)
                gens.append(attend(branch_heads(QA, tQ, KA, tK, VA, tV, GA, tG, YA, tY[0], lambda: (P("causal"), None)), PB, PT, stats))
                while gens[0] is mem_:
                    pump()
                f_b = last()
                tQ, tK, tV, tG = qkvg(4, QB, KB, VB, GB, f_b)
                gens.append(attend(branch_heads(QB, tQ, KB, tK, VB, tV, GB, tG, YB, tY[1], lambda: (SEL, selt[0])), PB, PT, stats))
                tX = []
                for m in range(0, 24, 2):
                    tX.extend(gated_pair(13, m, MIX, ACTF.Sigmoid, fl))
                    pump()
                drain()
                t_mg = []
                fmg = last()
                for m in range(KD):
                    acc, afree, ai = sqs.get()
                    acc, prev = acc[:, 0:L], afree
                    for n, Y in enumerate((YA, YB, YM)):
                        b, bi, tk = linear(tile_of("w_branch_2", (l, n), 128 * m), [(Y[k][0], Y[k][1], tY[n]) for k in range(4)], L)
                        t, free, i = tmps.get()
                        dst = acc if n == 0 else t[:, 0:L]
                        t1 = tt(DVE, dst, b[:, 0:L], MIX[8 * n + m], MUL, tk, tX[8 * n + m], free, prev if n == 0 else None)
                        banks.free[bi] = t1
                        if n:
                            t1 = tt(DVE, acc, acc, t[:, 0:L], ADD, t1, prev)
                        tmps.free[i] = t1
                        prev = t1
                    sqs.free[ai] = dual(acc, MG[m][0], MG[m][1], prev, fmg)
                    t_mg.append(sqs.free[ai])
                tsum = Sums(L, both=False)
                nxs = []
                for k in range(KD):
                    b, bi, tk = linear(tile_of("w_out_2", (l,), 128 * k), [(MG[m][0], MG[m][1], t_mg[m]) for m in range(KD)], L)
                    x = Xt[k][:, 0:L]
                    t = tt(DVE, x, x, b[:, 0:L], ADD, tk)
                    banks.free[bi] = t
                    tsum.add(x, t, k == KD - 1)
                    nxs.append(t)
                xs = nxs
            if depth == 2:
                r, tr, ri = tsum.finish(D, "eps6")
                xs = [stt(DVE, Xt[k][:, 0:L], Xt[k][:, 0:L], P("fin_g", k, k + 1), r[:, 0:L], MUL, MUL, tr) for k in range(KD)]
            return xs

        gens.append(ada(0, range(4)))
        drain()
        for q in (PE, ACT, DVE, POOL):
            q.wait(tc)
        G, Bc, tcol = norm_cols(None, None, 0, 0, 1, None)
        ms = []
        for k in range(KD):
            m, mfree, mi = sqs.get()
            for s, a, b in halves(T):
                t = ts(DVE, m[:, a:b], Xt[k][:, a:b], G[:, k, s:s + 1], Bc[:, k, s:s + 1], MUL, ADD, tx, tcol, mfree)
            sqs.free[mi] = dual(m, XM[k][0], XM[k][1], t)
            ms.append(sqs.free[mi])
        xs = [tx] * KD
        gens.append(ada(0, range(4, 18)))
        xs, ms = ffn(0, 0, T, xs, ms, ("ln_g00", "ln_b00"), lambda: norm_cols("ln_g00", "ln_b00", 0, 3, 4, None))

        if stage != "ffn0":
            gens.append(ada(1, range(18)))
            xs, ms = even_mixer(xs, ms)
        if stage not in ("ffn0", "even"):
            xs, ms = ffn(0, 1, T, xs, ms, ("ln_g02", "ln_b02"), lambda: norm_cols("ln_g02", "ln_b02", 1, 0, 1, None))
            xs, ms = ffn(1, 0, T, xs, ms, ("ln_g10", "ln_b10"), lambda: norm_cols("ln_g10", "ln_b10", 1, 3, 4, None))
        if stage not in ("ffn0", "even", "l1f"):
            xs, ms = odd_mixer(xs, ms)
        if stage not in ("ffn0", "even", "l1f", "odd"):
            xs, ms = ffn(1, 1, L, xs, ms, ("ln_g12", "ln_b12"), None)
        if stage not in ("ffn0", "even", "l1f", "odd", "first"):
            xs = second_block(xs, ms, 1 if stage == "second0" else 2)
        drain()
        no = T if stage in ("ffn0", "even", "l1f") else L
        for k in range(KD):
            SP.wait(xs[k])
            SP.ops.append([lambda e, k=k: e.dma_start(OUT[:, k, 0:no], Xt[k][:, 0:no]).then_inc(s_out, 16), None, 0])
        SP.ops.append([None, s_out, 16 * KD])

        block = ctx.enter_context(nc.Block())

        @block.sync
        def _(eng):
            SP.play(eng)

        @block.tensor
        def _(eng):
            PE.play(eng)

        @block.scalar
        def _(eng):
            ACT.play(eng)

        @block.vector
        def _(eng):
            DVE.play(eng)

        @block.gpsimd
        def _(eng):
            POOL.play(eng)
    return recipes


def program(nc, nch, stage="all"):
    pn = sum(n for _, n, _ in param_list())
    cn = sum(a.shape[1] for _, a in constant_list())

    def dram(name, shape, kind="ExternalInput"):
        return nc.dram_tensor(name, shape, F32, kind=kind).ap()

    args = [dram("w_stream", [nch, 128, CH]), dram("params", [128, pn]), dram("consts", [128, cn]),
            dram("x_t", [128, KD * T]), dram("mem_t", [128, KD * L]), dram("out_t", [128, KD, T if stage in ("ffn0", "even", "l1f") else L], "ExternalOutput")]
    return build(nc, nch, *args, stage=stage)


def lay_out(a, recipes):
    nch = recipes[-1][0] + 1
    w = np.zeros((nch, 128, CH), np.float32)
    for c, off, n, parts in recipes:
        for name, idx, r0, nr, c0, ncol, at in parts:
            w[c, 0:nr, off + at:off + at + ncol] = a[name][idx][r0:r0 + nr, c0:c0 + ncol]
    x = np.concatenate([a["x"][0], a["ctx"][0]], 0)
    return {
        "w_stream": w,
        "params": np.concatenate([fn(a) for _, _, fn in param_list()], 1),
        "consts": np.concatenate([c for _, c in constant_list()], 1),
        "x_t": np.ascontiguousarray(x.T.reshape(KD, 128, T).transpose(1, 0, 2).reshape(128, KD * T)),
        "mem_t": np.ascontiguousarray(a["mem_2"][0].T.reshape(KD, 128, L).transpose(1, 0, 2).reshape(128, KD * L)),
    }


def kernel(**inputs):
    import concourse.bacc as bacc
    from concourse.bass_utils import run_bass_kernel_spmd

    a = {k: np.asarray(v) for k, v in inputs.items()}
    nc = bacc.Bacc("TRN2", target_bir_lowering=False, num_devices=1)
    recipes = program(nc, NCH)
    assert recipes[-1][0] + 1 == NCH
    r = run_bass_kernel_spmd(nc, [lay_out(a, recipes)], core_ids=[0])
    y = r.results[0]["out_t"]
    return np.ascontiguousarray(y.transpose(2, 1, 0)).reshape(1, L, D)
```
